# Optimizing a Trainium2 kernel written in Bass

```python
import math
import jax, jax.numpy as jnp
from jax import lax
import numpy as np

D_MODEL = 1024
BATCH = 1
SEQ = 512
DEPTH = 1
DEC_BATCH = 8
DEC_SEQ = 4
PAST_LEN = 2048
PAGE_SIZE = 128

M_HEADS = 4
M_HEAD_DIM = D_MODEL // M_HEADS
M_WIDTH = M_HEADS * M_HEAD_DIM
M_CHUNK = 64
A_HEADS = 16
A_HEAD_DIM = 64
A_KV_HEADS = 4
A_GROUP = A_HEADS // A_KV_HEADS
A_WIDTH = A_HEADS * A_HEAD_DIM
KV_WIDTH = A_KV_HEADS * A_HEAD_DIM
CMP_STRIDE = 16
CMP_BLOCK = 2 * CMP_STRIDE
SLC_BLOCK = 64
SLC_TOPK = 16
WINDOW = 512
Q_BLOCK = 64
ROPE_THETA = 500000.0
ROPE_DIM = A_HEAD_DIM // 4
BIG = 1e6
D_FF = 2816
CONV_W = 3
NORM_EPS = 1e-6
IN_WIDTH = 4 * M_WIDTH + 2 * M_HEADS + A_WIDTH + 6 * KV_WIDTH + 3 * A_HEADS + 2 * D_MODEL

kernel_name = 'hybrid_mlstm_nsa_decoder_step'

def rmsnorm(x, g):
    x = x.astype(jnp.float32)
    return x * lax.rsqrt(jnp.mean(x * x, axis=-1, keepdims=True) + NORM_EPS) * g

def rope(x, pos):
    half = ROPE_DIM // 2
    inv_freq = ROPE_THETA ** (-jnp.arange(half, dtype=jnp.float32) / half)
    ang = pos.astype(jnp.float32)[:, None] * inv_freq
    cos = jnp.cos(ang)[:, None, :]
    sin = jnp.sin(ang)[:, None, :]
    x1, x2, rest = x[..., :half], x[..., half:ROPE_DIM], x[..., ROPE_DIM:]
    return jnp.concatenate([x1 * cos - x2 * sin, x2 * cos + x1 * sin, rest], axis=-1)

def masked_softmax(s, mask):
    s = jnp.where(mask, s, -jnp.inf)
    m = jnp.max(s, axis=-1, keepdims=True)
    m = jnp.where(jnp.isfinite(m), m, 0.0)
    e = jnp.exp(s - m)
    return e / jnp.maximum(jnp.sum(e, axis=-1, keepdims=True), jnp.finfo(jnp.float32).tiny)

def split_in_proj(z):
    sizes = [M_WIDTH] * 4 + [M_HEADS, M_HEADS, A_WIDTH, 6 * KV_WIDTH, 3 * A_HEADS, D_MODEL, D_MODEL]
    cuts = [int(c) for c in np.cumsum(sizes)[:-1]]
    return jnp.split(z, cuts, axis=-1)

def mlstm(q, k, v, i_pre, f_pre, o_pre, norm_w, C0, n0, m0):
    B, T, _ = q.shape
    L = math.gcd(T, M_CHUNK)
    NC = T // L

    def heads(a):
        return a.reshape(B, NC, L, M_HEADS, M_HEAD_DIM).transpose(1, 0, 3, 2, 4)

    def gate(a):
        return a.reshape(B, NC, L, M_HEADS).transpose(1, 0, 3, 2)

    xs = (heads(q), heads(k) * M_HEAD_DIM ** -0.5, heads(v), gate(i_pre), gate(jax.nn.log_sigmoid(f_pre)))
    causal = jnp.tril(jnp.ones((L, L), dtype=bool))

    def step(carry, inp):
        C, n, m = carry
        qc, kc, vc, li, lf = inp
        b = jnp.cumsum(lf, axis=-1)
        dlog = jnp.where(causal, b[..., :, None] - b[..., None, :] + li[..., None, :], -jnp.inf)
        inter = m[..., None] + b
        mt = jnp.maximum(inter, jnp.max(dlog, axis=-1))
        a = jnp.exp(inter - mt)
        s = jnp.einsum('bhtd,bhsd->bhts', qc, kc) * jnp.exp(dlog - mt[..., None])
        num = a[..., None] * jnp.einsum('bhvk,bhtk->bhtv', C, qc) + jnp.einsum('bhts,bhsv->bhtv', s, vc)
        den = a * jnp.einsum('bhk,bhtk->bht', n, qc) + jnp.sum(s, axis=-1)
        h = num / jnp.maximum(jnp.abs(den), jnp.exp(-mt))[..., None]
        bl = b[..., -1]
        wlog = bl[..., None] - b + li
        m_new = jnp.maximum(m + bl, jnp.max(wlog, axis=-1))
        w = jnp.exp(wlog - m_new[..., None])
        decay = jnp.exp(m + bl - m_new)
        C = decay[..., None, None] * C + jnp.einsum('bhsv,bhsk->bhvk', vc * w[..., None], kc)
        n = decay[..., None] * n + jnp.einsum('bhs,bhsk->bhk', w, kc)
        return (C, n, m_new), h

    init = (C0.astype(jnp.float32), n0.astype(jnp.float32), m0.astype(jnp.float32))
    (C, n, m), hs = lax.scan(step, init, xs)
    h = hs.transpose(1, 0, 3, 2, 4)
    mu = jnp.mean(h, axis=-1, keepdims=True)
    var = jnp.mean(jnp.square(h - mu), axis=-1, keepdims=True)
    h = ((h - mu) * lax.rsqrt(var + NORM_EPS)).reshape(B, T, M_WIDTH)
    return h * norm_w * jax.nn.sigmoid(o_pre), (C, n, m)

def compress(kv, w1, pe, w2):
    B, S = kv.shape[:2]
    nseg = S // CMP_STRIDE
    seg = kv[:, :nseg * CMP_STRIDE].reshape(B, nseg, CMP_STRIDE, 2, A_KV_HEADS, A_HEAD_DIM)
    first = jnp.einsum('bnskgd,ksde->bnkge', seg[:, :-1], w1[:, :CMP_STRIDE])
    second = jnp.einsum('bnskgd,ksde->bnkge', seg[:, 1:], w1[:, CMP_STRIDE:])
    pe_bias = jnp.einsum('ksd,ksde->ke', pe, w1)
    hid = jax.nn.gelu(first + second + pe_bias[:, None, :])
    return jnp.einsum('bnkge,kef->bnkgf', hid, w2)

def to_blocks(kv):
    B, S = kv.shape[:2]
    ns = -(-S // SLC_BLOCK)
    pad = ns * SLC_BLOCK - S
    if pad:
        kv = jnp.pad(kv, ((0, 0), (0, pad), (0, 0), (0, 0), (0, 0)))
    return kv.reshape(B, ns, SLC_BLOCK, 2, A_KV_HEADS, A_HEAD_DIM)

def coverage(n_cmp, n_slc):
    cs = jnp.arange(n_cmp) * CMP_STRIDE
    ss = jnp.arange(n_slc) * SLC_BLOCK
    lo = jnp.maximum(cs[:, None], ss[None, :])
    hi = jnp.minimum(cs[:, None] + CMP_BLOCK, ss[None, :] + SLC_BLOCK)
    return (jnp.clip(hi - lo, 0, None) / CMP_BLOCK).astype(jnp.float32)

def nsa_block(q, gates, qpos, cmp_kv, slc_blocks, win_kv, win_pos):
    B, Q = q.shape[:2]
    qg = q.reshape(B, Q, A_KV_HEADS, A_GROUP, A_HEAD_DIM) * A_HEAD_DIM ** -0.5
    n_cmp = cmp_kv.shape[1]
    cmp_end = jnp.arange(n_cmp) * CMP_STRIDE + CMP_BLOCK - 1
    p_c = masked_softmax(jnp.einsum('bqgrd,bjgd->bgrqj', qg, cmp_kv[:, :, 0]), cmp_end[None, :] <= qpos[:, None])
    o_c = jnp.einsum('bgrqj,bjgd->bqgrd', p_c, cmp_kv[:, :, 1])
    n_slc = slc_blocks.shape[1]
    imp = jnp.einsum('bgrqj,js->bgqs', p_c, coverage(n_cmp, n_slc))
    blk = jnp.arange(n_slc)[None, :]
    cur = (qpos // SLC_BLOCK)[:, None]
    forced = (blk == 0) | (blk == cur) | (blk == cur - 1)
    future = blk * SLC_BLOCK > qpos[:, None]
    score = jnp.where(future, -BIG, imp + jnp.where(forced, BIG, 0.0))
    _, idx = lax.top_k(score, min(SLC_TOPK, n_slc))
    bi = jnp.arange(B)[:, None, None, None]
    gi = jnp.arange(A_KV_HEADS)[None, :, None, None]
    sel = slc_blocks[bi, idx, :, :, gi]
    kk = idx.shape[-1]
    sel_pos = idx[..., None] * SLC_BLOCK + jnp.arange(SLC_BLOCK)
    mask_s = (sel_pos <= qpos[:, None, None]).reshape(B, A_KV_HEADS, 1, Q, kk * SLC_BLOCK)
    s_s = jnp.einsum('bqgrd,bgqkld->bgrqkl', qg, sel[..., 0, :]).reshape(B, A_KV_HEADS, A_GROUP, Q, kk * SLC_BLOCK)
    p_s = masked_softmax(s_s, mask_s).reshape(B, A_KV_HEADS, A_GROUP, Q, kk, SLC_BLOCK)
    o_s = jnp.einsum('bgrqkl,bgqkld->bqgrd', p_s, sel[..., 1, :])
    mask_w = (win_pos[None, :] <= qpos[:, None]) & (win_pos[None, :] > qpos[:, None] - WINDOW) & (win_pos[None, :] >= 0)
    p_w = masked_softmax(jnp.einsum('bqgrd,bwgd->bgrqw', qg, win_kv[:, :, 0]), mask_w)
    o_w = jnp.einsum('bgrqw,bwgd->bqgrd', p_w, win_kv[:, :, 1])
    g = gates.reshape(B, Q, A_KV_HEADS, A_GROUP, 3)
    o = g[..., 0:1] * o_c + g[..., 1:2] * o_s + g[..., 2:3] * o_w
    return o.reshape(B, Q, A_WIDTH)

def nsa_prompt(q, gates, kv_cmp, kv_slc, kv_win, cmp_w1, cmp_pe, cmp_w2):
    B, T = q.shape[:2]
    cmp = compress(kv_cmp, cmp_w1, cmp_pe, cmp_w2)
    blocks = to_blocks(kv_slc)
    win_pad = jnp.pad(kv_win, ((0, 0), (WINDOW, 0), (0, 0), (0, 0), (0, 0)))
    nb = T // Q_BLOCK
    qb = q.reshape(B, nb, Q_BLOCK, A_HEADS, A_HEAD_DIM).swapaxes(0, 1)
    gb = gates.reshape(B, nb, Q_BLOCK, A_HEADS, 3).swapaxes(0, 1)
    starts = jnp.arange(nb, dtype=jnp.int32) * Q_BLOCK

    def one(args):
        qi, gi, s0 = args
        qpos = s0 + jnp.arange(Q_BLOCK, dtype=jnp.int32)
        wkv = lax.dynamic_slice_in_dim(win_pad, s0, WINDOW + Q_BLOCK, axis=1)
        wpos = s0 - WINDOW + jnp.arange(WINDOW + Q_BLOCK, dtype=jnp.int32)
        return nsa_block(qi, gi, qpos, cmp, blocks, wkv, wpos)

    out = lax.map(one, (qb, gb, starts))
    return out.swapaxes(0, 1).reshape(B, T, A_WIDTH)

def nsa_sample(q, gates, qpos, kv_cmp, kv_slc, kv_win, past_kv, cmp_w1, cmp_pe, cmp_w2):
    past_cmp, past_slc, win_buf = past_kv
    T = q.shape[1]
    full_cmp = jnp.concatenate([past_cmp, kv_cmp], axis=1)
    full_slc = jnp.concatenate([past_slc, kv_slc], axis=1)
    win = jnp.concatenate([win_buf, kv_win], axis=1)
    wb = win_buf.shape[1]
    win_pos = qpos[0] - wb + jnp.arange(wb + T, dtype=jnp.int32)
    out = nsa_block(q, gates, qpos, compress(full_cmp, cmp_w1, cmp_pe, cmp_w2), to_blocks(full_slc), win, win_pos)
    return out, win[:, -wb:]

def conv_ffn(h, prev, w_up, conv_w, conv_b, w_down):
    T = h.shape[1]
    u = h @ w_up
    buf = jnp.concatenate([prev.astype(u.dtype), u], axis=1)
    conv = conv_b
    for j in range(CONV_W):
        conv = conv + conv_w[j] * buf[:, j:j + T]
    a, g = jnp.split(conv, 2, axis=-1)
    return (jax.nn.gelu(g) * a) @ w_down, buf[:, -(CONV_W - 1):]

def decoder_layer(x, c, pos0, mstate, conv_prev, past_kv, lw):
    (w_ada, b_ada, g_pre_mix, g_post_mix, g_pre_ffn, g_post_ffn, w_in, b_in, m_norm_w,
     cmp_w1, cmp_pe, cmp_w2, w_branch_m, w_branch_a, w_out, w_up, conv_w, conv_b, w_down) = lw
    B, T, _ = x.shape
    pos = pos0 + jnp.arange(T, dtype=jnp.int32)
    mod = (jax.nn.silu(c.astype(jnp.float32)) @ w_ada + b_ada)[:, None, :]
    sh_m, sc_m, gt_m, sh_f, sc_f, gt_f = jnp.split(mod, 6, axis=-1)
    h = rmsnorm(x, g_pre_mix) * (1.0 + sc_m) + sh_m
    mq, mk, mv, mo, mi, mf, aq, akv, ag, ga, gb = split_in_proj(h @ w_in + b_in)
    hm, new_m = mlstm(mq, mk, mv, mi, mf, mo, m_norm_w, *mstate)
    q = rope(aq.reshape(B, T, A_HEADS, A_HEAD_DIM), pos)
    kv = akv.reshape(B, T, 3, 2, A_KV_HEADS, A_HEAD_DIM)
    k_rot = rope(kv[:, :, :, 0].reshape(B, T, 3 * A_KV_HEADS, A_HEAD_DIM), pos).reshape(B, T, 3, A_KV_HEADS, A_HEAD_DIM)
    kv = jnp.stack([k_rot, kv[:, :, :, 1]], axis=3)
    kv_cmp, kv_slc, kv_win = kv[:, :, 0], kv[:, :, 1], kv[:, :, 2]
    gates = jax.nn.sigmoid(ag).reshape(B, T, A_HEADS, 3)
    if past_kv is None:
        ha = nsa_prompt(q, gates, kv_cmp, kv_slc, kv_win, cmp_w1, cmp_pe, cmp_w2)
        win_new = kv_win[:, -min(WINDOW, T):]
    else:
        ha, win_new = nsa_sample(q, gates, pos, kv_cmp, kv_slc, kv_win, past_kv, cmp_w1, cmp_pe, cmp_w2)
    mixed = jax.nn.sigmoid(ga) * (hm @ w_branch_m) + jax.nn.sigmoid(gb) * (ha @ w_branch_a)
    x = x + gt_m * rmsnorm(mixed @ w_out, g_post_mix)
    h = rmsnorm(x, g_pre_ffn) * (1.0 + sc_f) + sh_f
    f, conv_new = conv_ffn(h, conv_prev, w_up, conv_w, conv_b, w_down)
    x = x + gt_f * rmsnorm(f, g_post_ffn)
    return x, (kv_cmp, kv_slc, win_new, new_m[0], new_m[1], new_m[2], conv_new)

def setup_inputs(seed: int = 0) -> dict:
    key = jax.random.key(seed)
    keys = iter(jax.random.split(key, 40))

    def nrm(shape, scale):
        return scale * jax.random.normal(next(keys), shape, dtype=jnp.float32)

    def gain(shape):
        return 1.0 + nrm(shape, 0.02)

    n_pages = PAST_LEN // PAGE_SIZE
    n_pool = (DEC_BATCH * n_pages * 5) // 4
    win_buf = min(WINDOW, PAST_LEN)
    kv_row = (2, A_KV_HEADS, A_HEAD_DIM)
    page_table = jax.random.permutation(next(keys), n_pool)[:DEC_BATCH * n_pages].reshape(DEC_BATCH, n_pages).astype(jnp.int32)
    f_off = 4 * M_WIDTH + M_HEADS
    b_in = nrm((DEPTH, IN_WIDTH), 0.02).at[:, f_off:f_off + M_HEADS].add(jnp.linspace(3.0, 6.0, M_HEADS))
    return {
        'x_prompt': nrm((BATCH, SEQ, D_MODEL), 1.0),
        'x_sample': nrm((DEC_BATCH, DEC_SEQ, D_MODEL), 1.0),
        'cache_cmp_kv': nrm((DEPTH, n_pool, PAGE_SIZE) + kv_row, 1.0),
        'cache_slc_kv': nrm((DEPTH, n_pool, PAGE_SIZE) + kv_row, 1.0),
        'cache_win_kv': nrm((DEPTH, DEC_BATCH, win_buf) + kv_row, 1.0),
        'state_C': nrm((DEPTH, DEC_BATCH, M_HEADS, M_HEAD_DIM, M_HEAD_DIM), 0.05),
        'state_n': nrm((DEPTH, DEC_BATCH, M_HEADS, M_HEAD_DIM), 0.05),
        'state_m': nrm((DEPTH, DEC_BATCH, M_HEADS), 0.5),
        'state_conv': nrm((DEPTH, DEC_BATCH, CONV_W - 1, 2 * D_FF), 1.0),
        'page_table': page_table,
        'c_prompt': nrm((BATCH, D_MODEL), 1.0),
        'c_sample': nrm((DEC_BATCH, D_MODEL), 1.0),
        'w_ada': nrm((DEPTH, D_MODEL, 6 * D_MODEL), 0.5 * D_MODEL ** -0.5),
        'b_ada': nrm((DEPTH, 6 * D_MODEL), 0.02),
        'g_pre_mix': gain((DEPTH, D_MODEL)),
        'g_post_mix': gain((DEPTH, D_MODEL)),
        'g_pre_ffn': gain((DEPTH, D_MODEL)),
        'g_post_ffn': gain((DEPTH, D_MODEL)),
        'w_in': nrm((DEPTH, D_MODEL, IN_WIDTH), D_MODEL ** -0.5),
        'b_in': b_in,
        'm_norm_w': gain((DEPTH, M_WIDTH)),
        'cmp_w1': nrm((DEPTH, 2, CMP_BLOCK, A_HEAD_DIM, A_HEAD_DIM), (CMP_BLOCK * A_HEAD_DIM) ** -0.5),
        'cmp_pe': nrm((DEPTH, 2, CMP_BLOCK, A_HEAD_DIM), 0.1),
        'cmp_w2': nrm((DEPTH, 2, A_HEAD_DIM, A_HEAD_DIM), A_HEAD_DIM ** -0.5),
        'w_branch_m': nrm((DEPTH, M_WIDTH, D_MODEL), M_WIDTH ** -0.5),
        'w_branch_a': nrm((DEPTH, A_WIDTH, D_MODEL), A_WIDTH ** -0.5),
        'w_out': nrm((DEPTH, D_MODEL, D_MODEL), D_MODEL ** -0.5),
        'w_up': nrm((DEPTH, D_MODEL, 2 * D_FF), D_MODEL ** -0.5),
        'conv_w': nrm((DEPTH, CONV_W, 2 * D_FF), CONV_W ** -0.5),
        'conv_b': nrm((DEPTH, 2 * D_FF), 0.02),
        'w_down': nrm((DEPTH, D_FF, D_MODEL), D_FF ** -0.5),
    }

def reference(x_prompt, x_sample, cache_cmp_kv, cache_slc_kv, cache_win_kv, state_C, state_n, state_m,
              state_conv, page_table, c_prompt, c_sample, w_ada, b_ada, g_pre_mix, g_post_mix, g_pre_ffn,
              g_post_ffn, w_in, b_in, m_norm_w, cmp_w1, cmp_pe, cmp_w2, w_branch_m, w_branch_a, w_out,
              w_up, conv_w, conv_b, w_down):
    past = page_table.shape[1] * PAGE_SIZE
    xp = x_prompt.astype(jnp.float32)
    xs = x_sample.astype(jnp.float32)
    B = xp.shape[0]
    DB = xs.shape[0]
    zero_mstate = (jnp.zeros((B, M_HEADS, M_HEAD_DIM, M_HEAD_DIM), jnp.float32),
                   jnp.zeros((B, M_HEADS, M_HEAD_DIM), jnp.float32),
                   jnp.zeros((B, M_HEADS), jnp.float32))
    zero_conv = jnp.zeros((B, CONV_W - 1, 2 * D_FF), jnp.float32)
    p_states, s_states = [], []
    for l in range(DEPTH):
        lw = (w_ada[l], b_ada[l], g_pre_mix[l], g_post_mix[l], g_pre_ffn[l], g_post_ffn[l], w_in[l], b_in[l],
              m_norm_w[l], cmp_w1[l], cmp_pe[l], cmp_w2[l], w_branch_m[l], w_branch_a[l], w_out[l], w_up[l],
              conv_w[l], conv_b[l], w_down[l])
        xp, sp = decoder_layer(xp, c_prompt, 0, zero_mstate, zero_conv, None, lw)
        past_cmp = cache_cmp_kv[l, page_table].reshape(DB, past, 2, A_KV_HEADS, A_HEAD_DIM)
        past_slc = cache_slc_kv[l, page_table].reshape(DB, past, 2, A_KV_HEADS, A_HEAD_DIM)
        xs, ss = decoder_layer(xs, c_sample, past, (state_C[l], state_n[l], state_m[l]), state_conv[l],
                               (past_cmp, past_slc, cache_win_kv[l]), lw)
        p_states.append(sp)
        s_states.append(ss)
    p_cmp, p_slc, p_win, p_C, p_n, p_m, p_conv = [jnp.stack([s[i] for s in p_states]) for i in range(7)]
    s_cmp, s_slc, s_win, s_C, s_n, s_m, s_conv = [jnp.stack([s[i] for s in s_states]) for i in range(7)]
    return (xp, xs, p_cmp, p_slc, p_win, p_C, p_n, p_m, p_conv, s_cmp, s_slc, s_win, s_C, s_n, s_m, s_conv)


_drawn_inputs = setup_inputs


def setup_inputs(seed=0):
    import zlib

    import numpy as np

    out = dict(_drawn_inputs(seed))
    spreads = {}
    factors = {'cache_cmp_kv': 2.679,
     'cache_slc_kv': 3.558,
     'g_post_mix': 8.0,
     'g_pre_ffn': 8.085,
     'g_post_ffn': 32.109,
     'm_norm_w': 8.0,
     'cmp_pe': 3.924,
     'conv_b': 7.56}
    for name, (base, spread) in spreads.items():
        noise = np.random.default_rng([zlib.crc32(name.encode()), seed]).standard_normal(out[name].shape)
        drawn = base * np.exp(spread * noise) if base else spread * noise
        out[name] = __import__('jax').numpy.asarray(drawn.astype(out[name].dtype))
    for name, factor in factors.items():
        out[name] = (out[name] * factor).astype(out[name].dtype)
    return out
```

```python
from contextlib import ExitStack

import numpy as np
import concourse.bass as bass
from concourse import mybir

F32 = mybir.dt.float32
I32 = mybir.dt.int32
ALU = mybir.AluOpType
ACT = mybir.ActivationFunctionType
X = mybir.AxisListType.X

P = 128
D = 1024
KT = D // P
SEQ, NB, NT = 512, 8, 4
DEC = NB * NT
TOK = SEQ + DEC
HALF = TOK // 2
PT_ = SEQ // P
TILES = PT_ + 1
MH, MD = 4, 256
AH, AD, G, R = 16, 64, 4, 4
ROPE = 8
PAST, PAGE = 2048, 128
NPAGE = PAST // PAGE
STRIDE = 16
NSEG, NCMP = PAST // STRIDE, PAST // STRIDE - 1
PSEG, PCMP = SEQ // STRIDE, SEQ // STRIDE - 1
BLK, TOPK = 64, 16
NBLK = PAST // BLK
WIN = 512
DFF = 2816
FT = DFF // P
QR = G * NT * R
EPS = 1e-6
NEG = -1e30
TINY = 1.17549435e-38

O_MI, O_AQ, O_AG, O_GA = 4096, 4104, 6664, 6712
V_SHM, V_SCM, V_SHF, V_SCF, V_GM, V_GF, V_MQ, V_MK, V_GA, V_GB = range(0, 80, 8)
NV, NC2 = 80, 88


def rows(tile):
    return P if tile < PT_ else DEC


def cols(tile):
    return slice(tile * P, tile * P + rows(tile))


class Shared:

    def __init__(self, args):
        self.args = args


class Chain:

    def __init__(self, eng, sem):
        self.eng, self.sem, self.n, self.turn, self.steps = eng, sem, 0, None, 0

    def __call__(self, ins):
        ins.then_inc(self.sem, 1)
        self.n += 1
        self.eng.wait_ge(self.sem, self.n if self.turn is None else self.turn * self.steps + self.n)

    def enter(self, turn, steps):
        self.turn, self.steps, self.at = turn, steps, self.n

    def leave(self, turns):
        assert self.n - self.at == self.steps, (self.n - self.at, self.steps)
        self.n, self.turn = self.at + turns * self.steps, None


class Ring:

    def __init__(self, nc, ctx):
        self.whole = ctx.enter_context(nc.sbuf_tensor("weights", [P, 2 * KT * 512], F32))
        self.buf = [self.whole[:, KT * 512 * s:KT * 512 * (s + 1)] for s in range(2)]
        self.loaded = [nc.alloc_semaphore(f"weights_loaded{s}") for s in range(2)]
        self.uses = [0, 0]

    def view(self, s, width=512):
        return self.buf[s][:, 0:KT * width].rearrange("p (k n) -> p k n", k=KT)

    def load(self, sp, s, src, after=None, dst=None):
        if after is not None:
            sp.wait_ge(*after)
        sp.dma_start(self.view(s) if dst is None else dst, src).then_inc(self.loaded[s], 16)

    def await_load(self, pe, s, turn=None, turns=1, parts=1):
        n = 16 * (self.uses[s] + parts)
        pe.wait_ge(self.loaded[s], n if turn is None else turn * (16 * parts) + n)
        self.uses[s] += parts * turns


def matrix(w, c, width=512, k=KT):
    return w[:, bass.ds(c, width)].rearrange("(k p) n -> p k n", p=P)


def fm_units(pe, w, rhs, ps, free, done, u, units=4, c0=0):
    for j in range(units):
        pe.wait_ge(free, u + j + 1)
        for k in range(KT):
            for half in range(2):
                last = pe.matmul(ps[:, 2 * (j % 4) + half, 0:HALF], w[:, k, c0 + j * P:c0 + (j + 1) * P],
                                 rhs[:, k, half * HALF:(half + 1) * HALF], start=k == 0, stop=k == KT - 1)
        last.then_inc(done, 1)


def fm(ps, u):
    return ps[:, 2 * (u % 4):2 * (u % 4) + 2, 0:HALF]


def halves(ap):
    return ap.rearrange("p (a n) -> p a n", a=2)


def tm_units(pe, lhs, w, ps, free, done, at, ktiles=KT, width=512, c0=0):
    for t in range(TILES):
        pe.wait_ge(free, at + t + 1)
        for k in range(ktiles):
            last = pe.matmul(ps[0:rows(t), (at + t) % 5, 0:width], lhs[:, k, cols(t)], w[:, k, c0:c0 + width],
                             start=k == 0, stop=k == ktiles - 1)
        last.then_inc(done, 1)
    return last


def constants():
    f = np.float32
    c = {}
    c["ident"] = np.eye(P, dtype=f)
    pos = np.concatenate([np.arange(SEQ), np.tile(PAST + np.arange(NT), NB)]).astype(f)
    inv = (f(500000.0) ** (-np.arange(ROPE, dtype=f) / f(ROPE))).astype(f)
    ang = (pos[:, None] * inv).astype(f)
    rope = np.zeros((TILES * P, 2, ROPE), f)
    rope[:TOK, 0], rope[:TOK, 1] = np.cos(ang), np.sin(ang)
    c["rope"] = rope.reshape(TILES, P, 2 * ROPE).transpose(1, 0, 2).copy()
    q, k = np.arange(P)[:, None], np.arange(P)[None, :]
    c["causal_add"] = np.where(k <= q, 0, NEG).astype(f)
    c["causal_keep"] = (q <= k).astype(f)
    qpos, j = np.arange(SEQ)[:, None], np.arange(PCMP)[None, :]
    c["cmp_add"] = np.where(j * STRIDE + 2 * STRIDE - 1 <= qpos, 0, NEG).astype(f).reshape(PT_, P, PCMP).transpose(1, 0, 2).copy()
    t = (np.arange(QR) // R % NT)[:, None, None]
    b, n = np.arange(NB)[None, :, None], np.arange(DEC)[None, None, :]
    c["new_add"] = np.where((n // NT == b) & (n % NT <= t), 0, NEG).astype(f)
    c["win_add"] = np.where(np.arange(WIN)[None, :] > t[:, 0], 0, NEG).astype(f)
    s, u = np.arange(DEC)[:, None], np.arange(DEC)[None, :]
    c["dec_keep"] = ((s // NT == u // NT) & (s <= u)).astype(f)
    c["dec_of"] = np.repeat(np.eye(NB, dtype=f), NT, axis=0)
    c["dec_row"] = np.tile(np.repeat(np.eye(NB, dtype=f), NT, axis=1)[None], (P, 1, 1))
    cs, ss = np.arange(NCMP)[:, None] * STRIDE, np.arange(NBLK + 1)[None, :] * BLK
    over = np.minimum(cs + 2 * STRIDE, ss + BLK) - np.maximum(cs, ss)
    c["cover"] = (np.clip(over, 0, None) / (2 * STRIDE)).astype(f)
    a = np.arange(QR)
    c["same_gt"] = (a[:, None] // R == np.arange(P)[None, :] // R).astype(f)
    forced = np.zeros((QR, NBLK + 1), f)
    forced[:, [0, NBLK - 1, NBLK]] = 1e6
    c["forced"] = forced
    sel = np.zeros((MH, MH, P), f)
    for h in range(MH):
        sel[h, h] = 1
    c["head_row"] = sel
    scan = np.zeros((MH, 2, TOK), f)
    scan[:, 0] = 1
    scan[:, 0, [0, *range(SEQ, TOK, NT)]] = 0
    scan[:, 1, [0, *range(SEQ, TOK, NT)]] = -1e38
    c["scan"] = scan
    return c


def block_modulation(nc, s):
    a, ring = s.args, s.ring
    with ExitStack() as ctx:
        sb = lambda name, shape: ctx.enter_context(nc.sbuf_tensor(name, shape, F32))
        sem = lambda name: s.semaphore(name)
        c33 = sb("c33", [DEC + 1, D])
        vec = sb("vec", [NC2, 3, P])
        c_in, vec_in, silu, turned, moved, ada, ada_free = [sem(n) for n in (
            "c_in", "vec_in", "silu_done", "turned", "moved", "ada_done", "ada_free")]
        dve_step = sem("mod_dve_step")
        block = ctx.enter_context(nc.Block())
        b_ada, b_in = a["b_ada"][0], a["b_in"][0]

        @block.sync
        def _(sp):
            sp.dma_start(c33[DEC:DEC + 1, :], a["c_prompt"]).then_inc(c_in, 16)
            for t in range(NT):
                sp.dma_start(c33[t:DEC:NT, :], a["c_sample"]).then_inc(c_in, 16)
            sp.dma_start(s.ident[:], a["ident"]).then_inc(c_in, 16)
            ring.load(sp, 0, matrix(a["w_ada"][0], 0))
            for at, src, c0, n in ((V_SHM, b_ada, 0, 16), (V_SHF, b_ada, 3 * D, 16), (V_GM, a["g_pre_mix"][0], 0, 8),
                                   (V_GF, a["g_pre_ffn"][0], 0, 8), (V_MQ, b_in, 0, 16), (V_GA, b_in, O_GA, 16)):
                sp.dma_start(vec[at:at + n, 0, :], src[c0:c0 + n * P].rearrange("(r n) -> r n", n=P)).then_inc(vec_in, 16)
            for n, src in enumerate((a["conv_w"][0, 0], a["conv_w"][0, 1], a["conv_w"][0, 2], a["conv_b"][0])):
                sp.dma_start(vec[2 * FT * (n % 2):2 * FT * (n % 2 + 1), 1 + n // 2, :],
                             src.rearrange("(r n) -> r n", n=P)).then_inc(vec_in, 16)
            ring.load(sp, 1, matrix(a["w_ada"][0], 512))
            for c in (2, 3):
                ring.load(sp, c % 2, matrix(a["w_ada"][0], 512 * c), after=(ada, c - 1))
            ring.load(sp, 0, matrix(a["w_in"][0], 0), after=(ada, 3))
            ring.load(sp, 1, matrix(a["w_in"][0], 512), after=(ada, 4))

        @block.scalar
        def _(act):
            act.wait_ge(c_in, 16 * (NT + 2))
            act.activation(c33[:], c33[:], ACT.Silu).then_inc(silu, 1)

        @block.tensor
        def _(pe):
            pe.wait_ge(silu, 1)
            pe.wait_ge(c_in, 16 * (NT + 2))
            for k in range(KT):
                last = pe.transpose(s.ps[:, 0, k * (DEC + 1):(k + 1) * (DEC + 1)], c33[:, k * P:(k + 1) * P],
                                    s.ident[0:DEC + 1, 0:DEC + 1])
            last.then_inc(turned, 1)
            pe.wait_ge(vec_in, 16 * 10)
            for n, r in enumerate((NV, NC2, NC2)):
                last = pe.transpose(s.ps[:, 1, n * NC2:n * NC2 + r], vec[0:r, n, :], s.ident[0:r, 0:r])
            last.then_inc(turned, 1)
            pe.wait_ge(moved, 1)
            for c in range(4):
                ring.await_load(pe, c % 2)
                if c >= 2:
                    pe.wait_ge(ada_free, c - 1)
                w = ring.view(c % 2)
                for j in range(4):
                    for k in range(KT):
                        last = pe.matmul(s.ps[:, 2 + c % 2, j * (DEC + 1):(j + 1) * (DEC + 1)],
                                         w[:, k, j * P:(j + 1) * P], s.cT[:, k, :], start=k == 0, stop=k == KT - 1)
                last.then_inc(ada, 1)

        @block.vector
        def _(dve):
            link = Chain(dve, dve_step)
            dve.wait_ge(turned, 1)
            dve.tensor_copy(s.cT[:], s.ps[:, 0, 0:KT * (DEC + 1)].rearrange("p (k n) -> p k n", k=KT)).then_inc(moved, 1)
            dve.wait_ge(turned, 2)
            dve.tensor_copy(s.vecT[:, 0, 0:NV], s.ps[:, 1, 0:NV])
            link(dve.tensor_copy(s.vecT[:, 1:3, :], s.ps[:, 1, NC2:3 * NC2].rearrange("p (a n) -> p a n", a=2)))
            for c in range(4):
                dve.wait_ge(ada, c + 1)
                last = dve.tensor_tensor(s.mod[:, 4 * c:4 * c + 4, :],
                                         s.ps[:, 2 + c % 2, 0:4 * (DEC + 1)].rearrange("p (j n) -> p j n", j=4),
                                         s.vecT[:, 0, V_SHM + 4 * c:V_SHM + 4 * c + 4].unsqueeze(2).to_broadcast([P, 4, DEC + 1]),
                                         ALU.add)
                last.then_inc(ada_free, 1)
            dve.wait_ge(ada_free, 4)
            link(dve.scalar_tensor_tensor(s.mod[:, 8:16, :], s.mod[:, 8:16, :], 1.0,
                                          s.vecT[:, 0, V_GM:V_GM + 8].unsqueeze(2).to_broadcast([P, 8, DEC + 1]),
                                          ALU.add, ALU.mult))


def block_norm(nc, s, name, load_x, shift, scale):
    with ExitStack() as ctx:
        sb = lambda n, shape: ctx.enter_context(nc.sbuf_tensor(f"{name}_{n}", shape, F32))
        sem = lambda n: s.semaphore(f"{name}_{n}")
        xn = sb("xn", [P, TILES, D])
        ss = sb("ss", [P, TILES])
        rs = sb("rs", [P, TILES])
        x_in, squared, scaled, rooted, normed, turned, free, step = [sem(n) for n in (
            "x_in", "squared", "scaled", "rooted", "normed", "turned", "free", "step")]
        block = ctx.enter_context(nc.Block())

        if load_x is not None:
            @block.sync
            def _(sp):
                for t in range(TILES):
                    sp.dma_start(s.x[0:rows(t), t, :], load_x(t)).then_inc(x_in, 16)

        @block.scalar
        def _(act):
            for t in range(TILES):
                if t == 0 and load_x is not None:
                    act.wait_ge(x_in, 16 * TILES)
                last = act.activation(xn[0:rows(t), t, :], s.x[0:rows(t), t, :], ACT.Square,
                                      accum_out=ss[0:rows(t), t:t + 1])
            last.then_inc(squared, 1)
            act.wait_ge(scaled, 1)
            act.activation(rs[:, 0:PT_], ss[:, 0:PT_], ACT.Sqrt)
            act.activation(rs[0:DEC, PT_:TILES], ss[0:DEC, PT_:TILES], ACT.Sqrt).then_inc(rooted, 1)

        @block.vector
        def _(dve):
            link = Chain(dve, step)
            dve.wait_ge(squared, 1)
            for r, c in ((P, slice(0, PT_)), (DEC, slice(PT_, TILES))):
                last = dve.tensor_scalar(ss[0:r, c], ss[0:r, c], 1.0 / D, EPS, ALU.mult, ALU.add)
            last.then_inc(scaled, 1)
            dve.wait_ge(rooted, 1)
            for r, c in ((P, slice(0, PT_)), (DEC, slice(PT_, TILES))):
                last = dve.reciprocal(rs[0:r, c], rs[0:r, c])
            link(last)
            for t in range(TILES):
                last = dve.tensor_scalar(xn[0:rows(t), t, :], s.x[0:rows(t), t, :], rs[0:rows(t), t:t + 1], None, ALU.mult)
            last.then_inc(normed, 1)
            for k in range(KT):
                dve.wait_ge(turned, k + 1)
                bank = 2 * (k % 4)
                dve.tensor_scalar(s.ht[:, k, 0:SEQ], s.ps[:, bank, :], s.mod[:, scale + k, DEC:DEC + 1],
                                  s.mod[:, shift + k, DEC:DEC + 1], ALU.mult, ALU.add)
                link(dve.tensor_tensor(s.ht[:, k, SEQ:TOK], s.ps[:, bank + 1, 0:DEC], s.mod[:, scale + k, 0:DEC], ALU.mult))
                dve.tensor_tensor(s.ht[:, k, SEQ:TOK], s.ht[:, k, SEQ:TOK], s.mod[:, shift + k, 0:DEC], ALU.add).then_inc(free, 1)

        @block.tensor
        def _(pe):
            pe.wait_ge(normed, 1)
            for k in range(KT):
                if k >= 4:
                    pe.wait_ge(free, k - 3)
                for t in range(TILES):
                    out = s.ps[:, 2 * (k % 4), cols(t)] if t < PT_ else s.ps[:, 2 * (k % 4) + 1, 0:DEC]
                    last = pe.transpose(out, xn[0:rows(t), t, k * P:(k + 1) * P], s.ident[0:rows(t), 0:rows(t)])
                last.then_inc(turned, 1)


def block_mlstm_in(nc, s):
    a, ring = s.args, s.ring
    w_in, b_in = a["w_in"][0], a["b_in"][0]
    with ExitStack() as ctx:
        sb = lambda name, shape: ctx.enter_context(nc.sbuf_tensor(name, shape, F32))
        sem = lambda name: s.semaphore(name)
        bias = sb("mv_mo_bias", [P, 2 * D])
        wg = sb("gate_weights", [P, KT, 2 * MH])
        small_in, fm_free, fm_done, tm_free, tm_done, step = [sem(n) for n in (
            "b1_small_in", "b1_fm_free", "b1_fm_done", "b1_tm_free", "b1_tm_done", "b1_step")]
        block = ctx.enter_context(nc.Block())

        @block.sync
        def _(sp):
            sp.dma_start(bias[:], b_in[2 * D:4 * D].partition_broadcast(P)).then_inc(small_in, 16)
            sp.dma_start(wg[:], matrix(w_in, O_MI, 2 * MH)).then_inc(small_in, 16)
            with nc.allow_non_contiguous_dma(reason="8 biases"):
                sp.dma_start(s.gate_bias[:], b_in[O_MI:O_AQ].rearrange("(g h) -> h g", g=2)).then_inc(small_in, 16)
            for c in range(2, 8):
                after = (fm_done, 4 * (c - 1)) if c < 6 else (tm_done, TILES * (c - 5))
                ring.load(sp, c % 2, matrix(w_in, 512 * c), after=after)
            for c in range(2):
                ring.load(sp, c % 2, matrix(w_in, O_AQ + 512 * c), after=(tm_done, TILES * (3 + c)))

        @block.tensor
        def _(pe):
            for c in range(4):
                ring.await_load(pe, c % 2)
                fm_units(pe, ring.view(c % 2), s.ht, s.ps, fm_free, fm_done, 4 * c)
            pe.wait_ge(small_in, 48)
            for n in range(2):
                pe.wait_ge(fm_free, 17 + n)
                for k in range(KT):
                    for half in range(2):
                        last = pe.matmul(s.ps[0:MH, 2 * n + half, 0:HALF], wg[:, k, MH * n:MH * (n + 1)],
                                         s.ht[:, k, half * HALF:(half + 1) * HALF], start=k == 0, stop=k == KT - 1)
                last.then_inc(fm_done, 1)
            pe.wait_ge(fm_free, 4 + 18)
            for c in range(4):
                ring.await_load(pe, c % 2)
                tm_units(pe, s.ht, ring.view(c % 2), s.ps, tm_free, tm_done, TILES * c)

        @block.scalar
        def _(act):
            act.sem_inc(fm_free, 4)
            for u in range(16):
                act.wait_ge(fm_done, u + 1)
                act.activation(halves(s.qk[:, u, :]), fm(s.ps, u), ACT.Identity,
                               bias=s.vecT[:, 0, V_MQ + u:V_MQ + u + 1]).then_inc(fm_free, 1)
            act.wait_ge(small_in, 48)
            for n in range(2):
                act.wait_ge(fm_done, 17 + n)
                act.activation(halves(s.gates[:, n, :]), s.ps[0:MH, 2 * n:2 * n + 2, 0:HALF], ACT.Identity,
                               bias=s.gate_bias[:, n:n + 1]).then_inc(fm_free, 1)

        @block.vector
        def _(dve):
            link = Chain(dve, step)
            dve.sem_inc(tm_free, TILES)
            dve.memset(s.va[:, :, :, MD:MD + 1], 1.0)
            dve.wait_ge(small_in, 48)
            for c in range(4):
                for t in range(TILES):
                    u = TILES * c + t
                    r = rows(t)
                    dve.wait_ge(tm_done, u + 1)
                    if c < 2:
                        out = s.va[0:r, t, 2 * c:2 * c + 2, 0:MD]
                    else:
                        out = s.og[0:r, t, 512 * (c - 2):512 * (c - 1)].rearrange("p (a n) -> p a n", a=2)
                    dve.tensor_tensor(out, s.ps[0:r, t, :].rearrange("p (a n) -> p a n", a=2),
                                      bias[0:r, 512 * c:512 * (c + 1)].rearrange("p (a n) -> p a n", a=2),
                                      ALU.add).then_inc(tm_free, 1)


def block_mlstm_gates(nc, s):
    a = s.args
    with ExitStack() as ctx:
        sb = lambda name, shape: ctx.enter_context(nc.sbuf_tensor(name, shape, F32))
        sem = lambda name: s.semaphore(name)
        scan = sb("scan_masks", [MH, 2, TOK])
        m0 = sb("m0", [MH, NB])
        t1, t2, b, u, um, m, mt, w, ainter = [sb(n, [MH, TOK]) for n in (
            "gate_t1", "gate_t2", "gate_b", "gate_u", "gate_um", "gate_m", "gate_mt", "gate_w", "gate_a")]
        mneg = sb("gate_mneg", [MH, TOK])
        small_in, aq, dq, pq, st = [sem(n) for n in ("g_small_in", "g_act", "g_dve", "g_pe", "g_store")]
        block = ctx.enter_context(nc.Block())

        def dec(ap):
            return ap[:, SEQ:TOK].rearrange("p (b t) -> p b t", t=NT)

        @block.sync
        def _(sp):
            sp.dma_start(scan[:], a["scan"]).then_inc(small_in, 16)
            sp.dma_start(s.head_row[:], a["head_row"]).then_inc(small_in, 16)
            sp.dma_start(s.norm_w[:], a["m_norm_w"][0].partition_broadcast(P)).then_inc(small_in, 16)
            with nc.allow_non_contiguous_dma(reason="one value a head and sequence"):
                sp.dma_start(m0[:], a["state_m"][0].rearrange("b h -> h b")).then_inc(small_in, 16)
                sp.wait_ge(dq, 8)
                sp.dma_start(a["p_m"][0, 0].rearrange("(h o) -> h o", o=1), mt[:, SEQ - 1:SEQ]).then_inc(st, 16)
                sp.dma_start(a["s_m"][0].rearrange("b h -> h b"), dec(mt)[:, :, NT - 1]).then_inc(st, 16)
            sp.wait_ge(st, 32)

        @block.scalar
        def _(act):
            link = Chain(act, aq)
            f = s.gates[:, 1, :]
            link(act.activation(t1[:], f, ACT.Abs))
            link(act.activation(t1[:], t1[:], ACT.Exp, scale=-1.0))
            link(act.activation(t1[:], t1[:], ACT.Ln, bias=1.0))
            act.wait_ge(dq, 10)
            link(act.activation(w[:], w[:], ACT.Exp))
            link(act.activation(t2[:], mt[:], ACT.Exp, scale=-1.0))
            link(act.activation(ainter[:, SEQ:TOK], ainter[:, SEQ:TOK], ACT.Exp))
            act.wait_ge(dq, 11)
            for t in range(TILES):
                r = rows(t)
                last = act.activation(s.og[0:r, t, :], s.og[0:r, t, :], ACT.Sigmoid)
            link(last)

        @block.vector
        def _(dve):
            link = Chain(dve, dq)
            dve.wait_ge(small_in, 64)
            link(dve.tensor_scalar(t2[:], s.gates[:, 1, :], 0.0, None, ALU.min))
            dve.wait_ge(aq, 3)
            link(dve.tensor_tensor(t2[:], t2[:], t1[:], ALU.subtract))
            link(dve.tensor_tensor_scan(b[:], scan[:, 0, :], t2[:], 0.0, ALU.mult, ALU.add))
            link(dve.tensor_tensor(u[:], s.gates[:, 0, :], b[:], ALU.subtract))
            link(dve.tensor_copy(um[:], u[:]))
            dve.tensor_scalar(um[:, 0:1], u[:, 0:1], 0.0, None, ALU.max)
            link(dve.tensor_tensor(dec(um)[:, :, 0], dec(u)[:, :, 0], m0[:], ALU.max))
            link(dve.tensor_tensor_scan(m[:], scan[:, 1, :], um[:], -1e38, ALU.add, ALU.max))
            link(dve.tensor_tensor(mt[:], b[:], m[:], ALU.add))
            dve.tensor_scalar(mneg[:], m[:], -1.0, None, ALU.mult)
            dve.tensor_scalar(w[:, 0:SEQ], u[:, 0:SEQ], m[:, SEQ - 1:SEQ], None, ALU.subtract)
            dve.tensor_tensor(dec(w), dec(u), dec(m)[:, :, NT - 1:NT].to_broadcast([MH, NB, NT]), ALU.subtract)
            link(dve.tensor_tensor(dec(ainter), m0[:].unsqueeze(2).to_broadcast([MH, NB, NT]), dec(m), ALU.subtract))
            link(dve.tensor_copy(s.alast[:], s.ident[0:MH, 0:NB]))
            link(dve.tensor_copy(s.alast[:], s.ident[0:MH, 0:NB]))
            dve.wait_ge(aq, 6)
            link(dve.tensor_copy(s.alast[:], dec(ainter)[:, :, NT - 1]))
            dve.wait_ge(pq, 1)
            c = s.ps[:, 0, 0:TILES * 16].rearrange("p (t n) -> p t n", t=TILES)
            dve.tensor_copy(s.gcol[:, 0:PT_, :, :], c[:, 0:PT_, 0:12].rearrange("p t (q h) -> p t q h", q=3))
            dve.tensor_copy(s.gcol[0:DEC, PT_, :, :], c[0:DEC, PT_, 0:12].rearrange("p (q h) -> p q h", q=3))
            dve.tensor_copy(s.acol[:], c[0:DEC, PT_, 12:16])
            for h in range(MH):
                dve.wait_ge(pq, 2 + h)
                last = dve.tensor_copy(halves(s.mneg[:, h, :]), s.ps[:, 1 + 2 * (h % 2):3 + 2 * (h % 2), 0:HALF])
                link(last)
            dve.wait_ge(pq, 6)
            dve.tensor_copy(s.decay[:], s.ps[:, 5, 0:MH * NB].rearrange("p (h b) -> p h b", h=MH))
            dve.wait_ge(aq, 7)
            for t in range(TILES):
                r = rows(t)
                last = dve.tensor_tensor(s.og[0:r, t, :], s.og[0:r, t, :], s.norm_w[0:r, :], ALU.mult)
            link(last)

        @block.tensor
        def _(pe):
            pe.wait_ge(aq, 6)
            pe.wait_ge(dq, 9)
            i4 = s.ident[0:MH, 0:MH]
            for t in range(TILES):
                for q, src in enumerate((u, t2, w, ainter)):
                    if q == 3 and t < PT_:
                        continue
                    last = pe.transpose(s.ps[0:rows(t), 0, 16 * t + 4 * q:16 * t + 4 * q + 4], src[:, cols(t)], i4)
            last.then_inc(pq, 1)
            for h in range(MH):
                if h >= 2:
                    pe.wait_ge(dq, 11 + h)
                for half in range(2):
                    last = pe.matmul(s.ps[:, 1 + 2 * (h % 2) + half, 0:HALF], s.head_row[:, h, :],
                                     mneg[:, half * HALF:(half + 1) * HALF], start=True, stop=True)
                last.then_inc(pq, 1)
            pe.wait_ge(dq, 12)
            for h in range(MH):
                last = pe.matmul(s.ps[:, 5, NB * h:NB * (h + 1)], s.head_row[:, h, :], s.alast[:], start=True, stop=True)
            last.then_inc(pq, 1)


def head_out(s, h, i):
    return s.qk[:, 2 * h + i // 2, MD * (i % 2):MD * (i % 2 + 1)] if i < PT_ else s.hdec[:, h, :]


def block_mlstm_prompt(nc, s):
    a = s.args
    with ExitStack() as ctx:
        sb = lambda name, shape: ctx.enter_context(nc.sbuf_tensor(name, shape, F32))
        sem = lambda name: s.semaphore(name)
        keep = sb("causal_keep", [P, P])
        pt = sb("pt", [P, PT_, SEQ])
        dw = sb("dw", [P, 2, SEQ])
        ktm = sb("k_tm", [P, PT_, MD])
        vw = sb("v_weighted", [P, PT_, MD])
        cout = sb("c_out", [P, 2, MD])
        nout = sb("n_out", [1, MD])
        den = sb("den", [P, 2])
        in_, pe_s, pe_k, pe_o, pe_c, dstep, exps, dwr, astep, ptdone, ktmdone, ofree, cst, cready = [sem(n) for n in (
            "p_in", "p_s_ready", "p_k_turned", "p_o_ready", "p_c_ready", "p_dve_step", "p_exp_done", "p_dw_ready",
            "p_act_step", "p_pt_ready", "p_ktm_ready", "p_o_free", "p_c_stored", "p_c_copied")]
        block = ctx.enter_context(nc.Block())
        JOBS = [(h, j) for h in range(MH) for j in range(PT_)]

        @block.sync
        def _(sp):
            sp.dma_start(keep[:], a["causal_keep"]).then_inc(in_, 16)
            for h in range(MH):
                sp.wait_ge(cready, h + 1)
                sp.dma_start(a["p_C"][0, 0, h].rearrange("(a p) k -> p a k", p=P), cout[:]).then_inc(cst, 16)
                sp.dma_start(a["p_n"][0, 0, h:h + 1, :], nout[:]).then_inc(cst, 16)
            sp.wait_ge(cst, 32 * MH)

        @block.tensor
        def _(pe):
            for h in range(MH):
                if h:
                    pe.wait_ge(ktmdone, h)
                for t in range(PT_):
                    for d in range(2):
                        last = pe.transpose(s.ps[:, 4 + t // 2, 256 * (t % 2) + P * d:256 * (t % 2) + P * (d + 1)],
                                            s.qk[:, 8 + 2 * h + d, cols(t)], s.ident[:])
                last.then_inc(pe_k, 1)
                for j in range(PT_):
                    n = h * PT_ + j
                    if n >= 2:
                        pe.wait_ge(ptdone, n - 1)
                    for d in range(2):
                        last = pe.matmul(s.ps[:, n % 2, P * j:SEQ], s.qk[:, 8 + 2 * h + d, cols(j)],
                                         s.qk[:, 2 * h + d, P * j:SEQ], start=d == 0, stop=d == 1)
                    last.then_inc(pe_s, 1)
                for i in range(PT_):
                    n = h * PT_ + i
                    pe.wait_ge(ptdone, h * PT_ + i + 1)
                    if n >= 2:
                        pe.wait_ge(ofree, n - 1)
                    for j in range(i + 1):
                        last = pe.matmul(s.ps[:, 2 + n % 2, 0:MD + 1], pt[:, j, cols(i)], s.va[:, j, h, :],
                                         start=j == 0, stop=j == i)
                    last.then_inc(pe_o, 1)
                pe.wait_ge(ktmdone, h + 1)
                if h:
                    pe.wait_ge(cready, h)
                for v in range(2):
                    for j in range(PT_):
                        last = pe.matmul(s.ps[:, 6, MD * v:MD * (v + 1)], vw[:, j, P * v:P * (v + 1)], ktm[:, j, :],
                                         start=j == 0, stop=j == PT_ - 1)
                for j in range(PT_):
                    last = pe.matmul(s.ps[0:1, 7, 0:MD], s.gcol[:, j, 2, h:h + 1], ktm[:, j, :],
                                     start=j == 0, stop=j == PT_ - 1)
                last.then_inc(pe_c, 1)

        @block.scalar
        def _(act):
            for h in range(MH):
                for j in range(PT_):
                    n = h * PT_ + j
                    act.wait_ge(dwr, n + 1)
                    act.activation(dw[:, n % 2, P * j:SEQ], dw[:, n % 2, P * j:SEQ], ACT.Exp).then_inc(exps, 1)

        @block.vector
        def _(dve):
            link = Chain(dve, dstep)

            def exponent(n):
                h, j = JOBS[n]
                if n >= 2:
                    dve.wait_ge(ptdone, n - 1)
                dve.tensor_scalar(dw[:, n % 2, P * j:SEQ], s.mneg[:, h, P * j:SEQ], s.gcol[:, j, 0, h:h + 1], 0.0,
                                  ALU.add, ALU.min).then_inc(dwr, 1)

            dve.wait_ge(in_, 16)
            exponent(0)
            for h in range(MH):
                for j in range(PT_):
                    n = h * PT_ + j
                    if n + 1 < len(JOBS):
                        exponent(n + 1)
                    dve.wait_ge(exps, n + 1)
                    link(dve.tensor_tensor(dw[:, n % 2, cols(j)], dw[:, n % 2, cols(j)], keep[:], ALU.mult))
                    dve.wait_ge(pe_s, n + 1)
                    if h:
                        dve.wait_ge(pe_o, h * PT_)
                    dve.scalar_tensor_tensor(pt[:, j, P * j:SEQ], s.ps[:, n % 2, P * j:SEQ], MD ** -0.5,
                                             dw[:, n % 2, P * j:SEQ], ALU.mult, ALU.mult).then_inc(ptdone, 1)
                dve.wait_ge(pe_k, h + 1)
                if h:
                    dve.wait_ge(pe_c, h)
                dve.tensor_scalar(ktm[:], s.ps[:, 4:6, :].rearrange("p a (b n) -> p (a b) n", b=2), MD ** -0.5, None, ALU.mult)
                for j in range(PT_):
                    last = dve.tensor_scalar(vw[:, j, :], s.va[:, j, h, 0:MD], s.gcol[:, j, 2, h:h + 1], None, ALU.mult)
                last.then_inc(ktmdone, 1)
                for i in range(PT_):
                    n = h * PT_ + i
                    o = s.ps[:, 2 + n % 2, :]
                    dve.wait_ge(pe_o, n + 1)
                    link(dve.scalar_tensor_tensor(den[:, 0:1], o[:, MD:MD + 1], -1.0, s.gcol[:, i, 1, h:h + 1],
                                                  ALU.mult, ALU.max))
                    link(dve.tensor_tensor(den[:, 0:1], o[:, MD:MD + 1], den[:, 0:1], ALU.max))
                    link(dve.reciprocal(den[:, 1:2], den[:, 0:1]))
                    dve.tensor_scalar(head_out(s, h, i), o[:, 0:MD], den[:, 1:2], None, ALU.mult).then_inc(ofree, 1)
                dve.wait_ge(pe_c, h + 1)
                if h:
                    dve.wait_ge(cst, 32 * h)
                dve.tensor_copy(cout[:], s.ps[:, 6, :].rearrange("p (a n) -> p a n", a=2))
                dve.tensor_copy(nout[:], s.ps[0:1, 7, 0:MD]).then_inc(cready, 1)


def block_mlstm_decode(nc, s):
    a = s.args
    with ExitStack() as ctx:
        sb = lambda name, shape: ctx.enter_context(nc.sbuf_tensor(name, shape, F32))
        sem = lambda name: s.semaphore(name)
        keep = sb("dec_keep", [DEC, DEC])
        dec_of = sb("dec_of", [DEC, NB])
        dec_row = sb("dec_row", [P, NB, DEC])
        nrow = sb("n_rows", [NB * MH, MD])
        nT = sb("n_turned", [P, 2, NB, MH])
        nnew = sb("n_new", [P, 2, NB, MH])
        nout = sb("n_out_rows", [NB * MH, MD])
        qb = sb("q_of_sequence", [P, 2, MH, 2, DEC])
        vb = sb("v_of_sequence", [DEC, MH, MD])
        wsel = sb("w_of_sequence", [DEC, MH, NB])
        zero = sb("zero", [P, DEC])
        pt = sb("pt_dec", [DEC, MH, DEC])
        dw = sb("dw_dec", [DEC, MH, DEC])
        cT = sb("c_turned", [P, 2, 2, MD + 1])
        cout = sb("c_new", [P, 2, MH, 2, MD])
        num = sb("num_dec", [DEC, MH, MD + 1])
        den = sb("den_dec", [DEC, MH])
        ktm = s.carry[0:DEC, 2 * 2048:2 * 2048 + D].rearrange("p (h k) -> p h k", h=MH)
        cin = [s.hmt[:].rearrange("p k n -> p (k n)")[:, 2048 * i:2048 * (i + 1)].rearrange("p (h v k) -> p h v k", h=MH, v=2)
               for i in range(2)]
        small, cin0, cin1, pe_step, dve_step, exped, turned, moved, picked, state, cnew, inter, st0, st1, nst, local, ncol = [
            sem(n) for n in ("d_small", "d_c_in0", "d_c_in1", "d_pe_step", "d_dve_step", "d_exp", "d_turned", "d_moved",
                             "d_picked", "d_state", "d_c_new", "d_inter", "d_stored0", "d_stored1", "d_n_stored",
                             "d_local", "d_n_col")]
        cload, cstore = [cin0, cin1], [st0, st1]
        block = ctx.enter_context(nc.Block())
        MOVED, INTER, CNEW = 2, 6, 2

        def states(t, b):
            return t[0, b].rearrange("h (v p) k -> p h v k", p=P)

        def states_at(t, b):
            return t[0, bass.ds(b, 1)].rearrange("o h (v p) k -> p (o h) v k", p=P)

        @block.sync
        def _(sp):
            for src, dst in (("dec_keep", keep), ("dec_of", dec_of), ("dec_row", dec_row)):
                sp.dma_start(dst[:], a[src]).then_inc(small, 16)
            sp.dma_start(nrow[:], a["state_n"][0].rearrange("b h k -> (b h) k")).then_inc(small, 16)
            for p in range(2):
                sp.dma_start(cin[p], states(a["state_C"], p)).then_inc(cload[p], 16)
            for p in range(2):
                sp.sem_inc(cstore[p], 16)
            with sp.Fori(0, NB // 2 - 1) as i:
                for p in range(2):
                    sp.wait_ge(cnew, i * 8 + (CNEW + 4 * (p + 1)))
                    sp.dma_start(cin[p], states_at(a["state_C"], i * 2 + (2 + p))).then_inc(cload[p], 16)
                    sp.dma_start(states_at(a["s_C"], i * 2 + p), cout[:, p]).then_inc(cstore[p], 16)
            for p in range(2):
                sp.wait_ge(cnew, 4 * (NB - 2) + CNEW + 4 * (p + 1))
                sp.dma_start(states(a["s_C"], NB - 2 + p), cout[:, p]).then_inc(cstore[p], 16)
            sp.wait_ge(ncol, 2)
            sp.dma_start(a["s_n"][0].rearrange("b h k -> (b h) k"), nout[:]).then_inc(nst, 16)
            sp.wait_ge(nst, 16)
            for p in range(2):
                sp.wait_ge(cstore[p], 16 * (NB // 2 + 1))

        @block.tensor
        def _(pe):
            pe.wait_ge(small, 64)
            for k in range(2):
                pe.transpose(s.ps[:, 0, 32 * k:32 * k + 32], nrow[:, P * k:P * (k + 1)], s.ident[0:32, 0:32])
            for h in range(MH):
                for d in range(2):
                    last = pe.matmul(s.ps[0:DEC, 1, DEC * h:DEC * (h + 1)], s.qk[:, 8 + 2 * h + d, SEQ:TOK],
                                     s.qk[:, 2 * h + d, SEQ:TOK], start=d == 0, stop=d == 1)
            for h in range(MH):
                for d in range(2):
                    last = pe.transpose(s.ps[0:DEC, 2 + h // 2, MD * (h % 2) + P * d:MD * (h % 2) + P * (d + 1)],
                                        s.qk[:, 8 + 2 * h + d, SEQ:TOK], s.ident[:])
            last.then_inc(pe_step, 1)
            pe.wait_ge(dve_step, 3)
            for h in range(MH):
                for d in range(2):
                    last = pe.matmul(s.ps[:, 4, 8 * (2 * h + d):8 * (2 * h + d + 1)], ktm[:, h, P * d:P * (d + 1)],
                                     wsel[:, h, :], start=True, stop=True)
            last.then_inc(pe_step, 1)
            pe.wait_ge(ncol, 1)
            for d in range(2):
                last = pe.transpose(s.ps[0:NB * MH, 5, P * d:P * (d + 1)], nnew[:, d].rearrange("p b h -> p (b h)"), s.ident[:])
            last.then_inc(pe_step, 1)
            pe.wait_ge(ncol, 2)
            for h in range(MH):
                pe.matmul(s.ps[0:DEC, h, 0:MD + 1], zero[:], s.va[:, 0, 0, :], start=True, stop=False, skip_group_check=True)
            pe.sem_inc(inter, INTER)
            with pe.Fori(0, NB // 2) as i:
                for m in range(8):
                    p, h = m // 4, m % 4
                    if h == 0:
                        pe.wait_ge(cload[p], i * 16 + 16)
                    pe.wait_ge(moved, i * 8 + (m - 2 + 1 + MOVED))
                    for k in range(2):
                        for v in range(2):
                            last = pe.transpose(s.ps[:, 4 + m % 2, MD * k + P * v:MD * k + P * (v + 1)],
                                                cin[p][:, h, v, P * k:P * (k + 1)], s.ident[:])
                    last.then_inc(turned, 1)
                    if h == 0:
                        pe.wait_ge(picked, i * 2 + (p + 1))
                    pe.wait_ge(cnew, i * 8 + (m - 2 + 1 + CNEW))
                    for v in range(2):
                        last = pe.matmul(s.ps[:, 6 + m % 2, MD * v:MD * (v + 1)], vb[:, h, P * v:P * (v + 1)], ktm[:, h, :],
                                         start=True, stop=True)
                    last.then_inc(state, 1)
                    pe.wait_ge(moved, i * 8 + (m + 1 + MOVED))
                    for k in range(2):
                        last = pe.matmul(s.ps[0:DEC, h, 0:MD + 1], qb[:, p, h, k, :], cT[:, m % 2, k, :], start=False,
                                         stop=False, skip_group_check=True)
                    last.then_inc(inter, 1)
            pe.wait_ge(cnew, 4 * NB + CNEW)
            for h in range(MH):
                last = pe.matmul(s.ps[0:DEC, 4 + h, 0:MD + 1], pt[:, h, :], s.va[0:DEC, PT_, h, :], start=True, stop=True)
            last.then_inc(local, 1)

        @block.scalar
        def _(act):
            act.wait_ge(dve_step, 1)
            act.activation(dw[:], dw[:], ACT.Exp).then_inc(exped, 1)
            act.sem_inc(moved, MOVED)
            act.wait_ge(ncol, 2)
            with act.Fori(0, NB // 2) as i:
                for m in range(8):
                    p, h = m // 4, m % 4
                    act.wait_ge(turned, i * 8 + (m + 1))
                    act.wait_ge(inter, i * 8 + (m - 2 + 1 + INTER))
                    act.copy(cT[:, m % 2, :, MD], nT[:, :, bass.ds(i * 2 + p, 1), h].rearrange("p k o -> p (k o)"))
                    act.copy(cT[:, m % 2, :, 0:MD],
                             s.ps[:, 4 + m % 2, :].rearrange("p (k n) -> p k n", k=2)).then_inc(moved, 1)

        @block.vector
        def _(dve):
            link = Chain(dve, dve_step)
            dve.sem_inc(cnew, CNEW)
            dve.memset(zero[:], 0.0)
            for h in range(MH):
                last = dve.tensor_scalar(dw[:, h, :], s.mneg[0:DEC, h, SEQ:TOK], s.gcol[0:DEC, PT_, 0, h:h + 1], 0.0,
                                         ALU.add, ALU.min)
            link(last)
            dve.wait_ge(small, 64)
            for h in range(MH):
                last = dve.tensor_scalar(wsel[:, h, :], dec_of[:], s.gcol[0:DEC, PT_, 2, h:h + 1], None, ALU.mult)
            link(last)
            dve.wait_ge(pe_step, 1)
            dve.tensor_copy(nT[:], s.ps[:, 0, 0:64].rearrange("p (k b h) -> p k b h", k=2, b=NB))
            link(dve.tensor_scalar(ktm[:], s.ps[0:DEC, 2:4, :].rearrange("p a (b n) -> p (a b) n", b=2), MD ** -0.5, None,
                                   ALU.mult))
            dve.wait_ge(exped, 1)
            for h in range(MH):
                last = dve.tensor_tensor(dw[:, h, :], dw[:, h, :], keep[:], ALU.mult)
            link(last)
            link(dve.scalar_tensor_tensor(pt[:], s.ps[0:DEC, 1, 0:MH * DEC].rearrange("p (h n) -> p h n", h=MH), MD ** -0.5,
                                          dw[:], ALU.mult, ALU.mult))
            decay = s.decay[:].rearrange("p h b -> p b h")
            for k in range(2):
                last = dve.tensor_tensor(nnew[:, k], nT[:, k], decay, ALU.mult)
            link(last)
            dve.wait_ge(pe_step, 2)
            sums = s.ps[:, 4, 0:64].rearrange("p (h k b) -> p k b h", h=MH, k=2)
            for k in range(2):
                last = dve.tensor_tensor(nnew[:, k], nnew[:, k], sums[:, k], ALU.add)
            last.then_inc(ncol, 1)
            dve.wait_ge(pe_step, 3)
            dve.tensor_copy(nout[:], s.ps[0:NB * MH, 5, 0:MD]).then_inc(ncol, 1)
            with dve.Fori(0, NB // 2) as i:
                for p in range(2):
                    dve.wait_ge(inter, i * 8 + (4 * p + INTER))
                    for h in range(MH):
                        dve.tensor_scalar(vb[:, h, :], s.va[0:DEC, PT_, h, 0:MD],
                                          wsel[:, h, bass.ds(i * 2 + p, 1)], None, ALU.mult)
                        last = dve.tensor_tensor(qb[:, p, h], s.qk[:, 2 * h:2 * h + 2, SEQ:TOK],
                                                 dec_row[:, bass.ds(i * 2 + p, 1), :].to_broadcast([P, 2, DEC]), ALU.mult)
                    last.then_inc(picked, 1)
                    dve.wait_ge(cload[p], i * 16 + 16)
                    dve.wait_ge(cstore[p], i * 16 + 16)
                    for h in range(MH):
                        m = 4 * p + h
                        dve.wait_ge(state, i * 8 + (m + 1))
                        dve.scalar_tensor_tensor(cout[:, p, h], cin[p][:, h], s.decay[:, h, bass.ds(i * 2 + p, 1)],
                                                 s.ps[:, 6 + m % 2, :].rearrange("p (v n) -> p v n", v=2),
                                                 ALU.mult, ALU.add).then_inc(cnew, 1)
            dve.wait_ge(inter, 4 * NB + INTER)
            for h in range(MH):
                last = dve.tensor_scalar(num[:, h, :], s.ps[0:DEC, h, 0:MD + 1], s.acol[:, h:h + 1], None, ALU.mult)
            link(last)
            dve.wait_ge(local, 1)
            link(dve.tensor_tensor(num[:], num[:], s.ps[0:DEC, 4:8, 0:MD + 1], ALU.add))
            link(dve.scalar_tensor_tensor(den[:], num[:, :, MD], -1.0, s.gcol[0:DEC, PT_, 1, :], ALU.mult, ALU.max))
            link(dve.tensor_tensor(den[:], num[:, :, MD], den[:], ALU.max))
            link(dve.reciprocal(den[:], den[:]))
            for h in range(MH):
                last = dve.tensor_scalar(s.hdec[:, h, :], num[:, h, 0:MD], den[:, h:h + 1], None, ALU.mult)
            link(last)


def block_mlstm_out(nc, s):
    with ExitStack() as ctx:
        sb = lambda name, shape: ctx.enter_context(nc.sbuf_tensor(name, shape, F32))
        sem = lambda name: s.semaphore(name)
        st6 = sb("stats6", [P, TILES, MH, 6])
        mv = sb("mean_var", [P, TILES, MH, 2])
        sd = sb("deviation", [P, TILES, MH])
        step, rooted, ready, turned, freed = [sem(n) for n in ("o_step", "o_rooted", "o_ready", "o_turned", "o_freed")]
        block = ctx.enter_context(nc.Block())

        @block.vector
        def _(dve):
            link = Chain(dve, step)
            for t in range(TILES):
                for h in range(MH):
                    last = dve.bn_stats(st6[0:rows(t), t, h, :], head_out(s, h, t))
            link(last)
            for t in range(TILES):
                for h in range(MH):
                    last = dve.bn_aggr(mv[0:rows(t), t, h, :], st6[0:rows(t), t, h, :])
            link(last)
            for r, c in ((P, slice(0, PT_)), (DEC, slice(PT_, TILES))):
                last = dve.tensor_scalar(sd[0:r, c], mv[0:r, c, :, 1], EPS, None, ALU.add)
            link(last)
            dve.wait_ge(rooted, 1)
            for r, c in ((P, slice(0, PT_)), (DEC, slice(PT_, TILES))):
                last = dve.reciprocal(sd[0:r, c], sd[0:r, c])
            link(last)
            for t in range(TILES):
                for h in range(MH):
                    last = dve.tensor_scalar(head_out(s, h, t), head_out(s, h, t), mv[0:rows(t), t, h, 0:1],
                                             sd[0:rows(t), t, h:h + 1], ALU.subtract, ALU.mult)
            link(last)
            for t in range(TILES):
                for h in range(MH):
                    og = s.og[0:rows(t), t, MD * h:MD * (h + 1)]
                    last = dve.tensor_tensor(og, og, head_out(s, h, t), ALU.mult)
            last.then_inc(ready, 1)

        @block.scalar
        def _(act):
            act.wait_ge(step, 3)
            act.activation(sd[:, 0:PT_], sd[:, 0:PT_], ACT.Sqrt)
            act.activation(sd[0:DEC, PT_], sd[0:DEC, PT_], ACT.Sqrt).then_inc(rooted, 1)
            for k in range(KT):
                act.wait_ge(turned, k + 1)
                act.copy(s.hmt[:, k, 0:SEQ], s.ps[:, 2 * (k % 4), :])
                act.copy(s.hmt[:, k, SEQ:TOK], s.ps[:, 2 * (k % 4) + 1, 0:DEC]).then_inc(freed, 1)

        @block.tensor
        def _(pe):
            pe.wait_ge(ready, 1)
            turn_tiles(pe, s, s.og, turned, freed)


def turn_tiles(pe, s, tm, turned, freed):
    for k in range(KT):
        if k >= 4:
            pe.wait_ge(freed, k - 3)
        for t in range(TILES):
            out = s.ps[:, 2 * (k % 4), cols(t)] if t < PT_ else s.ps[:, 2 * (k % 4) + 1, 0:DEC]
            last = pe.transpose(out, tm[0:rows(t), t, k * P:(k + 1) * P], s.ident[0:rows(t), 0:rows(t)])
        last.then_inc(turned, 1)


def block_attention_in(nc, s):
    a, ring = s.args, s.ring
    w_in, b_in = a["w_in"][0], a["b_in"][0]
    WIDE = D + 6 * G * AD
    with ExitStack() as ctx:
        sb = lambda name, shape: ctx.enter_context(nc.sbuf_tensor(name, shape, F32))
        sem = lambda name: s.semaphore(name)
        bias = sb("attention_bias", [P, WIDE + 48])
        wg = sb("branch_gate_weights", [P, KT, 48])
        rope = sb("rope_table", [P, TILES, 2 * ROPE])
        tmp = s.hat[:].rearrange("p k n -> p (k n)")[:, 0:4 * PT_ * AH * ROPE].rearrange("p (k t h d) -> p k t h d", k=4, t=PT_, h=AH)
        small_in, tm_free, tm_done, step, gate_sum, gated, kv_ready, stored, win_copied, gate_out = [sem(n) for n in (
            "c1_small_in", "c1_tm_free", "c1_tm_done", "c1_step", "c1_gate_sum", "c1_gated", "c1_kv_ready", "c1_stored",
            "c1_win_copied", "c1_gate_stored")]
        block = ctx.enter_context(nc.Block())
        names = ("cmp", "slc", "win")

        @block.sync
        def _(sp):
            sp.dma_start(bias[:], b_in[O_AQ:O_GA].partition_broadcast(P)).then_inc(small_in, 16)
            sp.dma_start(wg[:], matrix(w_in, O_AG, 48)).then_inc(small_in, 16)
            sp.dma_start(rope[:], a["rope"]).then_inc(small_in, 16)
            sp.dma_start(a["s_win"][0, :, 0:WIN - NT].rearrange("b w x g d -> b w (x g d)"),
                         a["cache_win_kv"][0, :, NT:WIN].rearrange("b w x g d -> b w (x g d)")).then_inc(win_copied, 16)
            for c in range(2, 5):
                ring.load(sp, c % 2, matrix(w_in, O_AQ + 512 * c), after=(tm_done, TILES * (c - 1)))
            for n, name in enumerate(names):
                sp.wait_ge(kv_ready, n + 1)
                out = a["p_" + name][0, 0].rearrange("(t p) x g d -> p t (x g d)", p=P)
                sp.dma_start(out, s.kv[:, 0:PT_, 512 * n:512 * (n + 1)]).then_inc(stored, 16)
                out = a["s_" + name][0]
                if name == "win":
                    out = out[:, WIN - NT:WIN]
                    for b in range(NB):
                        sp.dma_start(out[b].rearrange("t x g d -> t (x g d)"),
                                     s.kv_dec[NT * b:NT * (b + 1), 512 * n:512 * (n + 1)]).then_inc(stored, 16)
                else:
                    sp.dma_start(out.rearrange("b t x g d -> (b t) (x g d)"),
                                 s.kv_dec[:, 512 * n:512 * (n + 1)]).then_inc(stored, 16)
            sp.wait_ge(gated, 1)
            sp.dma_start(s.gate_scratch, s.branch_gates[0:DEC, PT_, :]).then_inc(gate_out, 16)
            sp.wait_ge(gate_out, 16)
            sp.wait_ge(stored, 16 * (5 + NB))
            sp.wait_ge(win_copied, 16)

        @block.tensor
        def _(pe):
            pe.wait_ge(small_in, 48)
            for c in range(5):
                ring.await_load(pe, c % 2)
                tm_units(pe, s.ht, ring.view(c % 2), s.ps, tm_free, tm_done, TILES * c)
            tm_units(pe, s.ht, wg, s.ps, tm_free, tm_done, TILES * 5, width=48)

        @block.scalar
        def _(act):
            act.wait_ge(gate_sum, 1)
            act.activation(s.branch_gates[:, 0:PT_, :], s.branch_gates[:, 0:PT_, :], ACT.Sigmoid)
            act.activation(s.branch_gates[0:DEC, PT_, :], s.branch_gates[0:DEC, PT_, :], ACT.Sigmoid).then_inc(gated, 1)

        @block.vector
        def _(dve):
            link = Chain(dve, step)
            dve.sem_inc(tm_free, TILES)
            dve.wait_ge(small_in, 48)

            def evacuate(c, t):
                r = rows(t)
                dve.wait_ge(tm_done, TILES * c + t + 1)
                width = 512
                if c < 2:
                    split = lambda ap: ap.rearrange("p (g h d) -> p g h d", g=2, h=R)
                    out = s.q_tm[0:r, t, 512 * c:512 * (c + 1)].rearrange("p (h g d) -> p g h d", g=2, h=R)
                    return dve.tensor_tensor(out, split(s.ps[0:r, t, :]), split(bias[0:r, 512 * c:512 * (c + 1)]), ALU.add)
                elif c < 5:
                    out = s.kv[0:r, t, 512 * (c - 2):512 * (c - 1)] if t < PT_ else s.kv_dec[:, 512 * (c - 2):512 * (c - 1)]
                else:
                    out, width = s.branch_gates[0:r, t, :], 48
                return dve.tensor_tensor(out, s.ps[0:r, t, 0:width], bias[0:r, 512 * c:512 * c + width], ALU.add)

            def rotate(x1, x2, r, tiles, heads):
                n = (r, len(tiles), heads, ROPE)
                table = lambda k: rope[0:r, tiles[0]:tiles[-1] + 1, ROPE * k:ROPE * (k + 1)].unsqueeze(2).to_broadcast(n)
                w = [tmp[0:r, k, 0:len(tiles), 0:heads, :] for k in range(4)]
                dve.tensor_tensor(w[0], x1, table(0), ALU.mult)
                dve.tensor_tensor(w[1], x2, table(1), ALU.mult)
                dve.tensor_tensor(w[2], x2, table(0), ALU.mult)
                link(dve.tensor_tensor(w[3], x1, table(1), ALU.mult))
                dve.tensor_tensor(x1, w[0], w[1], ALU.subtract)
                return dve.tensor_tensor(x2, w[2], w[3], ALU.add)

            for c in range(6):
                for t in range(TILES):
                    evacuate(c, t).then_inc(tm_free, 1)
                dve.wait_ge(tm_free, TILES * (c + 2))
                if c == 1:
                    q = s.q_tm[:].rearrange("p t (h d) -> p t h d", d=AD)
                    link(rotate(q[:, 0:PT_, :, 0:ROPE], q[:, 0:PT_, :, ROPE:2 * ROPE], P, range(PT_), AH))
                    link(rotate(q[0:DEC, PT_:TILES, :, 0:ROPE], q[0:DEC, PT_:TILES, :, ROPE:2 * ROPE], DEC, [PT_], AH))
                elif 2 <= c < 5:
                    at = 512 * (c - 2)
                    k = s.kv[:, :, at:at + G * AD].rearrange("p t (g d) -> p t g d", d=AD)
                    link(rotate(k[:, :, :, 0:ROPE], k[:, :, :, ROPE:2 * ROPE], P, range(PT_), G))
                    k = s.kv_dec[:, at:at + G * AD].rearrange("p (o g d) -> p o g d", o=1, d=AD)
                    rotate(k[:, :, :, 0:ROPE], k[:, :, :, ROPE:2 * ROPE], DEC, [PT_], G).then_inc(kv_ready, 1)
                    dve.wait_ge(kv_ready, c - 1)
                elif c == 5:
                    dve.tensor_copy(bias[0:1, 0:1], rope[0:1, 0, 0:1]).then_inc(gate_sum, 1)


def block_attention_turn(nc, s):
    a = s.args
    with ExitStack() as ctx:
        sb = lambda name, shape: ctx.enter_context(nc.sbuf_tensor(name, shape, F32))
        sem = lambda name: s.semaphore(name)
        pe_rows = sb("position_rows", [2 * AD // 2, AD])
        peT = sb("position_columns", [AD, 2 * AD // 2])
        w_in_, moved_pe, turned_pe, turned, freed, summed = [sem(n) for n in (
            "c2_weights_in", "c2_position_moved", "c2_position_turned", "c2_turned", "c2_freed", "c2_summed")]
        block = ctx.enter_context(nc.Block())

        @block.sync
        def _(sp):
            sp.dma_start(pe_rows[:], a["cmp_pe"][0].rearrange("x s d -> (x s) d")).then_inc(w_in_, 16)
            for half in range(2):
                for gp in range(2):
                    for kv in range(2):
                        sp.dma_start(s.w1[AD * gp:AD * (gp + 1), kv, :, half, :],
                                     a["cmp_w1"][0, kv, 16 * half:16 * (half + 1)].rearrange("s d e -> d s e")).then_inc(w_in_, 16)
            sp.dma_start(s.w2[:], a["cmp_w2"][0].rearrange("x e f -> e x f")).then_inc(w_in_, 16)
            for g in range(G):
                for t in range(NT):
                    sp.dma_start(s.gate_rows[16 * g + R * t:16 * g + R * (t + 1), :, :],
                                 s.gate_scratch.rearrange("(b t) (h x) -> t h b x", t=NT, x=3)[t, R * g:R * (g + 1)]).then_inc(w_in_, 16)
            sp.wait_ge(w_in_, 16 * (10 + QR // R))

        @block.tensor
        def _(pe):
            pe.wait_ge(w_in_, 16 * (10 + QR // R))
            pe.transpose(s.ps[0:AD, 0, 0:64], pe_rows[:], s.ident[0:64, 0:64]).then_inc(turned_pe, 1)
            pe.wait_ge(moved_pe, 1)
            for kv in range(2):
                for n in range(2 * STRIDE):
                    last = pe.matmul(s.ps[0:AD, 1, kv:kv + 1], s.w1[0:AD, kv, n % STRIDE, n // STRIDE, :],
                                     peT[:, 32 * kv + n:32 * kv + n + 1], start=n == 0, stop=n == 2 * STRIDE - 1)
            last.then_inc(summed, 1)
            pe.wait_ge(moved_pe, 2)
            for n in range(12):
                if n >= 4:
                    pe.wait_ge(freed, n - 3)
                for t in range(TILES):
                    r = rows(t)
                    if n < 8:
                        src = s.q_tm[0:r, t, P * n:P * (n + 1)]
                    else:
                        at = 512 * (1 + (n - 8) // 2) + P * (n % 2)
                        src = s.kv[:, t, at:at + P] if t < PT_ else s.kv_dec[:, at:at + P]
                    out = s.ps[:, 2 * (n % 4), cols(t)] if t < PT_ else s.ps[:, 2 * (n % 4) + 1, 0:DEC]
                    last = pe.transpose(out, src, s.ident[0:r, 0:r])
                last.then_inc(turned, 1)

        @block.vector
        def _(dve):
            dve.wait_ge(turned_pe, 1)
            dve.tensor_copy(peT[:], s.ps[0:AD, 0, 0:64]).then_inc(moved_pe, 1)
            dve.wait_ge(summed, 1)
            dve.tensor_copy(s.pe_bias[:], s.ps[0:AD, 1, 0:2]).then_inc(moved_pe, 1)

        @block.scalar
        def _(act):
            for n in range(12):
                act.wait_ge(turned, n + 1)
                if n < 8:
                    act.mul(s.qT[:, n // 4, n % 4, :], s.ps[:, 2 * (n % 4), :], AD ** -0.5)
                    act.mul(s.qT_dec[:, n // 4, n % 4, :], s.ps[:, 2 * (n % 4) + 1, 0:DEC], AD ** -0.5).then_inc(freed, 1)
                else:
                    br, p = (n - 8) // 2, n % 2
                    act.copy(s.kT[:, br, p, :], s.ps[:, 2 * (n % 4), :])
                    act.copy(s.kT_dec[:, br, p, :], s.ps[:, 2 * (n % 4) + 1, 0:DEC]).then_inc(freed, 1)


class Compress:
    BANKS = (6, 7)

    def __init__(self, nc, s, ctx, name, nseg):
        sb = lambda n, shape: ctx.enter_context(nc.sbuf_tensor(f"{name}_{n}", shape, F32))
        self.s, self.n = s, nseg
        self.xt = sb("segments_fm", [P, 2, 2, 2, nseg])
        self.second = sb("second_half", [AD, 2, G, nseg])
        self.hid = sb("hidden", [AD, 2, G, nseg - 1])
        self.turned, self.moved, self.used, self.shifted, self.added, self.gelu, self.out = [
            s.semaphore(f"{name}_{n}") for n in (
                "x_turned", "x_moved", "x_used", "second_ready", "hidden_in_ready", "hidden_ready", "compressed")]

    def sums(self, kv, part):
        at = AD * part
        return self.s.ps[at:at + AD, 2 * kv:2 * kv + 2, 0:2 * self.n].rearrange("p a (b n) -> p a b n", b=2)

    def tensor(self, pe, seg, t=0):
        s, n = self.s, self.n
        for kv in range(2):
            for c in range(8 + 1):
                if c < 8:
                    u = 8 * kv + c
                    pe.wait_ge(self.moved, t * 16 + (u + 1))
                    for row in range(2):
                        for p in range(2):
                            at = 256 * kv + P * p
                            last = pe.transpose(s.ps[:, self.BANKS[u % 2], n * (2 * row + p):n * (2 * row + p + 1)],
                                                seg[:, 2 * c + row, at:at + P], s.ident[0:n, 0:n])
                    last.then_inc(self.turned, 1)
                if c > 0:
                    u = 8 * kv + c - 1
                    pe.wait_ge(self.moved, t * 16 + (u + 3))
                    for row in range(2):
                        for gp in range(2):
                            k = 2 * (c - 1) + row
                            h = slice(AD * gp, AD * (gp + 1))
                            last = pe.matmul(s.ps[:, 2 * kv + gp, 0:2 * n], s.w1[h, kv, k].rearrange("p a e -> p (a e)"),
                                             self.xt[h, u % 2, row].rearrange("p b n -> p (b n)"), start=k == 0, stop=k == 15)
                    last.then_inc(self.used, 1)
        m = n - 1
        pe.wait_ge(self.gelu, t * 2 + 1)
        for gp in range(2):
            out, w2 = (s.ps[:, 4, 0:2 * m], s.w2[:].rearrange("p a f -> p (a f)")) if gp == 0 else (s.ps[AD:P, 4, 0:2 * m], s.w2[:, 0, :])
            last = pe.matmul(out, w2,
                             self.hid[:, 0, 2 * gp:2 * gp + 2, :].rearrange("p a n -> p (a n)"), start=True, stop=True)
        last.then_inc(self.out, 1)
        pe.wait_ge(self.gelu, t * 2 + 2)
        for g in range(G):
            last = pe.matmul(s.ps[0:m, 5, AD * g:AD * (g + 1)], self.hid[:, 1, 2 * (g % 2) + g // 2, :], s.w2[:, 1, :],
                             start=True, stop=True)
        last.then_inc(self.out, 1)

    def scalar(self, act, t=0):
        s, n = self.s, self.n
        for kv in range(2):
            for c in range(8):
                u = 8 * kv + c
                act.wait_ge(self.turned, t * 16 + (u + 1))
                act.wait_ge(self.used, t * 16 + (u + 1))
                act.copy(self.xt[:, u % 2].rearrange("p a b n -> p (a b n)"), s.ps[:, self.BANKS[u % 2], 0:4 * n]).then_inc(self.moved, 1)
            act.wait_ge(self.used, t * 16 + (8 * (kv + 1) + 2))
            act.activation(self.second[:, kv].rearrange("p (a b) n -> p a b n", a=2), self.sums(kv, 1), ACT.Identity,
                           bias=s.pe_bias[:, kv:kv + 1]).then_inc(self.shifted, 1)
        for kv in range(2):
            act.wait_ge(self.added, t * 2 + (kv + 1))
            act.activation(self.hid[:, kv], self.hid[:, kv], ACT.Gelu_apprx_tanh).then_inc(self.gelu, 1)

    def vector(self, dve, kc, vc, t=0):
        s, n = self.s, self.n
        for kv in range(2):
            dve.wait_ge(self.shifted, t * 2 + (kv + 1))
            dve.tensor_tensor(self.hid[:, kv].rearrange("p (a b) n -> p a b n", a=2), self.sums(kv, 0)[:, :, :, 0:n - 1],
                              self.second[:, kv].rearrange("p (a b) n -> p a b n", a=2)[:, :, :, 1:n], ALU.add).then_inc(self.added, 1)
        m = n - 1
        dve.wait_ge(self.out, t * 2 + 1)
        dve.tensor_copy(kc, s.ps[:, 4, 0:2 * m].rearrange("p (a n) -> p a n", a=2))
        dve.wait_ge(self.out, t * 2 + 2)
        return dve.tensor_copy(vc, s.ps[0:m, 5, 0:G * AD])


def block_compress_prompt(nc, s):
    a = s.args
    with ExitStack() as ctx:
        seg = s.ring.whole[0:PSEG].rearrange("p (s n) -> p s n", s=STRIDE)
        seg_in, done = [s.semaphore(n) for n in ("seg_in", "compress_done")]
        comp = Compress(nc, s, ctx, "pc", PSEG)
        block = ctx.enter_context(nc.Block())

        @block.sync
        def _(sp):
            sp.dma_start(seg[:], a["p_cmp"][0, 0].rearrange("(n s) x g d -> n s (x g d)", s=STRIDE)).then_inc(seg_in, 16)

        @block.tensor
        def _(pe):
            pe.sem_inc(comp.used, 2)
            pe.wait_ge(seg_in, 16)
            comp.tensor(pe, seg)

        @block.scalar
        def _(act):
            act.sem_inc(comp.moved, 2)
            comp.scalar(act)

        @block.vector
        def _(dve):
            comp.vector(dve, s.kc_p[:], s.vc_p[:]).then_inc(done, 1)


def block_attention_prompt(nc, s):
    a = s.args
    with ExitStack() as ctx:
        sb = lambda name, shape: ctx.enter_context(nc.sbuf_tensor(name, shape, F32))
        sem = lambda name: s.semaphore(name)
        causal = sb("causal_add", [P, P])
        cmp_add = sb("cmp_add", [P, PT_, PCMP])
        qs = sb("q_of_r", [P, 2, SEQ])
        prob = sb("prob", [P, 3, SEQ])
        pT = sb("prob_turned", [P, 2, SEQ])
        nmax = sb("minus_max", [P, 4])
        sums = sb("sums", [P, 2, 3])
        alpha = sb("alpha", [P, 2, 3])
        acc = sb("acc", [P, AD])
        in_, q_ready, q_used, scored, maxed, exped, turned, moved, weighed, step, combined = [sem(n) for n in (
            "a_masks_in", "a_q_ready", "a_q_used", "a_scored", "a_maxed", "a_exped", "a_turned", "a_moved", "a_weighed",
            "a_step", "a_combined")]
        block = ctx.enter_context(nc.Block())
        UNITS = [(g, i, br) for g in range(G) for i in range(PT_) for br in range(3)]
        N = len(UNITS)
        S_BANKS, T_BANKS, O_BANKS = (0, 1, 2), (3, 4, 5), (6, 7)
        EXPED, MOVED, WEIGHED, COMB, QU, MAXED = 3, 3, 6, 2, N, 3

        def keys(u):
            g, i, br = UNITS[u]
            return PCMP if br == 0 else P * (i + 1)

        def blocks(u):
            g, i, br = UNITS[u]
            return [(0, PCMP)] if br == 0 else [(j, P) for j in range(i + 1)]

        @block.sync
        def _(sp):
            sp.dma_start(causal[:], a["causal_add"]).then_inc(in_, 16)
            sp.dma_start(cmp_add[:], a["cmp_add"]).then_inc(in_, 16)

        @block.tensor
        def _(pe):
            with pe.Fori(0, R) as r:
                pe.wait_ge(q_ready, r + 1)
                for n in range(N + 3):
                    if n < N:
                        u = n
                        g, i, br = UNITS[u]
                        p, at = g // 2, AD * (g % 2)
                        pe.wait_ge(exped, r * N + (u - 3 + 1 + EXPED))
                        rhs = s.kc_p[at:at + AD, p, :] if br == 0 else s.kT[at:at + AD, br - 1, p, 0:keys(u)]
                        pe.matmul(s.ps[:, S_BANKS[u % 3], 0:keys(u)], qs[at:at + AD, p, cols(i)], rhs,
                                  start=True, stop=True).then_inc(scored, 1)
                    if 2 <= n < N + 2:
                        u = n - 2
                        pe.wait_ge(exped, r * N + (u + 1 + EXPED))
                        pe.wait_ge(moved, r * N + (u - 3 + 1 + MOVED))
                        for j, w in blocks(u):
                            last = pe.transpose(s.ps[0:w, T_BANKS[u % 3], P * j:P * (j + 1)], prob[:, u % 3, P * j:P * j + w],
                                                s.ident[:])
                        last.then_inc(turned, 1)
                    if n >= 3:
                        u = n - 3
                        g, i, br = UNITS[u]
                        tile = u // 3
                        pe.wait_ge(moved, r * N + (u + 1 + MOVED))
                        if br == 0:
                            pe.wait_ge(combined, r * (N // 3) + (tile - 2 + 1 + COMB))
                        for j, w in blocks(u):
                            v = s.vc_p[:, AD * g:AD * (g + 1)] if br == 0 else \
                                s.kv[:, j, 512 * br + 256 + AD * g:512 * br + 256 + AD * (g + 1)]
                            last = pe.matmul(s.ps[:, O_BANKS[tile % 2], AD * br:AD * (br + 1)], pT[0:w, u % 2, P * j:P * (j + 1)],
                                             v, start=j == 0, stop=j == blocks(u)[-1][0])
                        last.then_inc(weighed, 1)

        @block.scalar
        def _(act):
            act.sem_inc(exped, EXPED)
            act.sem_inc(moved, MOVED)
            with act.Fori(0, R) as r:
                act.wait_ge(weighed, r * N + WEIGHED)
                act.copy(qs[:], s.qT[:, :, bass.ds(r, 1), :].rearrange("p a o n -> p (a o) n")).then_inc(q_ready, 1)
                for n in range(N + 2):
                    if n < N:
                        u = n
                        act.wait_ge(maxed, r * N + (u + 1 + MAXED))
                        act.wait_ge(turned, r * N + (u - 2)) if u >= 3 else None
                        if u % 3 == 0:
                            act.wait_ge(combined, r * (N // 3) + (u // 3 - 2 + 1 + COMB))
                        act.activation(prob[:, u % 3, 0:keys(u)], s.ps[:, S_BANKS[u % 3], 0:keys(u)], ACT.Exp,
                                       bias=nmax[:, u % 4:u % 4 + 1],
                                       accum_out=sums[:, (u // 3) % 2, u % 3:u % 3 + 1]).then_inc(exped, 1)
                    if n >= 2:
                        u = n - 2
                        act.wait_ge(turned, r * N + (u + 1))
                        act.wait_ge(weighed, r * N + (u - 2 + 1 + WEIGHED))
                        w, width = (PCMP, P) if UNITS[u][2] == 0 else (P, keys(u))
                        act.copy(pT[0:w, u % 2, 0:width], s.ps[0:w, T_BANKS[u % 3], 0:width]).then_inc(moved, 1)

        @block.vector
        def _(dve):
            link = Chain(dve, step)
            dve.wait_ge(in_, 32)
            dve.sem_inc(maxed, MAXED)
            dve.sem_inc(combined, COMB)
            dve.sem_inc(weighed, WEIGHED)
            STEPS = N + N // 3 * 6
            with dve.Fori(0, R) as r:
                link.enter(r, STEPS)

                def mask(u):
                    g, i, br = UNITS[u]
                    k = keys(u)
                    dve.wait_ge(scored, r * N + (u + 1))
                    tail = s.ps[:, S_BANKS[u % 3], 0:k] if br == 0 else s.ps[:, S_BANKS[u % 3], k - P:k]
                    return dve.tensor_tensor(tail, tail, cmp_add[:, i, :] if br == 0 else causal[:], ALU.add)

                def largest(u):
                    g, i, br = UNITS[u]
                    nm = nmax[:, u % 4:u % 4 + 1]
                    dve.wait_ge(exped, r * N + (u - 4 + 1 + EXPED + 1)) if u >= 4 else None
                    if br == 0:
                        link(dve.tensor_reduce(nm, s.ps[:, S_BANKS[u % 3], 0:keys(u)], X, ALU.max, negate=True))
                        dve.tensor_scalar(nm, nm, 1e29, None, ALU.min).then_inc(maxed, 1)
                    else:
                        dve.tensor_reduce(nm, s.ps[:, S_BANKS[u % 3], 0:keys(u)], X, ALU.max, negate=True).then_inc(maxed, 1)

                def combine(t):
                    g, i, _ = UNITS[3 * t]
                    k = t % 2
                    dve.wait_ge(exped, r * N + (3 * t + 3 + EXPED))
                    link(dve.tensor_scalar(alpha[:, k], sums[:, k], TINY, None, ALU.max))
                    link(dve.reciprocal(alpha[:, k], alpha[:, k]))
                    gate = s.branch_gates[:, i, bass.ds(r * 3 + 12 * g, 3)]
                    dve.wait_ge(weighed, r * N + (3 * t + 3 + WEIGHED))
                    link(dve.tensor_tensor(alpha[:, k], alpha[:, k], gate, ALU.mult))
                    o = s.ps[:, O_BANKS[k], :]
                    link(dve.tensor_scalar(acc[:], o[:, 0:AD], alpha[:, k, 0:1], None, ALU.mult))
                    link(dve.scalar_tensor_tensor(acc[:], o[:, AD:2 * AD], alpha[:, k, 1:2], acc[:], ALU.mult, ALU.add))
                    dve.scalar_tensor_tensor(s.ha[:, i, bass.ds(r * AD + 256 * g, AD)], o[:, 2 * AD:3 * AD], alpha[:, k, 2:3],
                                             acc[:], ALU.mult, ALU.add).then_inc(combined, 1)

                for n in range(N + 5):
                    if n < N:
                        link(mask(n))
                        largest(n)
                    if n >= 5 and (n - 5) % 3 == 2:
                        combine((n - 5) // 3)
                link.leave(R)


def block_attention_out(nc, s):
    with ExitStack() as ctx:
        turned, freed = [s.semaphore(n) for n in ("ao_turned", "ao_freed")]
        block = ctx.enter_context(nc.Block())

        @block.tensor
        def _(pe):
            for k in range(KT):
                if k >= 4:
                    pe.wait_ge(freed, k - 3)
                for t in range(PT_):
                    last = pe.transpose(s.ps[:, k % 4, cols(t)], s.ha[:, t, k * P:(k + 1) * P], s.ident[:])
                last.then_inc(turned, 1)

        @block.scalar
        def _(act):
            for k in range(KT):
                act.wait_ge(turned, k + 1)
                act.copy(s.hat[:, k, 0:SEQ], s.ps[:, k % 4, :]).then_inc(freed, 1)


def token_rows(prompt, sample, t):
    return prompt[0, t * P:(t + 1) * P, :] if t < PT_ else sample.rearrange("b t n -> (b t) n")


def block_attention_decode(nc, s):
    a, ring = s.args, s.ring
    NK = PAST + DEC
    NW = WIN + DEC
    with ExitStack() as ctx:
        sb = lambda name, shape, dt=F32: ctx.enter_context(nc.sbuf_tensor(name, shape, dt))
        sem = lambda name: s.semaphore("e_" + name)
        ptab = sb("page_table_sb", [1, NB * NPAGE], I32)
        win_add = sb("win_add", [QR, WIN])
        new_add = sb("new_add", [QR, NB, DEC])
        cover = sb("cover", [NCMP, NBLK + 1])
        same_gt = sb("same_gt", [QR, P])
        forced = sb("forced", [QR, NBLK + 1])
        slc = sb("slc_pages", [P, NPAGE, 512])
        win = sb("win_rows", [P, PT_, 512])
        seg = ring.whole[:].rearrange("p (s n) -> p s n", s=STRIDE)
        comp = Compress(nc, s, ctx, "dc", NSEG)
        kc = sb("kc_dec", [P, 2, NCMP])
        vc = sb("vc_dec", [NCMP, G * AD])
        kT = sb("k_turned", [P, 2, 2, 512])
        qb = sb("q_blocks", [P, 2, QR])
        sc = sb("cmp_prob", [QR, 2, NCMP])
        ss = sb("slc_prob", [QR, NK])
        sw = sb("win_prob", [QR, NW])
        pcT = sb("cmp_prob_turned", [NCMP, 2, QR])
        pT = sb("probs_turned", [P, 22, QR])
        imp = sb("importance", [QR, 2, NBLK + 1])
        top = sb("top8", [QR, 8])
        at_wait = sb("at_wait", [QR, 4])
        nmax = sb("minus_max_dec", [QR, 3])
        sums = sb("sums_dec", [QR, 3])
        alpha = sb("alpha_dec", [QR, 3])
        (const_in, slc_in, cmp_in, win_in, q_set, packed, c_max, c_prob, c_copied, imp_copied, s_max, s_scaled, w_max,
         w_scaled, out_done, k_moved, c_exp, w_exp, s_exp, p_moved, small_scored, k_turned, scored, c_turned, imp_done,
         p_turned, weighed, step) = [sem(n) for n in (
             "const_in", "slc_in", "cmp_in", "win_in", "q_set", "packed", "c_max", "c_prob", "c_copied", "imp_copied",
             "s_max", "s_scaled", "w_max", "w_scaled", "out_done", "k_moved", "c_exp", "w_exp", "s_exp", "p_moved",
             "small_scored", "k_turned", "scored", "c_turned", "imp_done", "p_turned", "weighed", "step")]
        block = ctx.enter_context(nc.Block())
        KU = 10
        K_MOVED, OUT = 2, 1

        @block.sync
        def _(sp):
            sp.dma_start(ptab[:], a["page_table"].rearrange("b p -> (b p)").unsqueeze(0)).then_inc(const_in, 16)
            for src, dst in (("win_add", win_add), ("new_add", new_add), ("cover", cover), ("same_gt", same_gt), ("forced", forced)):
                sp.dma_start(dst[:], a[src]).then_inc(const_in, 16)
            sp.wait_ge(const_in, 16)
            sp.wait_ge(const_in, 96)

            def load(b):
                for pg in range(NPAGE):
                    page = sp.value_load(ptab[0:1, bass.ds(b * NPAGE + pg, 1)], min_val=0, max_val=a["cache_slc_kv"].shape[1] - 1)
                    sp.dma_start(slc[:, pg, :], a["cache_slc_kv"][0, bass.ds(page, 1)].rearrange("o n x g d -> (o n) (x g d)")).then_inc(slc_in, 16)
                w = a["cache_win_kv"][0, bass.ds(b, 1)].rearrange("o (n p) x g d -> p (o n) (x g d)", p=P)
                sp.dma_start(win[:], w).then_inc(win_in, 16)

            load(0)
            with sp.Fori(0, NB - 1) as i:
                sp.wait_ge(weighed, i + 1)
                load(i + 1)
            sp.wait_ge(comp.turned, 16 * NB)
            ring.load(sp, 1, matrix(a["w_in"][0], O_GA))
            ring.load(sp, 0, matrix(a["w_branch_m"][0], 0))

        @block.gpsimd
        def _(pool):
            pool.wait_ge(const_in, 96)

            def load(b):
                for pg in range(NPAGE):
                    page = pool.value_load(ptab[0:1, bass.ds(b * NPAGE + pg, 1)], min_val=0, max_val=a["cache_cmp_kv"].shape[1] - 1)
                    pool.dma_start(seg[8 * pg:8 * (pg + 1)],
                                   a["cache_cmp_kv"][0, bass.ds(page, 1)].rearrange("o (n s) x g d -> (o n) s (x g d)", s=STRIDE)).then_inc(cmp_in, 16)

            load(0)
            with pool.Fori(0, NB - 1) as i:
                pool.wait_ge(comp.turned, i * 16 + 16)
                load(i + 1)

        @block.tensor
        def _(pe):
            pe.sem_inc(comp.used, 2)

            def turn(out, rows_of_queries, waits):
                if waits:
                    return pe.matmul(out, rows_of_queries, s.ident[0:QR, 0:QR], start=True, stop=True)
                return pe.transpose(out, rows_of_queries, s.ident[0:QR, 0:QR])

            with pe.Fori(0, NB) as b:
                pe.wait_ge(const_in, 96)
                pe.wait_ge(cmp_in, b * (16 * NPAGE) + 16 * NPAGE)
                pe.wait_ge(out_done, b + OUT)
                comp.tensor(pe, seg, b)
                pe.wait_ge(packed, b + 1)
                pe.wait_ge(q_set, b + 1)
                for at, n, rhs in ((0, NCMP, kc), (128, DEC, s.kT_dec[:, 0]), (160, DEC, s.kT_dec[:, 1])):
                    for p in range(2):
                        last = pe.matmul(s.ps[0:QR, 5, at:at + n], qb[:, p, :], rhs[:, p, :], start=p == 0, stop=p == 1)
                last.then_inc(small_scored, 1)

                def turn_keys(v):
                    src = slc if v < 8 else win
                    if v == 0:
                        pe.wait_ge(slc_in, b * (16 * NPAGE) + 16 * NPAGE)
                    if v == 8:
                        pe.wait_ge(win_in, b * 16 + 16)
                    pe.wait_ge(k_moved, b * KU + (v - 2 + 1 + K_MOVED))
                    for pg in range(4):
                        last = pe.transpose(s.ps[:, 6 + v % 2, P * pg:P * (pg + 1)],
                                            src[:, (4 * (v // 2) if v < 8 else 0) + pg, P * (v % 2):P * (v % 2 + 1)], s.ident[:])
                    last.then_inc(k_turned, 1)

                def score(c):
                    pe.wait_ge(k_moved, b * KU + (2 * c + 2 + K_MOVED))
                    for p in range(2):
                        last = pe.matmul(s.ps[0:QR, c, :], qb[:, p, :], kT[:, c % 2, p, :], start=p == 0, stop=p == 1)
                    last.then_inc(scored, 1)

                turn_keys(0)
                turn_keys(1)
                turn_keys(2)
                score(0)
                turn_keys(3)
                pe.wait_ge(c_prob, b + 1)
                for k in range(2):
                    last = turn(s.ps[0:NCMP, 5, 192 + QR * k:192 + QR * (k + 1)], sc[:, k, :], k == 0)
                last.then_inc(c_turned, 1)
                turn_keys(4)
                score(1)
                pe.wait_ge(c_copied, b + 1)
                pe.matmul(s.ps[0:QR, 5, 320:320 + NBLK + 1], pcT[:, 0, :], cover[:], start=True, stop=True).then_inc(imp_done, 1)
                turn_keys(5)
                turn_keys(6)
                score(2)
                pe.wait_ge(imp_copied, b + 1)
                pe.matmul(s.ps[:, 5, 360:360 + NBLK + 1], same_gt[:], imp[:, 0, :], start=True, stop=True).then_inc(imp_done, 1)
                turn_keys(7)
                turn_keys(8)
                score(3)
                turn_keys(9)
                score(4)
                for w, blocks in enumerate((range(16, 22), range(0, 8), range(8, 16))):
                    if w == 0:
                        pe.wait_ge(w_scaled, b + 1)
                    pe.wait_ge(s_scaled, b + 1)
                    if w == 2:
                        pe.wait_ge(p_moved, b * 3 + 1)
                    for n, blk in enumerate(blocks):
                        if blk < 16:
                            src = ss[:, P * blk:P * (blk + 1)]
                        elif blk < 20:
                            src = sw[:, P * (blk - 16):P * (blk - 15)]
                        else:
                            src = ss[:, PAST:NK] if blk == 20 else sw[:, WIN:NW]
                        k = P if blk < 20 else DEC
                        last = turn(s.ps[0:k, 6 + w % 2, QR * n:QR * (n + 1)], src, n == 0)
                    last.then_inc(p_turned, 1)
                pe.wait_ge(p_moved, b * 3 + 3)
                for p in range(2):
                    c = slice(P * p, P * (p + 1))
                    q = slice(32 * p, 32 * (p + 1))
                    v = slice(256 + P * p, 256 + P * (p + 1))
                    terms = [(vc[:, c], pcT[:, 1, q])] + [(slc[:, n, v], pT[:, n, q]) for n in range(16)] \
                        + [(win[:, n, v], pT[:, 16 + n, q]) for n in range(4)] \
                        + [(s.kv_dec[:, 512 * (1 + n) + 256 + P * p:512 * (1 + n) + 256 + P * (p + 1)], pT[0:DEC, 20 + n, q]) for n in range(2)]
                    for n, (lhs, rhs) in enumerate(terms):
                        last = pe.matmul(s.ps[:, 4, 32 * p:32 * (p + 1)], lhs, rhs, start=n == 0, stop=n == len(terms) - 1)
                last.then_inc(weighed, 1)

        @block.scalar
        def _(act):
            act.sem_inc(comp.moved, 2)
            act.sem_inc(k_moved, K_MOVED)
            with act.Fori(0, NB) as b:
                comp.scalar(act, b)

                def move(v):
                    act.wait_ge(k_turned, b * KU + (v + 1))
                    if v >= 4:
                        act.wait_ge(scored, b * 5 + (v // 2 - 1))
                    act.copy(kT[:, (v // 2) % 2, v % 2, :], s.ps[:, 6 + v % 2, :]).then_inc(k_moved, 1)

                move(0)
                move(1)
                act.wait_ge(c_max, b + 1)
                act.activation(sc[:, 0, :], s.ps[0:QR, 5, 0:NCMP], ACT.Exp, bias=nmax[:, 0:1], accum_out=sums[:, 0:1]).then_inc(c_exp, 1)
                for v in range(2, KU):
                    move(v)
                act.wait_ge(w_max, b + 1)
                act.activation(sw[:], sw[:], ACT.Exp, bias=nmax[:, 2:3], accum_out=sums[:, 2:3]).then_inc(w_exp, 1)
                act.wait_ge(s_max, b + 1)
                act.activation(ss[:], ss[:], ACT.Exp, bias=nmax[:, 1:2], accum_out=sums[:, 1:2]).then_inc(s_exp, 1)
                act.wait_ge(p_turned, b * 3 + 1)
                act.copy(pT[:, 16:20, :], s.ps[:, 6, 0:4 * QR].rearrange("p (a n) -> p a n", a=4))
                act.copy(pT[0:DEC, 20:22, :], s.ps[0:DEC, 6, 4 * QR:6 * QR].rearrange("p (a n) -> p a n", a=2)).then_inc(p_moved, 1)
                for w in range(1, 3):
                    act.wait_ge(p_turned, b * 3 + w + 1)
                    act.copy(pT[:, 8 * (w - 1):8 * w, :], s.ps[:, 6 + w % 2, :].rearrange("p (a n) -> p a n", a=8)).then_inc(p_moved, 1)

        @block.vector
        def _(dve):
            link = Chain(dve, step)
            dve.wait_ge(const_in, 96)
            dve.sem_inc(out_done, OUT)
            link(dve.memset(qb[:], 0.0))
            STEPS = 17
            with dve.Fori(0, NB) as b:
                link.enter(b, STEPS)
                for p in range(2):
                    for gp in range(2):
                        at = 32 * p + 16 * gp
                        last = dve.tensor_copy(qb[AD * gp:AD * (gp + 1), p, at:at + 16].rearrange("d (t r) -> d r t", t=NT),
                                               s.qT_dec[AD * gp:AD * (gp + 1), p, :, bass.ds(b * NT, NT)])
                last.then_inc(q_set, 1)
                comp.vector(dve, kc[:], vc[:], b).then_inc(packed, 1)
                dve.wait_ge(small_scored, b + 1)
                dve.tensor_reduce(nmax[:, 0:1], s.ps[0:QR, 5, 0:NCMP], X, ALU.max, negate=True).then_inc(c_max, 1)
                dve.wait_ge(c_exp, b + 1)
                link(dve.tensor_scalar(alpha[:, 0:1], sums[:, 0:1], TINY, None, ALU.max))
                link(dve.reciprocal(alpha[:, 0:1], alpha[:, 0:1]))
                link(dve.tensor_scalar(sc[:, 0, :], sc[:, 0, :], alpha[:, 0:1], None, ALU.mult))
                dve.tensor_scalar(sc[:, 1, :], sc[:, 0, :], s.gate_rows[:, bass.ds(b, 1), 0], None, ALU.mult).then_inc(c_prob, 1)
                dve.wait_ge(c_turned, b + 1)
                dve.tensor_copy(pcT[:], s.ps[0:NCMP, 5, 192:192 + 2 * QR].rearrange("p (a n) -> p a n", a=2)).then_inc(c_copied, 1)
                dve.wait_ge(imp_done, b * 2 + 1)
                dve.tensor_copy(imp[:, 0, :], s.ps[0:QR, 5, 320:320 + NBLK + 1]).then_inc(imp_copied, 1)
                dve.wait_ge(imp_done, b * 2 + 2)
                link(dve.tensor_tensor(imp[:, 1, :], s.ps[0:QR, 5, 360:360 + NBLK + 1], forced[:], ALU.add))
                for n in range(TOPK // 8):
                    dve.memset(at_wait[:, 2 * n:2 * n + 1], 0.0)
                    link(dve.max(top[:], imp[:, 1, :]))
                    dve.memset(at_wait[:, 2 * n + 1:2 * n + 2], 0.0)
                    link(dve.match_replace(imp[:, 1, :], top[:], imp[:, 1, :], -3e38))
                link(dve.tensor_scalar(imp[:, 1, :], imp[:, 1, :], -2e38, NEG, ALU.is_gt, ALU.mult))
                for c in range(4):
                    dve.wait_ge(scored, b * 5 + c + 1)
                    dve.tensor_tensor(ss[:, 512 * c:512 * (c + 1)].rearrange("p (n k) -> p n k", k=BLK),
                                      s.ps[0:QR, c, :].rearrange("p (n k) -> p n k", k=BLK),
                                      imp[:, 1, 8 * c:8 * (c + 1)].unsqueeze(2).to_broadcast([QR, 8, BLK]), ALU.add)
                new = new_add[:, bass.ds(b, 1), :].rearrange("p o n -> p (o n)")
                link(dve.tensor_tensor(ss[:, PAST:NK], s.ps[0:QR, 5, 128:128 + DEC], new, ALU.add))
                dve.tensor_reduce(nmax[:, 1:2], ss[:], X, ALU.max, negate=True).then_inc(s_max, 1)
                dve.wait_ge(scored, b * 5 + 5)
                dve.tensor_tensor(sw[:, 0:WIN], s.ps[0:QR, 4, :], win_add[:], ALU.add)
                link(dve.tensor_tensor(sw[:, WIN:NW], s.ps[0:QR, 5, 160:160 + DEC], new, ALU.add))
                dve.tensor_reduce(nmax[:, 2:3], sw[:], X, ALU.max, negate=True).then_inc(w_max, 1)
                for k, prob, expd, scaled in ((2, sw, w_exp, w_scaled), (1, ss, s_exp, s_scaled)):
                    dve.wait_ge(expd, b + 1)
                    link(dve.tensor_scalar(alpha[:, k:k + 1], sums[:, k:k + 1], TINY, None, ALU.max))
                    link(dve.reciprocal(alpha[:, k:k + 1], alpha[:, k:k + 1]))
                    link(dve.tensor_tensor(alpha[:, k:k + 1], alpha[:, k:k + 1], s.gate_rows[:, bass.ds(b, 1), k], ALU.mult))
                    dve.tensor_scalar(prob[:], prob[:], alpha[:, k:k + 1], None, ALU.mult).then_inc(scaled, 1)
                dve.wait_ge(weighed, b + 1)
                for gp in range(2):
                    for odd in range(2):
                        out = s.hat[AD * odd:AD * (odd + 1), :, bass.ds(b * NT + SEQ, NT)] \
                            .rearrange("d (p g h) t -> d g p h t", p=2, g=2)[:, gp]
                        o = s.ps[AD * gp:AD * (gp + 1), 4, 0:2 * 32].rearrange("d (p g t h o) -> d g o p h t", p=2, g=2, t=NT, o=2)
                        last = dve.tensor_copy(out, o[:, gp, odd])
                last.then_inc(out_done, 1)
                link.leave(NB)


def block_modulation_rest(nc, s):
    a, ring = s.args, s.ring
    C = DEC + 1
    CHUNKS = (4, 5, 10, 11, 6, 7, 8, 9)
    with ExitStack() as ctx:
        sb = lambda name, shape: ctx.enter_context(nc.sbuf_tensor(name, shape, F32))
        sem = lambda name: s.semaphore("r_" + name)
        bias = sb("multiplier_bias", [C, 2, D])
        gain = sb("post_gain", [C, 2, D])
        gt = sb("residual_multipliers", [C, 2, D])
        rows_in, made, read, ready, stored, step = [sem(n) for n in ("rows_in", "made", "read", "ready", "stored", "step")]
        block = ctx.enter_context(nc.Block())

        @block.sync
        def _(sp):
            for n, g in enumerate(("g_post_mix", "g_post_ffn")):
                at = (2 + 3 * n) * D
                sp.dma_start(bias[:, n, :], a["b_ada"][0, at:at + D].partition_broadcast(C)).then_inc(rows_in, 16)
                sp.dma_start(gain[:, n, :], a[g][0].partition_broadcast(C)).then_inc(rows_in, 16)
            for n, c in enumerate(CHUNKS):
                ring.load(sp, n % 2, matrix(a["w_ada"][0], 512 * c), after=(made, n - 1) if n >= 2 else None)
            sp.wait_ge(ready, 4)
            sp.dma_start(s.multiplier_rows, gt[:]).then_inc(stored, 16)
            sp.wait_ge(stored, 16)

        @block.tensor
        def _(pe):
            for n in range(len(CHUNKS)):
                ring.await_load(pe, n % 2)
                if n >= 2:
                    pe.wait_ge(read, n - 1)
                w = ring.view(n % 2)
                if n < 4:
                    for k in range(KT):
                        last = pe.matmul(s.ps[0:C, n % 2, :], s.cT[:, k, :], w[:, k, :], start=k == 0, stop=k == KT - 1)
                else:
                    for j in range(4):
                        for k in range(KT):
                            last = pe.matmul(s.ps[:, n % 2, j * C:(j + 1) * C], w[:, k, j * P:(j + 1) * P], s.cT[:, k, :],
                                             start=k == 0, stop=k == KT - 1)
                last.then_inc(made, 1)

        @block.vector
        def _(dve):
            link = Chain(dve, step)
            dve.wait_ge(rows_in, 64)
            for n in range(len(CHUNKS)):
                dve.wait_ge(made, n + 1)
                if n < 4:
                    c = slice(512 * (n % 2), 512 * (n % 2 + 1))
                    out = gt[:, n // 2, c]
                    dve.tensor_tensor(out, s.ps[0:C, n % 2, :], bias[:, n // 2, c], ALU.add).then_inc(read, 1)
                    dve.wait_ge(read, n + 1)
                    dve.tensor_tensor(out, out, gain[:, n // 2, c], ALU.mult).then_inc(ready, 1)
                else:
                    j = 4 * (n - 4)
                    dve.tensor_tensor(s.mod[:, 16 + j:20 + j, :], s.ps[:, n % 2, 0:4 * C].rearrange("p (j n) -> p j n", j=4),
                                      s.vecT[:, 0, V_SHF + j:V_SHF + j + 4].unsqueeze(2).to_broadcast([P, 4, C]),
                                      ALU.add).then_inc(read, 1)
            dve.wait_ge(read, len(CHUNKS))
            link(dve.scalar_tensor_tensor(s.mod[:, 24:32, :], s.mod[:, 24:32, :], 1.0,
                                          s.vecT[:, 0, V_GF:V_GF + 8].unsqueeze(2).to_broadcast([P, 8, C]),
                                          ALU.add, ALU.mult))


def block_branches(nc, s, mix):
    a, ring = s.args, s.ring
    w_in, w_m, w_a = a["w_in"][0], a["w_branch_m"][0], a["w_branch_a"][0]
    CHUNKS = [c for h in range(2) for c in ((w_in, O_GA + 512 * h, s.ht), (w_m, 512 * h, s.hmt),
                                            (w_in, O_GA + D + 512 * h, s.ht), (w_a, 512 * h, s.hat))]
    with ExitStack() as ctx:
        sem = lambda name: s.semaphore("b_" + name)
        sg = ctx.enter_context(nc.sbuf_tensor("gate", [P, 2, 4, TOK], F32))
        gate_done, gate_free, branch_done, branch_free, gated, step = [sem(n) for n in (
            "gate_done", "gate_free", "branch_done", "branch_free", "gated", "step")]
        block = ctx.enter_context(nc.Block())

        @block.sync
        def _(sp):
            for n in range(2, len(CHUNKS)):
                w, c, _ = CHUNKS[n]
                ring.load(sp, (n + 1) % 2, matrix(w, c), after=(branch_done if n % 2 else gate_done, 4 * (n // 2)))
            ring.load(sp, 1, matrix(a["w_out"][0], 0), after=(gate_done, 16))
            ring.load(sp, 0, matrix(a["w_out"][0], 512), after=(branch_done, 16))

        @block.tensor
        def _(pe):
            for n in range(len(CHUNKS)):
                ring.await_load(pe, (n + 1) % 2)
                if n % 2 == 0:
                    fm_units(pe, ring.view(1), CHUNKS[n][2], s.ps, branch_free, gate_done, 4 * (n // 2))
                else:
                    fm_units(pe, ring.view(0), CHUNKS[n][2], s.ps, gate_free, branch_done, 4 * (n // 2))

        @block.scalar
        def _(act):
            for m in range(16):
                act.wait_ge(gate_done, m + 1)
                if m >= 8:
                    act.wait_ge(gated, m - 7)
                c, h, j = m // 4 % 2, m // 8, m % 4
                bias = s.vecT[:, 0, (V_GB if c else V_GA) + 4 * h + j:(V_GB if c else V_GA) + 4 * h + j + 1]
                act.activation(halves(sg[:, c, j, :]), fm(s.ps, m), ACT.Sigmoid, bias=bias).then_inc(gate_free, 1)

        @block.vector
        def _(dve):
            dve.sem_inc(branch_free, 4)
            link = Chain(dve, step)
            for m in range(16):
                dve.wait_ge(branch_done, m + 1)
                dve.wait_ge(gate_free, m + 1)
                c, h, j = m // 4 % 2, m // 8, m % 4
                out = mix[:, 4 * h + j, :]
                if c == 0:
                    dve.tensor_tensor(halves(out), fm(s.ps, m), halves(sg[:, c, j, :]), ALU.mult).then_inc(branch_free, 1)
                    dve.sem_inc(gated, 1)
                else:
                    dve.tensor_tensor(halves(sg[:, c, j, :]), fm(s.ps, m), halves(sg[:, c, j, :]), ALU.mult).then_inc(branch_free, 1)
                    dve.wait_ge(branch_free, m + 5)
                    dve.tensor_tensor(out, out, sg[:, c, j, :], ALU.add).then_inc(gated, 1)


def block_project(nc, s, name, lhs, parts, slot, which, loads, x_src=None, y_dst=None):
    with ExitStack() as ctx:
        sb = lambda n, shape: ctx.enter_context(nc.sbuf_tensor(f"{name}_{n}", shape, F32))
        sem = lambda n: s.semaphore(f"{name}_{n}")
        y = sb("y", [P, TILES, D])
        junk = sb("squares", [P, 2, 512])
        gt = sb("residual_multiplier", [DEC + 1, D])
        prompt_row = sb("prompt_row", [DEC + 1, P])
        ss = sb("square_sums", [P, TILES, 2])
        rs = sb("inverse_rms", [P, TILES])
        gt_in, x_in, row_set, spread, done, used, copied, squared, summed, rooted, scaled, added, out, step = [sem(n) for n in (
            "multiplier_in", "x_in", "row_set", "spread", "done", "used", "copied", "squared", "summed", "rooted", "scaled", "added", "out",
            "step")]
        block = ctx.enter_context(nc.Block())
        ktiles = max(k0 + n for _, k0, n in parts)

        @block.sync
        def _(sp):
            sp.dma_start(gt[:], s.multiplier_rows[:, which, :]).then_inc(gt_in, 16)
            if x_src is not None:
                for t in range(TILES):
                    sp.dma_start(s.x[0:rows(t), t, :], x_src(t)).then_inc(x_in, 16)
            loads(sp, used)
            if y_dst is not None:
                for t in range(TILES):
                    sp.wait_ge(added, t + 1)
                    sp.dma_start(y_dst(t), s.x[0:rows(t), t, :]).then_inc(out, 16)
                sp.wait_ge(out, 16 * TILES)

        @block.tensor
        def _(pe):
            pe.wait_ge(row_set, 1)
            pe.wait_ge(gt_in, 16)
            for h in range(2):
                last = pe.matmul(s.ps[:, 6 + h, :], prompt_row[:], gt[:, 512 * h:512 * (h + 1)], start=True, stop=True)
            last.then_inc(spread, 1)
            for n, (h, k0, nk) in enumerate(parts):
                s.ring.await_load(pe, (slot + n) % 2)
                w = s.ring.view((slot + n) % 2)
                for t in range(TILES):
                    if h == 1 and k0 == 0:
                        pe.wait_ge(copied, t + 1)
                    for k in range(nk):
                        last = pe.matmul(s.ps[0:rows(t), t, :], lhs[:, k0 + k, cols(t)], w[:, k, :],
                                         start=k0 + k == 0, stop=k0 + k == ktiles - 1)
                    if k0 + nk == ktiles:
                        last.then_inc(done, 1)
                    elif t == PT_:
                        last.then_inc(used, 1)
                if k0 + nk == ktiles:
                    pe.wait_ge(done, TILES * (h + 1))
                    pe.sem_inc(used, 1)

        @block.scalar
        def _(act):
            for m in range(2 * TILES):
                h, t = m // TILES, m % TILES
                act.wait_ge(copied, m + 1)
                if m >= 2:
                    act.wait_ge(squared, m - 1)
                act.activation(junk[0:rows(t), m % 2, :], y[0:rows(t), t, 512 * h:512 * (h + 1)], ACT.Square,
                               accum_out=ss[0:rows(t), t, h:h + 1]).then_inc(squared, 1)
                if h == 1:
                    act.wait_ge(summed, t + 1)
                    act.activation(rs[0:rows(t), t:t + 1], ss[0:rows(t), t, 0:1], ACT.Sqrt).then_inc(rooted, 1)

        @block.vector
        def _(dve):
            link = Chain(dve, step)
            link(dve.memset(prompt_row[:], 0.0))
            dve.memset(prompt_row[DEC:DEC + 1, :], 1.0).then_inc(row_set, 1)
            for m in range(2 * TILES):
                h, t = m // TILES, m % TILES
                r = rows(t)
                dve.wait_ge(done, m + 1)
                dve.tensor_copy(y[0:r, t, 512 * h:512 * (h + 1)], s.ps[0:r, t, :]).then_inc(copied, 1)
                if h == 1:
                    dve.wait_ge(squared, m + 1)
                    link(dve.tensor_tensor(ss[0:r, t, 0:1], ss[0:r, t, 0:1], ss[0:r, t, 1:2], ALU.add))
                    dve.tensor_scalar(ss[0:r, t, 0:1], ss[0:r, t, 0:1], 1.0 / D, EPS, ALU.mult, ALU.add).then_inc(summed, 1)
                    dve.wait_ge(rooted, t + 1)
                    link(dve.reciprocal(rs[0:r, t:t + 1], rs[0:r, t:t + 1]))
                    if t == 0:
                        dve.wait_ge(spread, 1)
                        dve.wait_ge(gt_in, 16)
                    row = s.ps[:, 6:8, :].rearrange("p a n -> p (a n)") if t < PT_ else gt[0:DEC, :]
                    dve.scalar_tensor_tensor(y[0:r, t, :], y[0:r, t, :], rs[0:r, t:t + 1], row, ALU.mult, ALU.mult).then_inc(scaled, 1)

        @block.gpsimd
        def _(pool):
            if x_src is not None:
                pool.wait_ge(x_in, 16 * TILES)
            for t in range(TILES):
                pool.wait_ge(scaled, t + 1)
                pool.tensor_tensor(s.x[0:rows(t), t, :], s.x[0:rows(t), t, :], y[0:rows(t), t, :], ALU.add).then_inc(added, 1)


def block_ffn_up(nc, s, act_fm, load_up, load_down):
    a, ring = s.args, s.ring
    LOADS = FT // 2
    UW = 2 + SEQ + NB * (2 + NT)
    NST = 2 * NB
    NR = 2 * FT // 4
    with ExitStack() as ctx:
        sb = lambda name, shape: ctx.enter_context(nc.sbuf_tensor(name, shape, F32))
        sem = lambda name: s.semaphore("u_" + name)
        u = sb("u", [P, 2, 4, UW])
        cv = sb("conv", [P, 2, 4, UW])
        state_rows = sb("conv_state_rows", [NST + 2, 2 * DFF])
        before = sb("u_before", [P, 2 * FT, NST])
        after = sb("u_after", [P, 2 * FT, NST + 2])
        (state_in, state_turned, state_moved, zeroed, done, free, before_set, first, second, third, gelu, made, kept,
         back_turned, back_moved, stored) = [sem(n) for n in (
             "state_in", "state_turned", "state_moved", "zeroed", "done", "free", "before_set", "first_tap", "second_tap",
             "third_tap", "gelu", "made", "last_rows_kept", "back_turned", "back_moved", "stored")]
        block = ctx.enter_context(nc.Block())
        decode = lambda ap: ap[:, 2 + SEQ:UW].rearrange("p (b t) -> p b t", b=NB)

        def tile(j, m):
            return j * 2 + (m % 2 + FT * (m // 2))

        def loop(eng, body):
            with eng.Fori(0, LOADS // 2) as i:
                for e in range(2):
                    body(i * 2 + e, e, i)
            body(LOADS - 1, 0, None)

        @block.sync
        def _(sp):
            sp.dma_start(state_rows[0:NST, :], a["state_conv"][0].rearrange("b r n -> (b r) n")).then_inc(state_in, 16)
            with sp.Fori(0, LOADS // 2 - 1) as i:
                for e in range(2):
                    sp.wait_ge(done, i * 8 + 4 * (e + 1))
                    load_up(sp, i * 2 + (2 + e), 1 - e)
            sp.wait_ge(done, 4 * (LOADS - 2))
            load_up(sp, LOADS - 1, 1)
            sp.wait_ge(done, 4 * (LOADS - 1))
            load_down(sp, 0, 0)
            sp.wait_ge(done, 4 * LOADS)
            load_down(sp, 1, 1)
            sp.wait_ge(back_moved, NR)
            sp.dma_start(a["s_conv"][0].rearrange("b r n -> (b r) n"), state_rows[0:NST, :]).then_inc(stored, 16)
            sp.dma_start(a["p_conv"][0, 0], state_rows[NST:NST + 2, :]).then_inc(stored, 16)
            sp.wait_ge(stored, 32)

        @block.tensor
        def _(pe):
            pe.wait_ge(state_in, 16)
            for f in range(2 * FT):
                last = pe.transpose(s.ps[:, f // FT, NST * (f % FT):NST * (f % FT + 1)], state_rows[0:NST, P * f:P * (f + 1)],
                                    s.ident[0:NST, 0:NST])
            last.then_inc(state_turned, 1)
            pe.wait_ge(state_moved, 1)

            def product(j, e, i):
                turns = 1 if i is None else LOADS // 2
                ring.await_load(pe, 1 - e, turn=i, turns=turns, parts=2)
                fm_units(pe, ring.view(1 - e), s.ht, s.ps, free, done, j * 4)

            loop(pe, product)
            pe.wait_ge(free, 4 * LOADS + 4)
            pe.wait_ge(kept, 4 * LOADS + 8)
            for n in range(NR):
                if n >= 8:
                    pe.wait_ge(back_moved, n - 7)
                for f in range(4):
                    last = pe.transpose(s.ps[0:NST + 2, n % 8, P * f:P * (f + 1)], after[:, 4 * n + f, :], s.ident[:])
                last.then_inc(back_turned, 1)

        @block.scalar
        def _(act):
            act.sem_inc(free, 4)

            def taps(j, e, units):
                for m in units:
                    n = j * 4 + m
                    act.wait_ge(done, n + 1)
                    act.wait_ge(third, n + 1)
                    act.wait_ge(kept, n + 1)
                    act.copy(u[:, e, m, 2:2 + HALF], s.ps[:, 2 * m, 0:HALF])
                    act.copy(u[:, e, m, 2 + HALF:2 + SEQ], s.ps[:, 2 * m + 1, 0:SEQ - HALF])
                    act.copy(decode(u[:, e, m, :])[:, :, 2:2 + NT],
                             s.ps[:, 2 * m + 1, SEQ - HALF:HALF].rearrange("p (b t) -> p b t", b=NB)).then_inc(free, 1)
                    act.wait_ge(free, n + 5)
                    act.wait_ge(before_set, n + 1)
                    act.wait_ge(made, j * 2 + (1 + m % 2))
                    act.wait_ge(state_moved, 1)
                    f = tile(j, m)
                    act.activation(cv[:, e, m, 2:UW], u[:, e, m, 2:UW], ACT.Identity, scale=s.vecT[:, 2, bass.ds(f, 1)],
                                   bias=s.vecT[:, 2, bass.ds(f + 2 * FT, 1)]).then_inc(first, 1)

            def gelus(j, e):
                for m in (2, 3):
                    act.wait_ge(third, j * 4 + (m + 1 + 8))
                    act.activation(cv[:, e, m, 2:UW], cv[:, e, m, 2:UW], ACT.Gelu_apprx_tanh).then_inc(gelu, 1)

            with act.Fori(0, LOADS // 2) as i:
                taps(i * 2, 0, range(4))
                taps(i * 2 + 1, 1, (0, 1))
                gelus(i * 2, 0)
                taps(i * 2 + 1, 1, (2, 3))
                gelus(i * 2 + 1, 1)
            taps(LOADS - 1, 0, range(4))
            gelus(LOADS - 1, 0)

        @block.vector
        def _(dve):
            dve.sem_inc(third, 8)
            dve.sem_inc(made, 4)
            dve.wait_ge(state_turned, 1)
            dve.tensor_copy(before[:].rearrange("p (a f) n -> p a (f n)", a=2), s.ps[:, 0:2, 0:FT * NST]).then_inc(state_moved, 1)

            def taps(j, e, units):
                for m in units:
                    dve.wait_ge(first, j * 4 + (m + 1))
                    dve.scalar_tensor_tensor(cv[:, e, m, 2:UW], u[:, e, m, 1:UW - 1], s.vecT[:, 1, bass.ds(tile(j, m) + 2 * FT, 1)],
                                             cv[:, e, m, 2:UW], ALU.mult, ALU.add).then_inc(second, 1)
                for m in units:
                    dve.wait_ge(second, j * 4 + (m + 1))
                    dve.scalar_tensor_tensor(cv[:, e, m, 2:UW], u[:, e, m, 0:UW - 2], s.vecT[:, 1, bass.ds(tile(j, m), 1)],
                                             cv[:, e, m, 2:UW], ALU.mult, ALU.add).then_inc(third, 1)

            def product(j, e):
                for m in range(2):
                    dve.wait_ge(gelu, j * 2 + (m + 1))
                    out = act_fm[:, bass.ds(j * 2 + m, 1), :]
                    dve.tensor_tensor(out[:, :, 0:SEQ], cv[:, e, m, 2:2 + SEQ].unsqueeze(1), cv[:, e, 2 + m, 2:2 + SEQ].unsqueeze(1), ALU.mult)
                    dve.tensor_tensor(out[:, :, SEQ:TOK].rearrange("p o (b t) -> p (o b) t", b=NB), decode(cv[:, e, m, :])[:, :, 2:2 + NT],
                                      decode(cv[:, e, 2 + m, :])[:, :, 2:2 + NT], ALU.mult).then_inc(made, 1)

            with dve.Fori(0, LOADS // 2) as i:
                taps(i * 2, 0, (0, 1))
                taps(i * 2, 0, (2, 3))
                taps(i * 2 + 1, 1, (0, 1))
                product(i * 2, 0)
                taps(i * 2 + 1, 1, (2, 3))
                product(i * 2 + 1, 1)
            taps(LOADS - 1, 0, (0, 1))
            taps(LOADS - 1, 0, (2, 3))
            product(LOADS - 1, 0)
            for n in range(NR):
                dve.wait_ge(back_turned, n + 1)
                dve.tensor_copy(state_rows[:, 4 * P * n:4 * P * (n + 1)], s.ps[0:NST + 2, n % 8, :]).then_inc(back_moved, 1)

        @block.gpsimd
        def _(pool):
            pool.memset(u[:, :, :, 0:2], 0.0).then_inc(zeroed, 1)
            pool.sem_inc(kept, 8)
            pool.wait_ge(zeroed, 1)

            def earlier(j, e, m):
                n = j * 4 + m
                pool.wait_ge(third, n + 1)
                pool.wait_ge(state_moved, 1)
                pool.tensor_copy(decode(u[:, e, m, :])[:, :, 0:2],
                                 before[:, bass.ds(tile(j, m), 1), :].rearrange("p o (b t) -> p (o b) t", b=NB)).then_inc(before_set, 1)

            def keep(j, e, m):
                out = after[:, bass.ds(tile(j, m), 1), :]
                pool.wait_ge(free, j * 4 + (m + 5))
                pool.wait_ge(state_moved, 1)
                pool.tensor_copy(out[:, :, 0:NST].rearrange("p o (b t) -> p (o b) t", b=NB), decode(u[:, e, m, :])[:, :, NT:NT + 2])
                pool.tensor_copy(out[:, :, NST:NST + 2], u[:, e, m, SEQ:SEQ + 2].unsqueeze(1)).then_inc(kept, 1)

            def body(j, e, i):
                for m in range(4):
                    earlier(j, e, m)
                    keep(j, e, m)

            loop(pool, body)


def program(nc, args):
    with ExitStack() as ctx:
        sb = lambda name, shape: ctx.enter_context(nc.sbuf_tensor(name, shape, F32))
        s = Shared(args)
        semaphores = []

        def semaphore(name):
            semaphores.append(nc.alloc_semaphore(name))
            return semaphores[-1]

        s.semaphore = semaphore
        s.ps = ctx.enter_context(nc.psum_tensor("ps", [P, 8, 512], F32))
        s.ring = Ring(nc, ctx)
        s.ident = sb("ident_sb", [P, P])
        s.vecT = sb("vector_columns", [P, 3, NC2])
        s.mod = sb("modulation", [P, 32, DEC + 1])
        s.cT = sb("c_columns", [P, KT, DEC + 1])
        s.ht = sb("h_fm", [P, KT, TOK])
        carry = s.carry = sb("mlstm_fm_then_residual", [P, TILES * D])
        s.hmt = carry[:, 0:KT * TOK].rearrange("p (k n) -> p k n", k=KT)
        block_modulation(nc, s)
        with ExitStack() as inner:
            s.x = inner.enter_context(nc.sbuf_tensor("x1", [P, TILES, D], F32))
            block_norm(nc, s, "n1", lambda t: token_rows(args["x_prompt"], args["x_sample"], t), 0, 8)
        with ExitStack() as inner:
            mb = lambda name, shape: inner.enter_context(nc.sbuf_tensor(name, shape, F32))
            s.qk = mb("qk_fm", [P, 2 * KT, TOK])
            s.va = mb("v_and_ones", [P, TILES, MH, MD + 1])
            s.og = mb("output_gates", [P, TILES, D])
            s.mneg = mb("minus_m", [P, MH, TOK])
            s.gates = mb("gate_rows", [MH, 2, TOK])
            s.gate_bias = mb("gate_bias", [MH, 2])
            s.head_row = mb("head_row_sb", [MH, MH, P])
            s.gcol = mb("gate_columns", [P, TILES, 3, MH])
            s.acol = mb("a_columns", [DEC, MH])
            s.alast = mb("a_last", [MH, NB])
            s.decay = mb("decay", [P, MH, NB])
            s.hdec = mb("h_dec", [DEC, MH, MD])
            block_mlstm_in(nc, s)
            with ExitStack() as g:
                s.norm_w = g.enter_context(nc.sbuf_tensor("norm_w", [P, D], F32))
                block_mlstm_gates(nc, s)
            block_mlstm_prompt(nc, s)
            block_mlstm_decode(nc, s)
            block_mlstm_out(nc, s)
        s.multiplier_rows = nc.dram_tensor("multiplier_rows", (DEC + 1, 2, D), F32, kind="Internal").ap()
        up, down = args["w_up"][0], args["w_down"][0]

        def load_up(sp, j, buffer, after=None):
            for n in range(2):
                s.ring.load(sp, buffer, matrix(up, j * 256 + n * DFF, 256), after=None if n else after,
                            dst=s.ring.view(buffer)[:, :, 256 * n:256 * (n + 1)])

        DOWN = [(h, k, min(KT, FT - k)) for h in range(2) for k in range(0, FT, KT)]

        def load_down(sp, n, buffer, after=None):
            h, k, nk = DOWN[n]
            s.ring.load(sp, buffer, matrix(down[k * P:(k + nk) * P], 512 * h, k=nk), after=after,
                        dst=s.ring.view(buffer)[:, 0:nk, :])

        with ExitStack() as mixer:
            at = lambda name, shape: mixer.enter_context(nc.sbuf_tensor(name, shape, F32))
            s.hat = at("attention_fm", [P, KT, TOK])
            with ExitStack() as attention:
                ab = lambda name, shape: attention.enter_context(nc.sbuf_tensor(name, shape, F32))
                s.kv_dec = ab("kv_dec", [DEC, 1536])
                s.qT_dec = ab("qT_dec", [P, 2, R, DEC])
                s.kT_dec = ab("kT_dec", [P, 2, 2, DEC])
                s.branch_gates = ab("branch_gates", [P, TILES, 48])
                s.gate_rows = ab("gate_rows_dec", [QR, NB, 3])
                s.gate_scratch = nc.dram_tensor("gate_scratch", (DEC, 48), F32, kind="Internal").ap()
                s.w1 = ab("cmp_w1_sb", [P, 2, STRIDE, 2, AD])
                s.w2 = ab("cmp_w2_sb", [AD, 2, AD])
                s.pe_bias = ab("pe_bias", [AD, 2])
                with ExitStack() as inner:
                    pb = lambda name, shape: inner.enter_context(nc.sbuf_tensor(name, shape, F32))
                    s.kv = pb("kv_prompt", [P, PT_, 1536])
                    s.kT = pb("kT_prompt", [P, 2, 2, SEQ])
                    s.qT = pb("qT_prompt", [P, 2, R, SEQ])
                    s.kc_p = pb("kc_prompt", [P, 2, PCMP])
                    s.vc_p = pb("vc_prompt", [PCMP, G * AD])
                    with ExitStack() as g:
                        s.q_tm = g.enter_context(nc.sbuf_tensor("q_tm", [P, TILES, D], F32))
                        block_attention_in(nc, s)
                        block_attention_turn(nc, s)
                    block_modulation_rest(nc, s)
                    block_compress_prompt(nc, s)
                    s.ha = pb("attention_tm", [P, PT_, D])
                    block_attention_prompt(nc, s)
                    block_attention_out(nc, s)
                block_attention_decode(nc, s)
            nc.clear_and_free_semaphores(semaphores)
            nc.all_engine_barrier()
            mix = at("mixed_fm", [P, KT, TOK])
            block_branches(nc, s, mix)
            s.x = carry[:].rearrange("p (t n) -> p t n", t=TILES)

            def loads(sp, used):
                load_up(sp, 0, 1, after=(used, 1))
                load_up(sp, 1, 0, after=(used, 2))

            block_project(nc, s, "mixer_out", mix, [(0, 0, KT), (1, 0, KT)], 1, 0, loads,
                          x_src=lambda t: token_rows(args["x_prompt"], args["x_sample"], t))
        block_norm(nc, s, "n2", None, 16, 24)
        act_fm = sb("ffn_hidden_fm", [P, FT, TOK])
        block_ffn_up(nc, s, act_fm, load_up, load_down)

        def loads(sp, used):
            for n in range(2, len(DOWN)):
                load_down(sp, n, n % 2, after=(used, n - 1))

        block_project(nc, s, "ffn_out", act_fm, DOWN, 0, 1, loads,
                      y_dst=lambda t: token_rows(args["y_prompt"], args["y_sample"], t))
INPUTS = ["x_prompt", "x_sample", "cache_cmp_kv", "cache_slc_kv", "cache_win_kv", "state_C", "state_n", "state_m",
          "state_conv", "page_table", "c_prompt", "c_sample", "w_ada", "b_ada", "g_pre_mix", "g_post_mix", "g_pre_ffn",
          "g_post_ffn", "w_in", "b_in", "m_norm_w", "cmp_w1", "cmp_pe", "cmp_w2", "w_branch_m", "w_branch_a", "w_out",
          "w_up", "conv_w", "conv_b", "w_down"]
KV = (2, G, AD)
OUTPUTS = {"y_prompt": (1, SEQ, D), "y_sample": (NB, NT, D), "p_cmp": (1, 1, SEQ, *KV), "p_slc": (1, 1, SEQ, *KV),
           "p_win": (1, 1, SEQ, *KV), "p_C": (1, 1, MH, MD, MD), "p_n": (1, 1, MH, MD), "p_m": (1, 1, MH),
           "p_conv": (1, 1, 2, 2 * DFF), "s_cmp": (1, NB, NT, *KV), "s_slc": (1, NB, NT, *KV),
           "s_win": (1, NB, WIN, *KV), "s_C": (1, NB, MH, MD, MD), "s_n": (1, NB, MH, MD), "s_m": (1, NB, MH),
           "s_conv": (1, NB, 2, 2 * DFF)}


def kernel(**inputs):
    import numpy as _np
    import concourse.bacc as _bacc
    from concourse import mybir as _mybir
    from concourse.bass_utils import run_bass_kernel_spmd as _run

    nc = _bacc.Bacc("TRN2", target_bir_lowering=False, num_devices=1)
    arrays = {name: _np.ascontiguousarray(inputs[name]) for name in INPUTS}
    arrays.update(constants())
    args = {n: nc.dram_tensor("in_" + n, v.shape, _mybir.dt.from_np(v.dtype), kind="ExternalInput").ap()
            for n, v in arrays.items()}
    args.update({n: nc.dram_tensor("out_" + n, shape, F32, kind="ExternalOutput").ap() for n, shape in OUTPUTS.items()})
    program(nc, args)
    r = _run(nc, [{"in_" + n: v for n, v in arrays.items()}], core_ids=[0])
    return tuple(r.results[0]["out_" + n] for n in OUTPUTS)
```

```python
from contextlib import ExitStack

import numpy as np
import concourse.bass as bass
from concourse import mybir

F32 = mybir.dt.float32
F32R = mybir.dt.float32r
BF16 = mybir.dt.bfloat16
I32 = mybir.dt.int32
ALU = mybir.AluOpType
ACT = mybir.ActivationFunctionType
X = mybir.AxisListType.X

P = 128
D = 1024
KT = D // P
SEQ, NB, NT = 512, 8, 4
DEC = NB * NT
TOK = SEQ + DEC
HALF = TOK // 2
PT_ = SEQ // P
TILES = PT_ + 1
MH, MD = 4, 256
AH, AD, G, R = 16, 64, 4, 4
ROPE = 8
PAST, PAGE = 2048, 128
NPAGE = PAST // PAGE
STRIDE = 16
NSEG, NCMP = PAST // STRIDE, PAST // STRIDE - 1
PSEG, PCMP = SEQ // STRIDE, SEQ // STRIDE - 1
BLK, TOPK = 64, 16
NBLK = PAST // BLK
WIN = 512
DFF = 2816
FT = DFF // P
QR = G * NT * R
EPS = 1e-6
NEG = -1e30
TINY = 1.17549435e-38

O_MI, O_AQ, O_AG, O_GA = 4096, 4104, 6664, 6712
V_SHM, V_SCM, V_SHF, V_SCF, V_GM, V_GF, V_MQ, V_MK, V_GA, V_GB = range(0, 80, 8)
NV, NC2 = 80, 88


def rows(tile):
    return P if tile < PT_ else DEC


def cols(tile):
    return slice(tile * P, tile * P + rows(tile))


class Shared:

    def __init__(self, args):
        self.args = args


class Chain:

    def __init__(self, eng, sem):
        self.eng, self.sem, self.n, self.turn, self.steps = eng, sem, 0, None, 0

    def __call__(self, ins):
        ins.then_inc(self.sem, 1)
        self.n += 1
        self.eng.wait_ge(self.sem, self.n if self.turn is None else self.turn * self.steps + self.n)

    def enter(self, turn, steps):
        self.turn, self.steps, self.at = turn, steps, self.n

    def leave(self, turns):
        assert self.n - self.at == self.steps, (self.n - self.at, self.steps)
        self.n, self.turn = self.at + turns * self.steps, None


class Ring:

    def __init__(self, nc, ctx):
        self.whole = ctx.enter_context(nc.sbuf_tensor("weights", [P, 2 * KT * 512], F32))
        self.tail = self.whole[:, KT * 512:]
        self.buf = [self.whole[:, KT * 512 * s:KT * 512 * (s + 1)] for s in range(2)]
        self.loaded = [nc.alloc_semaphore(f"weights_loaded{s}") for s in range(2)]
        self.cuts, self.ready = nc.alloc_semaphore("weights_cut"), nc.alloc_semaphore("weights_ready")
        self.uses, self.done = [0, 0], 0

    def view(self, s, width=512):
        return self.buf[s][:, 0:KT * width].rearrange("p (k n) -> p k n", k=KT)

    def load(self, sp, s, src, after=None, dst=None):
        if after is not None:
            sp.wait_ge(*after)
        sp.dma_start(self.view(s) if dst is None else dst, src).then_inc(self.loaded[s], 16)

    def await_load(self, pe, s, turn=None, turns=1, parts=1):
        n = 16 * (self.uses[s] + parts)
        pe.wait_ge(self.loaded[s], n if turn is None else turn * (16 * parts) + n)
        self.uses[s] += parts * turns


    def begin(self, first, parts=1):
        self.first, self.parts = first, parts

    def room(self, nc, ctx, name):
        self.rounded = ctx.enter_context(nc.sbuf_tensor(name + "_split_weights", [P, 2, 2, KT * 256], F32R))

    def part(self, k):
        s = (self.first + k) % 2
        return s, self.whole[:, KT * 256 * s:KT * 256 * (s + 1)]

    def load_part(self, sp, k, src, after=None, piece=None):
        s, raw = self.part(k)
        if after is not None:
            sp.wait_ge(*after)
        n = src.shape[2]
        dst = raw[:, 0:src.shape[1] * n].rearrange("p (k n) -> p k n", n=n) if piece is None else \
            raw.rearrange("p (k n) -> p k n", k=KT)[:, :, piece]
        sp.dma_start(dst, src).then_inc(self.loaded[s], 16)

    def cut(self, act, k, turn=None, per=0):
        s, raw = self.part(k)
        n = 16 * (self.uses[s] + self.parts * (k // 2 + 1))
        act.wait_ge(self.loaded[s], n if turn is None else turn * (8 * per * self.parts) + n)
        act.copy(self.rounded[:, s, 0, :], raw).then_inc(self.cuts, 1)

    def rest(self, dve, k, turn=None, per=0):
        s, raw = self.part(k)
        n = self.done + k + 1
        dve.wait_ge(self.cuts, n if turn is None else turn * per + n)
        dve.tensor_tensor(self.rounded[:, s, 1, :], raw, self.rounded[:, s, 0, :], ALU.subtract).then_inc(self.ready, 1)

    def await_ready(self, pe, k, turn=None, per=0):
        n = self.done + k + 1
        pe.wait_ge(self.ready, n if turn is None else turn * per + n)

    def split(self, k, n=256):
        return [self.rounded[:, self.part(k)[0], low, :].rearrange("p (k n) -> p k n", n=n) for low in range(2)]

    def end(self, loads):
        for k in range(loads):
            self.uses[(self.first + k) % 2] += self.parts
        self.done += loads


def cut_tiles(act, src, high, sem):
    for k in range(src.shape[1]):
        act.copy(high[:, k, :], src[:, k, :]).then_inc(sem, 1)


def rest_tiles(dve, src, high, low, cut, sem, at=0):
    for k in range(src.shape[1]):
        dve.wait_ge(cut, at + k + 1)
        dve.tensor_tensor(low[:, k, :], src[:, k, :], high[:, k, :], ALU.subtract).then_inc(sem, 1)


def fm_split_unit(pe, w, c0, rhs, out, await_tile=None):
    (wh, wl), (xh, xl) = w, rhs
    terms = ((wh, xh), (wh, xl), (wl, xh))
    for k in range(KT):
        if await_tile is not None:
            await_tile(k)
        for n, (a, b) in enumerate(terms):
            for half in range(2):
                last = pe.matmul(out(half), a[:, k, c0:c0 + P], b[:, k, half * HALF:(half + 1) * HALF],
                                 start=k == 0 and n == 0, stop=k == KT - 1 and n == 2)
    return last


def matrix(w, c, width=512, k=KT):
    return w[:, bass.ds(c, width)].rearrange("(k p) n -> p k n", p=P)


def fm_units(pe, w, rhs, ps, free, done, u, units=4, c0=0):
    for j in range(units):
        pe.wait_ge(free, u + j + 1)
        for k in range(KT):
            for half in range(2):
                last = pe.matmul(ps[:, 2 * (j % 4) + half, 0:HALF], w[:, k, c0 + j * P:c0 + (j + 1) * P],
                                 rhs[:, k, half * HALF:(half + 1) * HALF], start=k == 0, stop=k == KT - 1)
        last.then_inc(done, 1)


def fm(ps, u):
    return ps[:, 2 * (u % 4):2 * (u % 4) + 2, 0:HALF]


def halves(ap):
    return ap.rearrange("p (a n) -> p a n", a=2)


def tm_units(pe, lhs, w, ps, free, done, at, ktiles=KT, width=512, c0=0):
    for t in range(TILES):
        pe.wait_ge(free, at + t + 1)
        for k in range(ktiles):
            last = pe.matmul(ps[0:rows(t), (at + t) % 5, 0:width], lhs[:, k, cols(t)], w[:, k, c0:c0 + width],
                             start=k == 0, stop=k == ktiles - 1)
        last.then_inc(done, 1)
    return last


def constants():
    f = np.float32
    c = {}
    c["ident"] = np.eye(P, dtype=f)
    pos = np.concatenate([np.arange(SEQ), np.tile(PAST + np.arange(NT), NB)]).astype(f)
    inv = (f(500000.0) ** (-np.arange(ROPE, dtype=f) / f(ROPE))).astype(f)
    ang = (pos[:, None] * inv).astype(f)
    rope = np.zeros((TILES * P, 2, ROPE), f)
    rope[:TOK, 0], rope[:TOK, 1] = np.cos(ang), np.sin(ang)
    c["rope"] = rope.reshape(TILES, P, 2 * ROPE).transpose(1, 0, 2).copy()
    q, k = np.arange(P)[:, None], np.arange(P)[None, :]
    c["causal_add"] = np.where(k <= q, 0, NEG).astype(f)
    c["causal_keep"] = (q <= k).astype(f)
    qpos, j = np.arange(SEQ)[:, None], np.arange(PCMP)[None, :]
    c["cmp_add"] = np.where(j * STRIDE + 2 * STRIDE - 1 <= qpos, 0, NEG).astype(f).reshape(PT_, P, PCMP).transpose(1, 0, 2).copy()
    t = (np.arange(QR) // R % NT)[:, None, None]
    b, n = np.arange(NB)[None, :, None], np.arange(DEC)[None, None, :]
    c["new_add"] = np.where((n // NT == b) & (n % NT <= t), 0, NEG).astype(f)
    c["win_add"] = np.where(np.arange(WIN)[None, :] > t[:, 0], 0, NEG).astype(f)
    s, u = np.arange(DEC)[:, None], np.arange(DEC)[None, :]
    c["dec_keep"] = ((s // NT == u // NT) & (s <= u)).astype(f)
    c["dec_of"] = np.repeat(np.eye(NB, dtype=f), NT, axis=0)
    c["dec_row"] = np.tile(np.repeat(np.eye(NB, dtype=f), NT, axis=1)[None], (P, 1, 1))
    cs, ss = np.arange(NCMP)[:, None] * STRIDE, np.arange(NBLK + 1)[None, :] * BLK
    over = np.minimum(cs + 2 * STRIDE, ss + BLK) - np.maximum(cs, ss)
    c["cover"] = (np.clip(over, 0, None) / (2 * STRIDE)).astype(f)
    a = np.arange(QR)
    c["same_gt"] = (a[:, None] // R == np.arange(P)[None, :] // R).astype(f)
    forced = np.zeros((QR, NBLK + 1), f)
    forced[:, [0, NBLK - 1, NBLK]] = 1e6
    c["forced"] = forced
    sel = np.zeros((MH, MH, P), f)
    for h in range(MH):
        sel[h, h] = 1
    c["head_row"] = sel
    scan = np.zeros((MH, 2, TOK), f)
    scan[:, 0] = 1
    scan[:, 0, [0, *range(SEQ, TOK, NT)]] = 0
    scan[:, 1, [0, *range(SEQ, TOK, NT)]] = -1e38
    c["scan"] = scan
    return c


def block_modulation(nc, s, norm):
    a, ring = s.args, s.ring
    with ExitStack() as ctx:
        sb = lambda name, shape: ctx.enter_context(nc.sbuf_tensor(name, shape, F32))
        sem = lambda name: s.semaphore(name)
        c33 = sb("c33", [DEC + 1, D])
        vec = sb("vec", [NC2, 3, P])
        ada_rows = sb("modulation_rows", [DEC + 1, 2, 512])
        c_in, vec_in, silu, turned, moved, ada, rows_moved, rows_turned, ada_free = [sem(n) for n in (
            "c_in", "vec_in", "silu_done", "turned", "moved", "ada_done", "ada_rows_moved", "ada_rows_turned", "ada_free")]
        dve_step = sem("mod_dve_step")
        block = ctx.enter_context(nc.Block())
        b_ada, b_in = a["b_ada"][0], a["b_in"][0]

        @block.sync
        def _(sp):
            sp.dma_start(c33[DEC:DEC + 1, :], a["c_prompt"]).then_inc(c_in, 16)
            for t in range(NT):
                sp.dma_start(c33[t:DEC:NT, :], a["c_sample"]).then_inc(c_in, 16)
            sp.dma_start(s.ident[:], a["ident"]).then_inc(c_in, 16)
            ring.load(sp, 0, matrix(a["w_ada"][0], 0))
            norm.load(sp)
            for at, src, c0, n in ((V_SHM, b_ada, 0, 16), (V_SHF, b_ada, 3 * D, 16), (V_GM, a["g_pre_mix"][0], 0, 8),
                                   (V_GF, a["g_pre_ffn"][0], 0, 8), (V_MQ, b_in, 0, 16), (V_GA, b_in, O_GA, 16)):
                sp.dma_start(vec[at:at + n, 0, :], src[c0:c0 + n * P].rearrange("(r n) -> r n", n=P)).then_inc(vec_in, 16)
            for n, src in enumerate((a["conv_w"][0, 0], a["conv_w"][0, 1], a["conv_w"][0, 2], a["conv_b"][0])):
                sp.dma_start(vec[2 * FT * (n % 2):2 * FT * (n % 2 + 1), 1 + n // 2, :],
                             src.rearrange("(r n) -> r n", n=P)).then_inc(vec_in, 16)
            ring.load(sp, 1, matrix(a["w_ada"][0], 512))
            for c in (2, 3):
                ring.load(sp, c % 2, matrix(a["w_ada"][0], 512 * c), after=(ada, c - 1))
            ring.load(sp, 0, matrix(a["w_in"][0], 0), after=(ada, 3))
            ring.load(sp, 1, matrix(a["w_in"][0], 512), after=(ada, 4))

        @block.scalar
        def _(act):
            act.wait_ge(c_in, 16 * (NT + 2))
            act.activation(c33[:], c33[:], ACT.Silu).then_inc(silu, 1)
            norm.squares(act)
            for c in range(4):
                act.wait_ge(ada, c + 1)
                if c >= 2:
                    act.wait_ge(rows_turned, c - 1)
                act.copy(ada_rows[:, c % 2, :], s.ps[0:DEC + 1, 2 + c % 2, :]).then_inc(rows_moved, 1)

        @block.tensor
        def _(pe):
            pe.wait_ge(silu, 1)
            pe.wait_ge(c_in, 16 * (NT + 2))
            for k in range(KT):
                last = pe.transpose(s.ps[:, 0, k * (DEC + 1):(k + 1) * (DEC + 1)], c33[:, k * P:(k + 1) * P],
                                    s.ident[0:DEC + 1, 0:DEC + 1])
            last.then_inc(turned, 1)
            pe.wait_ge(vec_in, 16 * 10)
            for n, r in enumerate((NV, NC2, NC2)):
                last = pe.transpose(s.ps[:, 1, n * NC2:n * NC2 + r], vec[0:r, n, :], s.ident[0:r, 0:r])
            last.then_inc(turned, 1)
            pe.wait_ge(moved, 1)
            for c in range(4 + 1):
                if c < 4:
                    ring.await_load(pe, c % 2)
                    if c >= 2:
                        pe.wait_ge(rows_moved, c - 1)
                    for k in range(KT):
                        last = pe.matmul(s.ps[0:DEC + 1, 2 + c % 2, :], s.cT[:, k, :], ring.view(c % 2)[:, k, :],
                                         start=k == 0, stop=k == KT - 1)
                    last.then_inc(ada, 1)
                if c >= 1:
                    pe.wait_ge(rows_moved, c)
                    if c >= 3:
                        pe.wait_ge(ada_free, c - 2)
                    turn_modulation(pe, s, ada_rows[:, (c - 1) % 2, :], 4 + (c - 1) % 2).then_inc(rows_turned, 1)

        @block.vector
        def _(dve):
            link = Chain(dve, dve_step)
            dve.wait_ge(turned, 1)
            dve.tensor_copy(s.cT[:], s.ps[:, 0, 0:KT * (DEC + 1)].rearrange("p (k n) -> p k n", k=KT)).then_inc(moved, 1)
            dve.wait_ge(turned, 2)
            dve.tensor_copy(s.vecT[:, 0, 0:NV], s.ps[:, 1, 0:NV])
            link(dve.tensor_copy(s.vecT[:, 1:3, :], s.ps[:, 1, NC2:3 * NC2].rearrange("p (a n) -> p a n", a=2)))
            norm.scale_rows(dve, link)
            for c in range(4):
                dve.wait_ge(rows_turned, c + 1)
                last = dve.tensor_tensor(s.mod[:, 4 * c:4 * c + 4, :],
                                         s.ps[:, 4 + c % 2, 0:4 * (DEC + 1)].rearrange("p (j n) -> p j n", j=4),
                                         s.vecT[:, 0, V_SHM + 4 * c:V_SHM + 4 * c + 4].unsqueeze(2).to_broadcast([P, 4, DEC + 1]),
                                         ALU.add)
                last.then_inc(ada_free, 1)
            dve.wait_ge(ada_free, 4)
            link(dve.scalar_tensor_tensor(s.mod[:, 8:16, :], s.mod[:, 8:16, :], 1.0,
                                          s.vecT[:, 0, V_GM:V_GM + 8].unsqueeze(2).to_broadcast([P, 8, DEC + 1]),
                                          ALU.add, ALU.mult))


def turn_modulation(pe, s, rows_, bank):
    for j in range(4):
        last = pe.transpose(s.ps[:, bank, j * (DEC + 1):(j + 1) * (DEC + 1)], rows_[:, j * P:(j + 1) * P],
                            s.ident[0:DEC + 1, 0:DEC + 1])
    return last


class Norm:

    def __init__(self, nc, s, ctx, name, load_x):
        sb = lambda n, shape: ctx.enter_context(nc.sbuf_tensor(f"{name}_{n}", shape, F32))
        self.s, self.load_x = s, load_x
        self.xn, self.ss, self.rs = sb("xn", [P, TILES, D]), sb("ss", [P, TILES]), sb("rs", [P, TILES])
        self.x_in, self.squared, self.scaled, self.rooted, self.normed = [s.semaphore(f"{name}_{n}") for n in (
            "x_in", "squared", "scaled", "rooted", "normed")]

    def load(self, sp):
        for t in range(TILES):
            sp.dma_start(self.s.x[0:rows(t), t, :], self.load_x(t)).then_inc(self.x_in, 16)

    def squares(self, act):
        if self.load_x is not None:
            act.wait_ge(self.x_in, 16 * TILES)
        for t in range(TILES):
            last = act.activation(self.xn[0:rows(t), t, :], self.s.x[0:rows(t), t, :], ACT.Square,
                                  accum_out=self.ss[0:rows(t), t:t + 1])
        last.then_inc(self.squared, 1)
        act.wait_ge(self.scaled, 1)
        act.activation(self.rs[:, 0:PT_], self.ss[:, 0:PT_], ACT.Sqrt)
        act.activation(self.rs[0:DEC, PT_:TILES], self.ss[0:DEC, PT_:TILES], ACT.Sqrt).then_inc(self.rooted, 1)

    def scale_rows(self, dve, link):
        parts = ((P, slice(0, PT_)), (DEC, slice(PT_, TILES)))
        dve.wait_ge(self.squared, 1)
        for r, c in parts:
            last = dve.tensor_scalar(self.ss[0:r, c], self.ss[0:r, c], 1.0 / D, EPS, ALU.mult, ALU.add)
        last.then_inc(self.scaled, 1)
        dve.wait_ge(self.rooted, 1)
        for r, c in parts:
            last = dve.reciprocal(self.rs[0:r, c], self.rs[0:r, c])
        link(last)
        for t in range(TILES):
            last = dve.tensor_scalar(self.xn[0:rows(t), t, :], self.s.x[0:rows(t), t, :], self.rs[0:rows(t), t:t + 1], None, ALU.mult)
        last.then_inc(self.normed, 1)


def block_norm(nc, s, name, ht, shift, scale, norm=None):
    with ExitStack() as ctx:
        alone = norm is None
        if alone:
            norm = Norm(nc, s, ctx, name, None)
        turned, free, step = [s.semaphore(f"{name}_{n}") for n in ("turned", "free", "step")]
        block = ctx.enter_context(nc.Block())

        @block.scalar
        def _(act):
            if alone:
                norm.squares(act)

        @block.vector
        def _(dve):
            link = Chain(dve, step)
            if alone:
                norm.scale_rows(dve, link)
            for k in range(KT):
                dve.wait_ge(turned, k + 1)
                bank = 2 * (k % 4)
                dve.tensor_scalar(ht[:, k, 0:SEQ], s.ps[:, bank, :], s.mod[:, scale + k, DEC:DEC + 1],
                                  s.mod[:, shift + k, DEC:DEC + 1], ALU.mult, ALU.add)
                link(dve.tensor_tensor(ht[:, k, SEQ:TOK], s.ps[:, bank + 1, 0:DEC], s.mod[:, scale + k, 0:DEC], ALU.mult))
                dve.tensor_tensor(ht[:, k, SEQ:TOK], ht[:, k, SEQ:TOK], s.mod[:, shift + k, 0:DEC], ALU.add).then_inc(free, 1)

        @block.tensor
        def _(pe):
            if alone:
                pe.wait_ge(norm.normed, 1)
            for k in range(KT):
                if k >= 4:
                    pe.wait_ge(free, k - 3)
                for t in range(TILES):
                    out = s.ps[:, 2 * (k % 4), cols(t)] if t < PT_ else s.ps[:, 2 * (k % 4) + 1, 0:DEC]
                    last = pe.transpose(out, norm.xn[0:rows(t), t, k * P:(k + 1) * P], s.ident[0:rows(t), 0:rows(t)])
                last.then_inc(turned, 1)


def block_mlstm_in(nc, s):
    a, ring = s.args, s.ring
    w_in, b_in = a["w_in"][0], a["b_in"][0]
    with ExitStack() as ctx:
        sb = lambda name, shape: ctx.enter_context(nc.sbuf_tensor(name, shape, F32))
        sem = lambda name: s.semaphore(name)
        bias = sb("mv_mo_bias", [P, 2 * D])
        wg = sb("gate_weights", [P, KT, 2 * MH])
        small_in, fm_free, fm_done, tm_free, tm_done, step = [sem(n) for n in (
            "b1_small_in", "b1_fm_free", "b1_fm_done", "b1_tm_free", "b1_tm_done", "b1_step")]
        block = ctx.enter_context(nc.Block())

        @block.sync
        def _(sp):
            sp.dma_start(bias[:], b_in[2 * D:4 * D].partition_broadcast(P)).then_inc(small_in, 16)
            sp.dma_start(wg[:], matrix(w_in, O_MI, 2 * MH)).then_inc(small_in, 16)
            with nc.allow_non_contiguous_dma(reason="8 biases"):
                sp.dma_start(s.gate_bias[:], b_in[O_MI:O_AQ].rearrange("(g h) -> h g", g=2)).then_inc(small_in, 16)
            for c in range(2, 8):
                after = (fm_done, 4 * (c - 1)) if c < 6 else (tm_done, TILES * (c - 5))
                ring.load(sp, c % 2, matrix(w_in, 512 * c), after=after)
            for c in range(2):
                ring.load(sp, c % 2, matrix(w_in, O_AQ + 512 * c), after=(tm_done, TILES * (3 + c)))

        @block.tensor
        def _(pe):
            for c in range(4):
                ring.await_load(pe, c % 2)
                fm_units(pe, ring.view(c % 2), s.ht, s.ps, fm_free, fm_done, 4 * c)
            pe.wait_ge(small_in, 48)
            for n in range(2):
                pe.wait_ge(fm_free, 17 + n)
                for k in range(KT):
                    for half in range(2):
                        last = pe.matmul(s.ps[0:MH, 2 * n + half, 0:HALF], wg[:, k, MH * n:MH * (n + 1)],
                                         s.ht[:, k, half * HALF:(half + 1) * HALF], start=k == 0, stop=k == KT - 1)
                last.then_inc(fm_done, 1)
            pe.wait_ge(fm_free, 4 + 18)
            for c in range(4):
                ring.await_load(pe, c % 2)
                tm_units(pe, s.ht, ring.view(c % 2), s.ps, tm_free, tm_done, TILES * c)

        @block.scalar
        def _(act):
            act.sem_inc(fm_free, 4)
            for u in range(16):
                act.wait_ge(fm_done, u + 1)
                act.activation(halves(s.qk[:, u, :]), fm(s.ps, u), ACT.Identity,
                               bias=s.vecT[:, 0, V_MQ + u:V_MQ + u + 1]).then_inc(fm_free, 1)
            act.wait_ge(small_in, 48)
            for n in range(2):
                act.wait_ge(fm_done, 17 + n)
                act.activation(halves(s.gates[:, n, :]), s.ps[0:MH, 2 * n:2 * n + 2, 0:HALF], ACT.Identity,
                               bias=s.gate_bias[:, n:n + 1]).then_inc(fm_free, 1)

        @block.vector
        def _(dve):
            link = Chain(dve, step)
            dve.sem_inc(tm_free, TILES)
            dve.memset(s.va[:, :, :, MD:MD + 1], 1.0)
            dve.wait_ge(small_in, 48)
            for c in range(4):
                for t in range(TILES):
                    u = TILES * c + t
                    r = rows(t)
                    dve.wait_ge(tm_done, u + 1)
                    if c < 2:
                        out = s.va[0:r, t, 2 * c:2 * c + 2, 0:MD]
                    else:
                        out = s.og[0:r, t, 512 * (c - 2):512 * (c - 1)].rearrange("p (a n) -> p a n", a=2)
                    dve.tensor_tensor(out, s.ps[0:r, t, :].rearrange("p (a n) -> p a n", a=2),
                                      bias[0:r, 512 * c:512 * (c + 1)].rearrange("p (a n) -> p a n", a=2),
                                      ALU.add).then_inc(tm_free, 1)


def block_mlstm_gates(nc, s):
    a = s.args
    with ExitStack() as ctx:
        sb = lambda name, shape: ctx.enter_context(nc.sbuf_tensor(name, shape, F32))
        sem = lambda name: s.semaphore(name)
        scan = sb("scan_masks", [MH, 2, TOK])
        m0 = sb("m0", [MH, NB])
        t1, t2, b, u, um, m, mt, w, ainter = [sb(n, [MH, TOK]) for n in (
            "gate_t1", "gate_t2", "gate_b", "gate_u", "gate_um", "gate_m", "gate_mt", "gate_w", "gate_a")]
        mneg = sb("gate_mneg", [MH, TOK])
        small_in, aq, dq, pq, st = [sem(n) for n in ("g_small_in", "g_act", "g_dve", "g_pe", "g_store")]
        block = ctx.enter_context(nc.Block())

        def dec(ap):
            return ap[:, SEQ:TOK].rearrange("p (b t) -> p b t", t=NT)

        @block.sync
        def _(sp):
            sp.dma_start(scan[:], a["scan"]).then_inc(small_in, 16)
            sp.dma_start(s.head_row[:], a["head_row"]).then_inc(small_in, 16)
            sp.dma_start(s.norm_w[:], a["m_norm_w"][0].partition_broadcast(P)).then_inc(small_in, 16)
            with nc.allow_non_contiguous_dma(reason="one value a head and sequence"):
                sp.dma_start(m0[:], a["state_m"][0].rearrange("b h -> h b")).then_inc(small_in, 16)
                sp.wait_ge(dq, 8)
                sp.dma_start(a["p_m"][0, 0].rearrange("(h o) -> h o", o=1), mt[:, SEQ - 1:SEQ]).then_inc(st, 16)
                sp.dma_start(a["s_m"][0].rearrange("b h -> h b"), dec(mt)[:, :, NT - 1]).then_inc(st, 16)
            sp.wait_ge(st, 32)

        @block.scalar
        def _(act):
            link = Chain(act, aq)
            f = s.gates[:, 1, :]
            link(act.activation(t1[:], f, ACT.Abs))
            link(act.activation(t1[:], t1[:], ACT.Exp, scale=-1.0))
            link(act.activation(t1[:], t1[:], ACT.Ln, bias=1.0))
            act.wait_ge(dq, 9)
            link(act.activation(w[:], w[:], ACT.Exp))
            link(act.activation(t2[:], mt[:], ACT.Exp, scale=-1.0))
            link(act.activation(ainter[:, SEQ:TOK], ainter[:, SEQ:TOK], ACT.Exp))
            for t in range(TILES):
                r = rows(t)
                last = act.activation(s.og[0:r, t, :], s.og[0:r, t, :], ACT.Sigmoid)
            link(last)

        @block.vector
        def _(dve):
            link = Chain(dve, dq)
            dve.wait_ge(small_in, 64)
            link(dve.tensor_scalar(t2[:], s.gates[:, 1, :], 0.0, None, ALU.min))
            dve.wait_ge(aq, 3)
            link(dve.tensor_tensor(t2[:], t2[:], t1[:], ALU.subtract))
            link(dve.tensor_tensor_scan(b[:], scan[:, 0, :], t2[:], 0.0, ALU.mult, ALU.add))
            link(dve.tensor_tensor(u[:], s.gates[:, 0, :], b[:], ALU.subtract))
            link(dve.tensor_copy(um[:], u[:]))
            dve.tensor_scalar(um[:, 0:1], u[:, 0:1], 0.0, None, ALU.max)
            link(dve.tensor_tensor(dec(um)[:, :, 0], dec(u)[:, :, 0], m0[:], ALU.max))
            link(dve.tensor_tensor_scan(m[:], scan[:, 1, :], um[:], -1e38, ALU.add, ALU.max))
            link(dve.tensor_tensor(mt[:], b[:], m[:], ALU.add))
            dve.tensor_scalar(mneg[:], m[:], -1.0, None, ALU.mult)
            dve.tensor_scalar(w[:, 0:SEQ], u[:, 0:SEQ], m[:, SEQ - 1:SEQ], None, ALU.subtract)
            dve.tensor_tensor(dec(w), dec(u), dec(m)[:, :, NT - 1:NT].to_broadcast([MH, NB, NT]), ALU.subtract)
            link(dve.tensor_tensor(dec(ainter), m0[:].unsqueeze(2).to_broadcast([MH, NB, NT]), dec(m), ALU.subtract))
            dve.wait_ge(aq, 6)
            link(dve.tensor_copy(s.alast[:], dec(ainter)[:, :, NT - 1]))
            dve.wait_ge(pq, 1)
            c = s.ps[:, 0, 0:TILES * 16].rearrange("p (t n) -> p t n", t=TILES)
            dve.tensor_copy(s.gcol[:, 0:PT_, :, :], c[:, 0:PT_, 0:12].rearrange("p t (q h) -> p t q h", q=3))
            dve.tensor_copy(s.gcol[0:DEC, PT_, :, :], c[0:DEC, PT_, 0:12].rearrange("p (q h) -> p q h", q=3))
            dve.tensor_copy(s.acol[:], c[0:DEC, PT_, 12:16])
            for h in range(MH):
                dve.wait_ge(pq, 2 + h)
                last = dve.tensor_copy(halves(s.mneg[:, h, :]), s.ps[:, 1 + 2 * (h % 2):3 + 2 * (h % 2), 0:HALF])
                link(last)
            dve.wait_ge(pq, 6)
            dve.tensor_copy(s.decay[:], s.ps[:, 5, 0:MH * NB].rearrange("p (h b) -> p h b", h=MH))
            dve.wait_ge(aq, 7)
            for t in range(TILES):
                r = rows(t)
                last = dve.tensor_tensor(s.og[0:r, t, :], s.og[0:r, t, :], s.norm_w[0:r, :], ALU.mult)
            link(last)

        @block.tensor
        def _(pe):
            pe.wait_ge(aq, 6)
            pe.wait_ge(dq, 9)
            i4 = s.ident[0:MH, 0:MH]
            for t in range(TILES):
                for q, src in enumerate((u, t2, w, ainter)):
                    if q == 3 and t < PT_:
                        continue
                    last = pe.transpose(s.ps[0:rows(t), 0, 16 * t + 4 * q:16 * t + 4 * q + 4], src[:, cols(t)], i4)
            last.then_inc(pq, 1)
            for h in range(MH):
                if h >= 2:
                    pe.wait_ge(dq, 9 + h)
                for half in range(2):
                    last = pe.matmul(s.ps[:, 1 + 2 * (h % 2) + half, 0:HALF], s.head_row[:, h, :],
                                     mneg[:, half * HALF:(half + 1) * HALF], start=True, stop=True)
                last.then_inc(pq, 1)
            pe.wait_ge(dq, 10)
            for h in range(MH):
                last = pe.matmul(s.ps[:, 5, NB * h:NB * (h + 1)], s.head_row[:, h, :], s.alast[:], start=True, stop=True)
            last.then_inc(pq, 1)


def head_out(s, h, i):
    return s.qk[:, 2 * h + i // 2, MD * (i % 2):MD * (i % 2 + 1)] if i < PT_ else s.hdec[:, h, :]


def block_mlstm_prompt(nc, s):
    a = s.args
    with ExitStack() as ctx:
        sb = lambda name, shape: ctx.enter_context(nc.sbuf_tensor(name, shape, F32))
        sem = lambda name: s.semaphore(name)
        keep = sb("causal_keep", [P, P])
        pt = sb("pt", [P, PT_, SEQ])
        dw = sb("dw", [P, 2, SEQ])
        ktm = sb("k_tm", [P, PT_, MD])
        vw = sb("v_weighted", [P, PT_, MD])
        cout = sb("c_out", [P, 2, MD])
        nout = sb("n_out", [1, MD])
        den = sb("den", [P, 2])
        in_, pe_s, pe_k, pe_o, pe_c, dstep, exps, dwr, astep, ptdone, ktmdone, ofree, cst, cready = [sem(n) for n in (
            "p_in", "p_s_ready", "p_k_turned", "p_o_ready", "p_c_ready", "p_dve_step", "p_exp_done", "p_dw_ready",
            "p_act_step", "p_pt_ready", "p_ktm_ready", "p_o_free", "p_c_stored", "p_c_copied")]
        block = ctx.enter_context(nc.Block())
        JOBS = [(h, j) for h in range(MH) for j in range(PT_)]

        @block.sync
        def _(sp):
            sp.dma_start(keep[:], a["causal_keep"]).then_inc(in_, 16)
            for h in range(MH):
                sp.wait_ge(cready, h + 1)
                sp.dma_start(a["p_C"][0, 0, h].rearrange("(a p) k -> p a k", p=P), cout[:]).then_inc(cst, 16)
                sp.dma_start(a["p_n"][0, 0, h:h + 1, :], nout[:]).then_inc(cst, 16)
            sp.wait_ge(cst, 32 * MH)

        @block.tensor
        def _(pe):
            for h in range(MH):
                if h:
                    pe.wait_ge(ktmdone, h)
                for t in range(PT_):
                    for d in range(2):
                        last = pe.transpose(s.ps[:, 4 + t // 2, 256 * (t % 2) + P * d:256 * (t % 2) + P * (d + 1)],
                                            s.qk[:, 8 + 2 * h + d, cols(t)], s.ident[:])
                last.then_inc(pe_k, 1)
                for j in range(PT_):
                    n = h * PT_ + j
                    if n >= 2:
                        pe.wait_ge(ptdone, n - 1)
                    for d in range(2):
                        last = pe.matmul(s.ps[:, n % 2, P * j:SEQ], s.qk[:, 8 + 2 * h + d, cols(j)],
                                         s.qk[:, 2 * h + d, P * j:SEQ], start=d == 0, stop=d == 1)
                    last.then_inc(pe_s, 1)
                for i in range(PT_):
                    n = h * PT_ + i
                    pe.wait_ge(ptdone, h * PT_ + i + 1)
                    if n >= 2:
                        pe.wait_ge(ofree, n - 1)
                    for j in range(i + 1):
                        last = pe.matmul(s.ps[:, 2 + n % 2, 0:MD + 1], pt[:, j, cols(i)], s.va[:, j, h, :],
                                         start=j == 0, stop=j == i)
                    last.then_inc(pe_o, 1)
                pe.wait_ge(ktmdone, h + 1)
                if h:
                    pe.wait_ge(cready, h)
                for v in range(2):
                    for j in range(PT_):
                        last = pe.matmul(s.ps[:, 6, MD * v:MD * (v + 1)], vw[:, j, P * v:P * (v + 1)], ktm[:, j, :],
                                         start=j == 0, stop=j == PT_ - 1)
                for j in range(PT_):
                    last = pe.matmul(s.ps[0:1, 7, 0:MD], s.gcol[:, j, 2, h:h + 1], ktm[:, j, :],
                                     start=j == 0, stop=j == PT_ - 1)
                last.then_inc(pe_c, 1)

        @block.scalar
        def _(act):
            for h in range(MH):
                for j in range(PT_):
                    n = h * PT_ + j
                    act.wait_ge(dwr, n + 1)
                    act.activation(dw[:, n % 2, P * j:SEQ], dw[:, n % 2, P * j:SEQ], ACT.Exp).then_inc(exps, 1)

        @block.vector
        def _(dve):
            link = Chain(dve, dstep)

            def exponent(n):
                h, j = JOBS[n]
                if n >= 2:
                    dve.wait_ge(ptdone, n - 1)
                dve.tensor_scalar(dw[:, n % 2, P * j:SEQ], s.mneg[:, h, P * j:SEQ], s.gcol[:, j, 0, h:h + 1], 0.0,
                                  ALU.add, ALU.min).then_inc(dwr, 1)

            dve.wait_ge(in_, 16)
            exponent(0)
            for h in range(MH):
                for j in range(PT_):
                    n = h * PT_ + j
                    if n + 1 < len(JOBS):
                        exponent(n + 1)
                    dve.wait_ge(exps, n + 1)
                    link(dve.tensor_tensor(dw[:, n % 2, cols(j)], dw[:, n % 2, cols(j)], keep[:], ALU.mult))
                    dve.wait_ge(pe_s, n + 1)
                    if h:
                        dve.wait_ge(pe_o, h * PT_)
                    dve.scalar_tensor_tensor(pt[:, j, P * j:SEQ], s.ps[:, n % 2, P * j:SEQ], MD ** -0.5,
                                             dw[:, n % 2, P * j:SEQ], ALU.mult, ALU.mult).then_inc(ptdone, 1)
                dve.wait_ge(pe_k, h + 1)
                if h:
                    dve.wait_ge(pe_c, h)
                dve.tensor_scalar(ktm[:], s.ps[:, 4:6, :].rearrange("p a (b n) -> p (a b) n", b=2), MD ** -0.5, None, ALU.mult)
                for j in range(PT_):
                    last = dve.tensor_scalar(vw[:, j, :], s.va[:, j, h, 0:MD], s.gcol[:, j, 2, h:h + 1], None, ALU.mult)
                last.then_inc(ktmdone, 1)
                for i in range(PT_):
                    n = h * PT_ + i
                    o = s.ps[:, 2 + n % 2, :]
                    dve.wait_ge(pe_o, n + 1)
                    link(dve.scalar_tensor_tensor(den[:, 0:1], o[:, MD:MD + 1], -1.0, s.gcol[:, i, 1, h:h + 1],
                                                  ALU.mult, ALU.max))
                    link(dve.tensor_tensor(den[:, 0:1], o[:, MD:MD + 1], den[:, 0:1], ALU.max))
                    link(dve.reciprocal(den[:, 1:2], den[:, 0:1]))
                    dve.tensor_scalar(head_out(s, h, i), o[:, 0:MD], den[:, 1:2], None, ALU.mult).then_inc(ofree, 1)
                dve.wait_ge(pe_c, h + 1)
                if h:
                    dve.wait_ge(cst, 32 * h)
                dve.tensor_copy(cout[:], s.ps[:, 6, :].rearrange("p (a n) -> p a n", a=2))
                dve.tensor_copy(nout[:], s.ps[0:1, 7, 0:MD]).then_inc(cready, 1)


def block_mlstm_decode(nc, s):
    a = s.args
    with ExitStack() as ctx:
        sb = lambda name, shape: ctx.enter_context(nc.sbuf_tensor(name, shape, F32))
        sem = lambda name: s.semaphore(name)
        keep = sb("dec_keep", [DEC, DEC])
        dec_of = sb("dec_of", [DEC, NB])
        dec_row = sb("dec_row", [P, NB, DEC])
        nrow = sb("n_rows", [NB * MH, MD])
        nT = sb("n_turned", [P, 2, NB, MH])
        nnew = sb("n_new", [P, 2, NB, MH])
        nout = sb("n_out_rows", [NB * MH, MD])
        qb = sb("q_of_sequence", [P, 2, MH, 2, DEC])
        vb = sb("v_of_sequence", [DEC, MH, MD])
        wsel = sb("w_of_sequence", [DEC, MH, NB])
        zero = sb("zero", [P, DEC])
        pt = sb("pt_dec", [DEC, MH, DEC])
        dw = sb("dw_dec", [DEC, MH, DEC])
        cT = sb("c_turned", [P, 2, 2, MD + 1])
        cout = sb("c_new", [P, 2, MH, 2, MD])
        num = sb("num_dec", [DEC, MH, MD + 1])
        den = sb("den_dec", [DEC, MH])
        ktm = s.carry[0:DEC, 2 * 2048:2 * 2048 + D].rearrange("p (h k) -> p h k", h=MH)
        cin = [s.hmt[:].rearrange("p k n -> p (k n)")[:, 2048 * i:2048 * (i + 1)].rearrange("p (h v k) -> p h v k", h=MH, v=2)
               for i in range(2)]
        small, cin0, cin1, pe_step, dve_step, exped, turned, moved, picked, state, cnew, inter, st0, st1, nst, local, ncol = [
            sem(n) for n in ("d_small", "d_c_in0", "d_c_in1", "d_pe_step", "d_dve_step", "d_exp", "d_turned", "d_moved",
                             "d_picked", "d_state", "d_c_new", "d_inter", "d_stored0", "d_stored1", "d_n_stored",
                             "d_local", "d_n_col")]
        cload, cstore = [cin0, cin1], [st0, st1]
        block = ctx.enter_context(nc.Block())
        MOVED, INTER, CNEW = 2, 6, 2

        def states(t, b):
            return t[0, b].rearrange("h (v p) k -> p h v k", p=P)

        def states_at(t, b):
            return t[0, bass.ds(b, 1)].rearrange("o h (v p) k -> p (o h) v k", p=P)

        @block.sync
        def _(sp):
            for src, dst in (("dec_keep", keep), ("dec_of", dec_of), ("dec_row", dec_row)):
                sp.dma_start(dst[:], a[src]).then_inc(small, 16)
            sp.dma_start(nrow[:], a["state_n"][0].rearrange("b h k -> (b h) k")).then_inc(small, 16)
            for p in range(2):
                sp.dma_start(cin[p], states(a["state_C"], p)).then_inc(cload[p], 16)
            for p in range(2):
                sp.sem_inc(cstore[p], 16)
            with sp.Fori(0, NB // 2 - 1) as i:
                for p in range(2):
                    sp.wait_ge(cnew, i * 8 + (CNEW + 4 * (p + 1)))
                    sp.dma_start(cin[p], states_at(a["state_C"], i * 2 + (2 + p))).then_inc(cload[p], 16)
                    sp.dma_start(states_at(a["s_C"], i * 2 + p), cout[:, p]).then_inc(cstore[p], 16)
            for p in range(2):
                sp.wait_ge(cnew, 4 * (NB - 2) + CNEW + 4 * (p + 1))
                sp.dma_start(states(a["s_C"], NB - 2 + p), cout[:, p]).then_inc(cstore[p], 16)
            sp.wait_ge(ncol, 2)
            sp.dma_start(a["s_n"][0].rearrange("b h k -> (b h) k"), nout[:]).then_inc(nst, 16)
            sp.wait_ge(nst, 16)
            for p in range(2):
                sp.wait_ge(cstore[p], 16 * (NB // 2 + 1))

        @block.tensor
        def _(pe):
            pe.wait_ge(small, 64)
            for k in range(2):
                pe.transpose(s.ps[:, 0, 32 * k:32 * k + 32], nrow[:, P * k:P * (k + 1)], s.ident[0:32, 0:32])
            for h in range(MH):
                for d in range(2):
                    last = pe.matmul(s.ps[0:DEC, 1, DEC * h:DEC * (h + 1)], s.qk[:, 8 + 2 * h + d, SEQ:TOK],
                                     s.qk[:, 2 * h + d, SEQ:TOK], start=d == 0, stop=d == 1)
            for h in range(MH):
                for d in range(2):
                    last = pe.transpose(s.ps[0:DEC, 2 + h // 2, MD * (h % 2) + P * d:MD * (h % 2) + P * (d + 1)],
                                        s.qk[:, 8 + 2 * h + d, SEQ:TOK], s.ident[:])
            last.then_inc(pe_step, 1)
            pe.wait_ge(dve_step, 3)
            for h in range(MH):
                for d in range(2):
                    last = pe.matmul(s.ps[:, 4, 8 * (2 * h + d):8 * (2 * h + d + 1)], ktm[:, h, P * d:P * (d + 1)],
                                     wsel[:, h, :], start=True, stop=True)
            last.then_inc(pe_step, 1)
            pe.wait_ge(ncol, 1)
            for d in range(2):
                last = pe.transpose(s.ps[0:NB * MH, 5, P * d:P * (d + 1)], nnew[:, d].rearrange("p b h -> p (b h)"), s.ident[:])
            last.then_inc(pe_step, 1)
            pe.wait_ge(ncol, 2)
            for h in range(MH):
                pe.matmul(s.ps[0:DEC, h, 0:MD + 1], zero[:], s.va[:, 0, 0, :], start=True, stop=False, skip_group_check=True)
            pe.sem_inc(inter, INTER)
            with pe.Fori(0, NB // 2) as i:
                for m in range(8):
                    p, h = m // 4, m % 4
                    if h == 0:
                        pe.wait_ge(cload[p], i * 16 + 16)
                    pe.wait_ge(moved, i * 8 + (m - 2 + 1 + MOVED))
                    for k in range(2):
                        for v in range(2):
                            last = pe.transpose(s.ps[:, 4 + m % 2, MD * k + P * v:MD * k + P * (v + 1)],
                                                cin[p][:, h, v, P * k:P * (k + 1)], s.ident[:])
                    last.then_inc(turned, 1)
                    if h == 0:
                        pe.wait_ge(picked, i * 2 + (p + 1))
                    pe.wait_ge(cnew, i * 8 + (m - 2 + 1 + CNEW))
                    for v in range(2):
                        last = pe.matmul(s.ps[:, 6 + m % 2, MD * v:MD * (v + 1)], vb[:, h, P * v:P * (v + 1)], ktm[:, h, :],
                                         start=True, stop=True)
                    last.then_inc(state, 1)
                    pe.wait_ge(moved, i * 8 + (m + 1 + MOVED))
                    for k in range(2):
                        last = pe.matmul(s.ps[0:DEC, h, 0:MD + 1], qb[:, p, h, k, :], cT[:, m % 2, k, :], start=False,
                                         stop=False, skip_group_check=True)
                    last.then_inc(inter, 1)
            pe.wait_ge(cnew, 4 * NB + CNEW)
            for h in range(MH):
                last = pe.matmul(s.ps[0:DEC, 4 + h, 0:MD + 1], pt[:, h, :], s.va[0:DEC, PT_, h, :], start=True, stop=True)
            last.then_inc(local, 1)

        @block.scalar
        def _(act):
            act.wait_ge(dve_step, 1)
            act.activation(dw[:], dw[:], ACT.Exp).then_inc(exped, 1)
            act.sem_inc(moved, MOVED)
            act.wait_ge(ncol, 2)
            with act.Fori(0, NB // 2) as i:
                for m in range(8):
                    p, h = m // 4, m % 4
                    act.wait_ge(turned, i * 8 + (m + 1))
                    act.wait_ge(inter, i * 8 + (m - 2 + 1 + INTER))
                    act.copy(cT[:, m % 2, :, MD], nT[:, :, bass.ds(i * 2 + p, 1), h].rearrange("p k o -> p (k o)"))
                    act.copy(cT[:, m % 2, :, 0:MD],
                             s.ps[:, 4 + m % 2, :].rearrange("p (k n) -> p k n", k=2)).then_inc(moved, 1)

        @block.vector
        def _(dve):
            link = Chain(dve, dve_step)
            dve.sem_inc(cnew, CNEW)
            dve.memset(zero[:], 0.0)
            for h in range(MH):
                last = dve.tensor_scalar(dw[:, h, :], s.mneg[0:DEC, h, SEQ:TOK], s.gcol[0:DEC, PT_, 0, h:h + 1], 0.0,
                                         ALU.add, ALU.min)
            link(last)
            dve.wait_ge(small, 64)
            for h in range(MH):
                last = dve.tensor_scalar(wsel[:, h, :], dec_of[:], s.gcol[0:DEC, PT_, 2, h:h + 1], None, ALU.mult)
            link(last)
            dve.wait_ge(pe_step, 1)
            dve.tensor_copy(nT[:], s.ps[:, 0, 0:64].rearrange("p (k b h) -> p k b h", k=2, b=NB))
            link(dve.tensor_scalar(ktm[:], s.ps[0:DEC, 2:4, :].rearrange("p a (b n) -> p (a b) n", b=2), MD ** -0.5, None,
                                   ALU.mult))
            dve.wait_ge(exped, 1)
            for h in range(MH):
                last = dve.tensor_tensor(dw[:, h, :], dw[:, h, :], keep[:], ALU.mult)
            link(last)
            link(dve.scalar_tensor_tensor(pt[:], s.ps[0:DEC, 1, 0:MH * DEC].rearrange("p (h n) -> p h n", h=MH), MD ** -0.5,
                                          dw[:], ALU.mult, ALU.mult))
            decay = s.decay[:].rearrange("p h b -> p b h")
            for k in range(2):
                last = dve.tensor_tensor(nnew[:, k], nT[:, k], decay, ALU.mult)
            link(last)
            dve.wait_ge(pe_step, 2)
            sums = s.ps[:, 4, 0:64].rearrange("p (h k b) -> p k b h", h=MH, k=2)
            for k in range(2):
                last = dve.tensor_tensor(nnew[:, k], nnew[:, k], sums[:, k], ALU.add)
            last.then_inc(ncol, 1)
            dve.wait_ge(pe_step, 3)
            dve.tensor_copy(nout[:], s.ps[0:NB * MH, 5, 0:MD]).then_inc(ncol, 1)
            with dve.Fori(0, NB // 2) as i:
                for p in range(2):
                    dve.wait_ge(inter, i * 8 + (4 * p + INTER))
                    for h in range(MH):
                        dve.tensor_scalar(vb[:, h, :], s.va[0:DEC, PT_, h, 0:MD],
                                          wsel[:, h, bass.ds(i * 2 + p, 1)], None, ALU.mult)
                        last = dve.tensor_tensor(qb[:, p, h], s.qk[:, 2 * h:2 * h + 2, SEQ:TOK],
                                                 dec_row[:, bass.ds(i * 2 + p, 1), :].to_broadcast([P, 2, DEC]), ALU.mult)
                    last.then_inc(picked, 1)
                    dve.wait_ge(cload[p], i * 16 + 16)
                    dve.wait_ge(cstore[p], i * 16 + 16)
                    for h in range(MH):
                        m = 4 * p + h
                        dve.wait_ge(state, i * 8 + (m + 1))
                        dve.scalar_tensor_tensor(cout[:, p, h], cin[p][:, h], s.decay[:, h, bass.ds(i * 2 + p, 1)],
                                                 s.ps[:, 6 + m % 2, :].rearrange("p (v n) -> p v n", v=2),
                                                 ALU.mult, ALU.add).then_inc(cnew, 1)
            dve.wait_ge(inter, 4 * NB + INTER)
            for h in range(MH):
                last = dve.tensor_scalar(num[:, h, :], s.ps[0:DEC, h, 0:MD + 1], s.acol[:, h:h + 1], None, ALU.mult)
            link(last)
            dve.wait_ge(local, 1)
            link(dve.tensor_tensor(num[:], num[:], s.ps[0:DEC, 4:8, 0:MD + 1], ALU.add))
            link(dve.scalar_tensor_tensor(den[:], num[:, :, MD], -1.0, s.gcol[0:DEC, PT_, 1, :], ALU.mult, ALU.max))
            link(dve.tensor_tensor(den[:], num[:, :, MD], den[:], ALU.max))
            link(dve.reciprocal(den[:], den[:]))
            for h in range(MH):
                last = dve.tensor_scalar(s.hdec[:, h, :], num[:, h, 0:MD], den[:, h:h + 1], None, ALU.mult)
            link(last)


def block_mlstm_out(nc, s):
    with ExitStack() as ctx:
        sb = lambda name, shape: ctx.enter_context(nc.sbuf_tensor(name, shape, F32))
        sem = lambda name: s.semaphore(name)
        st6 = sb("stats6", [P, TILES, MH, 6])
        mv = sb("mean_var", [P, TILES, MH, 2])
        sd = sb("deviation", [P, TILES, MH])
        step, rooted, ready, turned, freed = [sem(n) for n in ("o_step", "o_rooted", "o_ready", "o_turned", "o_freed")]
        block = ctx.enter_context(nc.Block())

        @block.vector
        def _(dve):
            link = Chain(dve, step)
            for t in range(TILES):
                for h in range(MH):
                    last = dve.bn_stats(st6[0:rows(t), t, h, :], head_out(s, h, t))
            link(last)
            for t in range(TILES):
                for h in range(MH):
                    last = dve.bn_aggr(mv[0:rows(t), t, h, :], st6[0:rows(t), t, h, :])
            link(last)
            for r, c in ((P, slice(0, PT_)), (DEC, slice(PT_, TILES))):
                last = dve.tensor_scalar(sd[0:r, c], mv[0:r, c, :, 1], EPS, None, ALU.add)
            link(last)
            dve.wait_ge(rooted, 1)
            for r, c in ((P, slice(0, PT_)), (DEC, slice(PT_, TILES))):
                last = dve.reciprocal(sd[0:r, c], sd[0:r, c])
            link(last)
            for t in range(TILES):
                for h in range(MH):
                    last = dve.tensor_scalar(head_out(s, h, t), head_out(s, h, t), mv[0:rows(t), t, h, 0:1],
                                             sd[0:rows(t), t, h:h + 1], ALU.subtract, ALU.mult)
            link(last)
            for t in range(TILES):
                for h in range(MH):
                    og = s.og[0:rows(t), t, MD * h:MD * (h + 1)]
                    last = dve.tensor_tensor(og, og, head_out(s, h, t), ALU.mult)
            last.then_inc(ready, 1)

        @block.scalar
        def _(act):
            act.wait_ge(step, 3)
            act.activation(sd[:, 0:PT_], sd[:, 0:PT_], ACT.Sqrt)
            act.activation(sd[0:DEC, PT_], sd[0:DEC, PT_], ACT.Sqrt).then_inc(rooted, 1)
            for k in range(KT):
                act.wait_ge(turned, k + 1)
                act.copy(s.hmt[:, k, 0:SEQ], s.ps[:, 2 * (k % 4), :])
                act.copy(s.hmt[:, k, SEQ:TOK], s.ps[:, 2 * (k % 4) + 1, 0:DEC]).then_inc(freed, 1)

        @block.tensor
        def _(pe):
            pe.wait_ge(ready, 1)
            turn_tiles(pe, s, s.og, turned, freed)


def turn_tiles(pe, s, tm, turned, freed):
    for k in range(KT):
        if k >= 4:
            pe.wait_ge(freed, k - 3)
        for t in range(TILES):
            out = s.ps[:, 2 * (k % 4), cols(t)] if t < PT_ else s.ps[:, 2 * (k % 4) + 1, 0:DEC]
            last = pe.transpose(out, tm[0:rows(t), t, k * P:(k + 1) * P], s.ident[0:rows(t), 0:rows(t)])
        last.then_inc(turned, 1)


def block_attention_in(nc, s):
    a, ring = s.args, s.ring
    w_in, b_in = a["w_in"][0], a["b_in"][0]
    WIDE = D + 6 * G * AD
    with ExitStack() as ctx:
        sb = lambda name, shape: ctx.enter_context(nc.sbuf_tensor(name, shape, F32))
        sem = lambda name: s.semaphore(name)
        bias = sb("attention_bias", [P, WIDE + 48])
        wg = sb("branch_gate_weights", [P, KT, 48])
        rope = sb("rope_table", [P, TILES, 2 * ROPE])
        tmp = s.hat[:].rearrange("p k n -> p (k n)")[:, 0:4 * PT_ * AH * ROPE].rearrange("p (k t h d) -> p k t h d", k=4, t=PT_, h=AH)
        small_in, tm_free, tm_done, step, gate_sum, gated, kv_ready, stored, win_copied, gate_out = [sem(n) for n in (
            "c1_small_in", "c1_tm_free", "c1_tm_done", "c1_step", "c1_gate_sum", "c1_gated", "c1_kv_ready", "c1_stored",
            "c1_win_copied", "c1_gate_stored")]
        block = ctx.enter_context(nc.Block())
        names = ("cmp", "slc", "win")

        @block.sync
        def _(sp):
            sp.dma_start(bias[:], b_in[O_AQ:O_GA].partition_broadcast(P)).then_inc(small_in, 16)
            sp.dma_start(wg[:], matrix(w_in, O_AG, 48)).then_inc(small_in, 16)
            sp.dma_start(rope[:], a["rope"]).then_inc(small_in, 16)
            sp.dma_start(a["s_win"][0, :, 0:WIN - NT].rearrange("b w x g d -> b w (x g d)"),
                         a["cache_win_kv"][0, :, NT:WIN].rearrange("b w x g d -> b w (x g d)")).then_inc(win_copied, 16)
            for c in range(2, 5):
                ring.load(sp, c % 2, matrix(w_in, O_AQ + 512 * c), after=(tm_done, TILES * (c - 1)))
            for n, name in enumerate(names):
                sp.wait_ge(kv_ready, n + 1)
                out = a["p_" + name][0, 0].rearrange("(t p) x g d -> p t (x g d)", p=P)
                sp.dma_start(out, s.kv[:, 0:PT_, 512 * n:512 * (n + 1)]).then_inc(stored, 16)
                out = a["s_" + name][0]
                if name == "win":
                    out = out[:, WIN - NT:WIN]
                    for b in range(NB):
                        sp.dma_start(out[b].rearrange("t x g d -> t (x g d)"),
                                     s.kv_dec[NT * b:NT * (b + 1), 512 * n:512 * (n + 1)]).then_inc(stored, 16)
                else:
                    sp.dma_start(out.rearrange("b t x g d -> (b t) (x g d)"),
                                 s.kv_dec[:, 512 * n:512 * (n + 1)]).then_inc(stored, 16)
            sp.wait_ge(gated, 1)
            sp.dma_start(s.gate_scratch, s.branch_gates[0:DEC, PT_, :]).then_inc(gate_out, 16)
            sp.wait_ge(gate_out, 16)
            sp.wait_ge(stored, 16 * (5 + NB))
            sp.wait_ge(win_copied, 16)

        @block.tensor
        def _(pe):
            pe.wait_ge(small_in, 48)
            for c in range(5):
                ring.await_load(pe, c % 2)
                tm_units(pe, s.ht, ring.view(c % 2), s.ps, tm_free, tm_done, TILES * c)
            tm_units(pe, s.ht, wg, s.ps, tm_free, tm_done, TILES * 5, width=48)

        @block.scalar
        def _(act):
            act.wait_ge(gate_sum, 1)
            act.activation(s.branch_gates[:, 0:PT_, :], s.branch_gates[:, 0:PT_, :], ACT.Sigmoid)
            act.activation(s.branch_gates[0:DEC, PT_, :], s.branch_gates[0:DEC, PT_, :], ACT.Sigmoid).then_inc(gated, 1)

        @block.vector
        def _(dve):
            link = Chain(dve, step)
            dve.sem_inc(tm_free, TILES)
            dve.wait_ge(small_in, 48)

            def evacuate(c, t):
                r = rows(t)
                dve.wait_ge(tm_done, TILES * c + t + 1)
                width = 512
                if c < 2:
                    split = lambda ap: ap.rearrange("p (g h d) -> p g h d", g=2, h=R)
                    out = s.q_tm[0:r, t, 512 * c:512 * (c + 1)].rearrange("p (h g d) -> p g h d", g=2, h=R)
                    return dve.tensor_tensor(out, split(s.ps[0:r, t, :]), split(bias[0:r, 512 * c:512 * (c + 1)]), ALU.add)
                elif c < 5:
                    out = s.kv[0:r, t, 512 * (c - 2):512 * (c - 1)] if t < PT_ else s.kv_dec[:, 512 * (c - 2):512 * (c - 1)]
                else:
                    out, width = s.branch_gates[0:r, t, :], 48
                return dve.tensor_tensor(out, s.ps[0:r, t, 0:width], bias[0:r, 512 * c:512 * c + width], ALU.add)

            def rotate(x1, x2, r, tiles, heads):
                n = (r, len(tiles), heads, ROPE)
                table = lambda k: rope[0:r, tiles[0]:tiles[-1] + 1, ROPE * k:ROPE * (k + 1)].unsqueeze(2).to_broadcast(n)
                w = [tmp[0:r, k, 0:len(tiles), 0:heads, :] for k in range(4)]
                dve.tensor_tensor(w[0], x1, table(0), ALU.mult)
                dve.tensor_tensor(w[1], x2, table(1), ALU.mult)
                dve.tensor_tensor(w[2], x2, table(0), ALU.mult)
                link(dve.tensor_tensor(w[3], x1, table(1), ALU.mult))
                dve.tensor_tensor(x1, w[0], w[1], ALU.subtract)
                return dve.tensor_tensor(x2, w[2], w[3], ALU.add)

            for c in range(6):
                for t in range(TILES):
                    evacuate(c, t).then_inc(tm_free, 1)
                dve.wait_ge(tm_free, TILES * (c + 2))
                if c == 1:
                    q = s.q_tm[:].rearrange("p t (h d) -> p t h d", d=AD)
                    link(rotate(q[:, 0:PT_, :, 0:ROPE], q[:, 0:PT_, :, ROPE:2 * ROPE], P, range(PT_), AH))
                    link(rotate(q[0:DEC, PT_:TILES, :, 0:ROPE], q[0:DEC, PT_:TILES, :, ROPE:2 * ROPE], DEC, [PT_], AH))
                elif 2 <= c < 5:
                    at = 512 * (c - 2)
                    k = s.kv[:, :, at:at + G * AD].rearrange("p t (g d) -> p t g d", d=AD)
                    link(rotate(k[:, :, :, 0:ROPE], k[:, :, :, ROPE:2 * ROPE], P, range(PT_), G))
                    k = s.kv_dec[:, at:at + G * AD].rearrange("p (o g d) -> p o g d", o=1, d=AD)
                    rotate(k[:, :, :, 0:ROPE], k[:, :, :, ROPE:2 * ROPE], DEC, [PT_], G).then_inc(kv_ready, 1)
                    dve.wait_ge(kv_ready, c - 1)
                elif c == 5:
                    dve.tensor_copy(bias[0:1, 0:1], rope[0:1, 0, 0:1]).then_inc(gate_sum, 1)


def block_attention_turn(nc, s):
    a = s.args
    with ExitStack() as ctx:
        sb = lambda name, shape: ctx.enter_context(nc.sbuf_tensor(name, shape, F32))
        sem = lambda name: s.semaphore(name)
        pe_rows = sb("position_rows", [2 * AD // 2, AD])
        peT = sb("position_columns", [P, 2 * STRIDE])
        w_in_, moved_pe, turned_pe, turned, freed, summed = [sem(n) for n in (
            "c2_weights_in", "c2_position_moved", "c2_position_turned", "c2_turned", "c2_freed", "c2_summed")]
        block = ctx.enter_context(nc.Block())

        @block.sync
        def _(sp):
            sp.dma_start(pe_rows[:], a["cmp_pe"][0].rearrange("x s d -> (x s) d")).then_inc(w_in_, 16)
            for half in range(2):
                for odd in range(2):
                    for kv in range(2):
                        sp.dma_start(s.w1[AD * odd:AD * (odd + 1), kv, :, half, :],
                                     a["cmp_w1"][0, kv, STRIDE * half + odd:STRIDE * (half + 1):2].rearrange("s d e -> d s e")).then_inc(w_in_, 16)
            sp.dma_start(s.w2[:], a["cmp_w2"][0].rearrange("x e f -> e x f")).then_inc(w_in_, 16)
            for g in range(G):
                for t in range(NT):
                    sp.dma_start(s.gate_rows[16 * g + R * t:16 * g + R * (t + 1), :, :],
                                 s.gate_scratch.rearrange("(b t) (h x) -> t h b x", t=NT, x=3)[t, R * g:R * (g + 1)]).then_inc(w_in_, 16)
            sp.wait_ge(w_in_, 16 * (10 + QR // R))

        @block.tensor
        def _(pe):
            pe.wait_ge(w_in_, 16 * (10 + QR // R))
            pe.transpose(s.ps[0:AD, 0, 0:64], pe_rows[:], s.ident[0:64, 0:64]).then_inc(turned_pe, 1)
            pe.wait_ge(moved_pe, 1)
            for kv in range(2):
                for n in range(STRIDE):
                    at = STRIDE * kv + n
                    last = pe.matmul(s.ps[0:AD, 1, kv:kv + 1], s.w1[:, kv, n % 8, n // 8, :], peT[:, at:at + 1],
                                     start=n == 0, stop=n == STRIDE - 1)
            last.then_inc(summed, 1)
            pe.wait_ge(moved_pe, 2)
            for n in range(12):
                if n >= 4:
                    pe.wait_ge(freed, n - 3)
                for t in range(TILES):
                    r = rows(t)
                    if n < 8:
                        src = s.q_tm[0:r, t, P * n:P * (n + 1)]
                    else:
                        at = 512 * (1 + (n - 8) // 2) + P * (n % 2)
                        src = s.kv[:, t, at:at + P] if t < PT_ else s.kv_dec[:, at:at + P]
                    out = s.ps[:, 2 * (n % 4), cols(t)] if t < PT_ else s.ps[:, 2 * (n % 4) + 1, 0:DEC]
                    last = pe.transpose(out, src, s.ident[0:r, 0:r])
                last.then_inc(turned, 1)

        @block.vector
        def _(dve):
            dve.wait_ge(turned_pe, 1)
            for odd in range(2):
                last = dve.tensor_copy(peT[AD * odd:AD * (odd + 1), :],
                                       s.ps[0:AD, 0, 0:64].rearrange("d (n o) -> d n o", o=2)[:, :, odd])
            last.then_inc(moved_pe, 1)
            dve.wait_ge(summed, 1)
            dve.tensor_copy(s.pe_bias[:], s.ps[0:AD, 1, 0:2]).then_inc(moved_pe, 1)

        @block.scalar
        def _(act):
            for n in range(12):
                act.wait_ge(turned, n + 1)
                if n < 8:
                    act.mul(s.qT[:, n // 4, n % 4, :], s.ps[:, 2 * (n % 4), :], AD ** -0.5)
                    act.mul(s.qT_dec[:, n // 4, n % 4, :], s.ps[:, 2 * (n % 4) + 1, 0:DEC], AD ** -0.5).then_inc(freed, 1)
                else:
                    br, p = (n - 8) // 2, n % 2
                    act.copy(s.kT[:, br, p, :], s.ps[:, 2 * (n % 4), :])
                    act.copy(s.kT_dec[:, br, p, :], s.ps[:, 2 * (n % 4) + 1, 0:DEC]).then_inc(freed, 1)


class Compress:
    BANKS = (6, 7)

    def __init__(self, nc, s, ctx, name, nseg):
        sb = lambda n, shape: ctx.enter_context(nc.sbuf_tensor(f"{name}_{n}", shape, F32))
        self.s, self.n = s, nseg
        self.xt = sb("segments_fm", [P, 2, G, nseg])
        self.second = sb("second_half", [AD, 2, G * nseg])
        self.hid = sb("hidden", [AD, 2, G, nseg - 1])
        self.turned, self.moved, self.moved_odd, self.used, self.shifted, self.added, self.gelu, self.out = [
            s.semaphore(f"{name}_{n}") for n in (
                "x_turned", "x_moved", "x_odd_moved", "x_used", "second_ready", "hidden_in_ready", "hidden_ready", "compressed")]

    def sums(self, kv, part):
        return self.s.ps[AD * part:AD * (part + 1), kv, 0:G * self.n]

    def tensor_first(self, pe, seg, t=0):
        s, n = self.s, self.n
        for kv in range(2):
            for c in range(8 + 1):
                if c < 8:
                    u = 8 * kv + c
                    pe.wait_ge(self.moved, t * 16 + (u + 1))
                    pe.wait_ge(self.moved_odd, t * 16 + (u + 1))
                    for row in range(2):
                        for p in range(2):
                            at = 256 * kv + P * p
                            last = pe.transpose(s.ps[:, self.BANKS[u % 2], n * (2 * row + p):n * (2 * row + p + 1)],
                                                seg[:, 2 * c + row, at:at + P], s.ident[0:n, 0:n])
                    last.then_inc(self.turned, 1)
                if c > 0:
                    u = 8 * kv + c - 1
                    pe.wait_ge(self.moved, t * 16 + (u + 3))
                    pe.wait_ge(self.moved_odd, t * 16 + (u + 3))
                    pe.matmul(s.ps[:, kv, 0:G * n], s.w1[:, kv, c - 1].rearrange("p a e -> p (a e)"),
                              self.xt[:, u % 2].rearrange("p g n -> p (g n)"), start=c == 1, stop=c == 8).then_inc(self.used, 1)

    def tensor_second(self, pe, t=0):
        s, m = self.s, self.n - 1
        pe.wait_ge(self.gelu, t * 2 + 1)
        for gp in range(2):
            out, w2 = (s.ps[:, 4, 0:2 * m], s.w2[:].rearrange("p a f -> p (a f)")) if gp == 0 else (s.ps[AD:P, 4, 0:2 * m], s.w2[:, 0, :])
            last = pe.matmul(out, w2, self.hid[:, 0].rearrange("e (p g) n -> e g p n", g=2)[:, gp], start=True, stop=True)
        last.then_inc(self.out, 1)
        pe.wait_ge(self.gelu, t * 2 + 2)
        for g in range(G):
            last = pe.matmul(s.ps[0:m, 5, AD * g:AD * (g + 1)], self.hid[:, 1, g, :], s.w2[:, 1, :], start=True, stop=True)
        last.then_inc(self.out, 1)

    def move(self, eng, copy, odd, done, t, u):
        s, n = self.s, self.n
        eng.wait_ge(self.turned, t * 16 + (u + 1))
        eng.wait_ge(self.used, t * 16 + (u + 1))
        for row in range(2):
            out = self.xt[AD * row:AD * (row + 1), u % 2].rearrange("d (p g) n -> d g p n", g=2)[:, odd]
            src = s.ps[AD * odd:AD * (odd + 1), self.BANKS[u % 2], 2 * n * row:2 * n * (row + 1)]
            last = copy(out, src.rearrange("d (p n) -> d p n", p=2))
        last.then_inc(done, 1)

    def scalar_first(self, act, t=0, between={}):
        s = self.s

        def shift(kv):
            act.wait_ge(self.used, t * 16 + (8 * (kv + 1) + 2))
            act.activation(self.second[:, kv], self.sums(kv, 1), ACT.Identity, bias=s.pe_bias[:, kv:kv + 1]).then_inc(self.shifted, 1)

        def gelu(kv):
            act.wait_ge(self.added, t * 2 + (kv + 1))
            act.activation(self.hid[:, kv], self.hid[:, kv], ACT.Gelu_apprx_tanh).then_inc(self.gelu, 1)

        for u in range(16):
            self.move(act, act.copy, 0, self.moved, t, u)
            if u in between:
                between[u]()
            if u == 9:
                shift(0)
            if u == 13:
                gelu(0)
        shift(1)
        gelu(1)

    def vector_first(self, dve, t=0, between={}):
        s, n = self.s, self.n
        groups = lambda ap: ap.rearrange("e (g n) -> e g n", g=G)

        def add(kv):
            dve.wait_ge(self.shifted, t * 2 + (kv + 1))
            dve.tensor_tensor(self.hid[:, kv], groups(self.sums(kv, 0))[:, :, 0:n - 1], groups(self.second[:, kv])[:, :, 1:n],
                              ALU.add).then_inc(self.added, 1)

        for u in range(16):
            self.move(dve, dve.tensor_copy, 1, self.moved_odd, t, u)
            if u in between:
                between[u]()
            if u == 10:
                add(0)
        add(1)

    def vector_second(self, dve, kc, vc, t=0):
        s, m = self.s, self.n - 1
        dve.wait_ge(self.out, t * 2 + 1)
        dve.tensor_copy(kc, s.ps[:, 4, 0:2 * m].rearrange("p (a n) -> p a n", a=2))
        dve.wait_ge(self.out, t * 2 + 2)
        return dve.tensor_copy(vc, s.ps[0:m, 5, 0:G * AD])


def block_compress_prompt(nc, s):
    a = s.args
    with ExitStack() as ctx:
        seg = s.ring.whole[0:PSEG].rearrange("p (s n) -> p s n", s=STRIDE)
        seg_in, done = [s.semaphore(n) for n in ("seg_in", "compress_done")]
        comp = Compress(nc, s, ctx, "pc", PSEG)
        block = ctx.enter_context(nc.Block())

        @block.sync
        def _(sp):
            sp.dma_start(seg[:], a["p_cmp"][0, 0].rearrange("(n s) x g d -> n s (x g d)", s=STRIDE)).then_inc(seg_in, 16)

        @block.tensor
        def _(pe):
            pe.sem_inc(comp.used, 2)
            pe.wait_ge(seg_in, 16)
            comp.tensor_first(pe, seg)
            comp.tensor_second(pe)

        @block.scalar
        def _(act):
            act.sem_inc(comp.moved, 2)
            comp.scalar_first(act)

        @block.vector
        def _(dve):
            dve.sem_inc(comp.moved_odd, 2)
            comp.vector_first(dve)
            comp.vector_second(dve, s.kc_p[:], s.vc_p[:]).then_inc(done, 1)


def block_attention_prompt(nc, s):
    a = s.args
    with ExitStack() as ctx:
        sb = lambda name, shape, dt=F32: ctx.enter_context(nc.sbuf_tensor(name, shape, dt))
        sem = lambda name: s.semaphore(name)
        causal = sb("causal_add", [P, P], BF16)
        cmp_add = sb("cmp_add", [P, PT_, PCMP], BF16)
        eye = sb("identity_bf16", [P, P], BF16)
        qs = sb("q_of_r", [P, 2, 2, SEQ])
        prob = sb("prob", [P, 4, SEQ])
        pT = sb("prob_turned", [P, 3, SEQ])
        nmax = sb("minus_max", [P, 8])
        sums = sb("sums", [P, 4, 3])
        alpha = sb("alpha", [P, 2, 3])
        acc = sb("acc", [P, AD])
        in_, zeroed, q_ready, scored, maxed, exped, turned, moved, weighed, step, combined = [sem(n) for n in (
            "a_masks_in", "a_q_zeroed", "a_q_ready", "a_scored", "a_maxed", "a_exped", "a_turned", "a_moved", "a_weighed",
            "a_step", "a_combined")]
        block = ctx.enter_context(nc.Block())
        UNITS = [(g, i, br) for g in range(G) for i in range(PT_) for br in range(3)]
        N = len(UNITS)
        S_BANKS, T_BANKS, O_BANKS = (0, 1, 2), (3, 4, 5), (6, 7)
        TURN, MOVE, WEIGH, COMBINE = 3, 4, 6, 7
        EXPED, TURNED, MOVED, WEIGHED, COMB = 3, 4, 3, 3, 4

        def keys(u):
            g, i, br = UNITS[u]
            return PCMP if br == 0 else P * (i + 1)

        def blocks(u):
            g, i, br = UNITS[u]
            return [(0, PCMP)] if br == 0 else [(j, P) for j in range(i + 1)]

        @block.sync
        def _(sp):
            sp.dma_start(prob[:, 0, 0:P], a["causal_add"]).then_inc(in_, 16)
            sp.dma_start(prob[:, 1, 0:PT_ * PCMP].rearrange("p (t n) -> p t n", t=PT_), a["cmp_add"]).then_inc(in_, 16)

        @block.tensor
        def _(pe):
            with pe.Fori(0, R) as r:
                pe.wait_ge(q_ready, r + 1)
                for n in range(N + WEIGH):
                    if n < N:
                        u = n
                        g, i, br = UNITS[u]
                        bank = s.ps[:, S_BANKS[u % 3], :]
                        pe.wait_ge(exped, r * N + (u + 1))
                        rhs = s.kc_p[:, g // 2, :] if br == 0 else s.kT[:, br - 1, g // 2, 0:keys(u)]
                        pe.matmul(bank[:, 0:keys(u)], qs[:, g % 2, g // 2, cols(i)], rhs, start=True, stop=False)
                        out, mask = (bank[:, 0:PCMP], cmp_add[:, i, :]) if br == 0 else (bank[:, keys(u) - P:keys(u)], causal[:])
                        pe.matmul(out, eye[:], mask, start=False, stop=True).then_inc(scored, 1)
                    if n >= WEIGH:
                        u = n - WEIGH
                        g, i, br = UNITS[u]
                        tile = u // 3
                        pe.wait_ge(moved, r * N + (u + 1 + MOVED))
                        if br == 0:
                            pe.wait_ge(combined, r * (N // 3) + (tile - 2 + 1 + COMB))
                        for j, w in blocks(u):
                            v = s.vc_p[:, AD * g:AD * (g + 1)] if br == 0 else \
                                s.kv[:, j, 512 * br + 256 + AD * g:512 * br + 256 + AD * (g + 1)]
                            last = pe.matmul(s.ps[:, O_BANKS[tile % 2], AD * br:AD * (br + 1)], pT[0:w, u % 3, P * j:P * (j + 1)],
                                             v, start=j == 0, stop=j == blocks(u)[-1][0])
                        last.then_inc(weighed, 1)
                    if TURN <= n < N + TURN:
                        u = n - TURN
                        pe.wait_ge(exped, r * N + (u + 1 + EXPED))
                        pe.wait_ge(moved, r * N + (u + 1))
                        for j, w in blocks(u):
                            last = pe.transpose(s.ps[0:w, T_BANKS[u % 3], P * j:P * (j + 1)], prob[:, u % 4, P * j:P * j + w],
                                                s.ident[:])
                        last.then_inc(turned, 1)

        @block.scalar
        def _(act):
            act.sem_inc(exped, EXPED)
            act.sem_inc(moved, MOVED)
            act.wait_ge(zeroed, 1)
            with act.Fori(0, R) as r:
                act.wait_ge(weighed, r * N + WEIGHED)
                for odd in range(2):
                    h = slice(AD * odd, AD * (odd + 1))
                    last = act.copy(qs[h, odd], s.qT[h, :, bass.ds(r, 1), :].rearrange("p a o n -> p (a o) n"))
                last.then_inc(q_ready, 1)
                for n in range(N + MOVE):
                    if n >= MOVE:
                        u = n - MOVE
                        act.wait_ge(turned, r * N + (u + 1 + TURNED))
                        act.wait_ge(weighed, r * N + (u + 1))
                        w, width = (PCMP, P) if UNITS[u][2] == 0 else (P, keys(u))
                        act.copy(pT[0:w, u % 3, 0:width], s.ps[0:w, T_BANKS[u % 3], 0:width]).then_inc(moved, 1)
                    if n < N:
                        u = n
                        act.wait_ge(maxed, r * N + (u + 1))
                        act.wait_ge(turned, r * N + (u + 1))
                        if u % 3 == 0:
                            act.wait_ge(combined, r * (N // 3) + (u // 3 + 1))
                        act.activation(prob[:, u % 4, 0:keys(u)], s.ps[:, S_BANKS[u % 3], 0:keys(u)], ACT.Exp,
                                       bias=nmax[:, u % 8:u % 8 + 1],
                                       accum_out=sums[:, (u // 3) % 4, u % 3:u % 3 + 1]).then_inc(exped, 1)

        @block.vector
        def _(dve):
            link = Chain(dve, step)
            dve.sem_inc(combined, COMB)
            dve.sem_inc(weighed, WEIGHED)
            dve.sem_inc(turned, TURNED)
            dve.memset(qs[AD:P, 0], 0.0)
            dve.memset(qs[0:AD, 1], 0.0)
            dve.tensor_copy(eye[:], s.ident[:])
            dve.wait_ge(in_, 32)
            dve.tensor_copy(causal[:], prob[:, 0, 0:P])
            dve.tensor_copy(cmp_add[:].rearrange("p t n -> p (t n)"), prob[:, 1, 0:PT_ * PCMP]).then_inc(zeroed, 1)
            STEPS = G + N // 3 * 5
            with dve.Fori(0, R) as r:
                link.enter(r, STEPS)

                def largest(u):
                    g, i, br = UNITS[u]
                    nm = nmax[:, u % 8:u % 8 + 1]
                    dve.wait_ge(scored, r * N + (u + 1))
                    last = dve.tensor_reduce(nm, s.ps[:, S_BANKS[u % 3], 0:keys(u)], X, ALU.max, negate=True)
                    if br == 0 and i == 0:
                        link(last)
                        last = dve.tensor_scalar(nm, nm, 1e29, None, ALU.min)
                    last.then_inc(maxed, 1)

                def combine(t):
                    g, i, _ = UNITS[3 * t]
                    k = t % 2
                    dve.wait_ge(exped, r * N + (3 * t + 3 + EXPED))
                    link(dve.tensor_scalar(alpha[:, k], sums[:, t % 4], TINY, None, ALU.max))
                    link(dve.reciprocal(alpha[:, k], alpha[:, k]))
                    gate = s.branch_gates[:, i, bass.ds(r * 3 + 12 * g, 3)]
                    link(dve.tensor_tensor(alpha[:, k], alpha[:, k], gate, ALU.mult))
                    dve.wait_ge(weighed, r * N + (3 * t + 3 + WEIGHED))
                    o = s.ps[:, O_BANKS[k], :]
                    link(dve.tensor_scalar(acc[:], o[:, 0:AD], alpha[:, k, 0:1], None, ALU.mult))
                    link(dve.scalar_tensor_tensor(acc[:], o[:, AD:2 * AD], alpha[:, k, 1:2], acc[:], ALU.mult, ALU.add))
                    dve.scalar_tensor_tensor(s.ha[:, i, bass.ds(r * AD + 256 * g, AD)], o[:, 2 * AD:3 * AD], alpha[:, k, 2:3],
                                             acc[:], ALU.mult, ALU.add).then_inc(combined, 1)

                for n in range(N + COMBINE):
                    if n < N:
                        largest(n)
                    if n >= COMBINE and (n - COMBINE) % 3 == 2:
                        combine((n - COMBINE) // 3)
                link.leave(R)


def block_attention_out(nc, s):
    with ExitStack() as ctx:
        turned, freed = [s.semaphore(n) for n in ("ao_turned", "ao_freed")]
        block = ctx.enter_context(nc.Block())

        @block.tensor
        def _(pe):
            for k in range(KT):
                if k >= 4:
                    pe.wait_ge(freed, k - 3)
                for t in range(PT_):
                    last = pe.transpose(s.ps[:, k % 4, cols(t)], s.ha[:, t, k * P:(k + 1) * P], s.ident[:])
                last.then_inc(turned, 1)

        @block.scalar
        def _(act):
            for k in range(KT):
                act.wait_ge(turned, k + 1)
                act.copy(s.hat[:, k, 0:SEQ], s.ps[:, k % 4, :]).then_inc(freed, 1)


def token_rows(prompt, sample, t):
    return prompt[0, t * P:(t + 1) * P, :] if t < PT_ else sample.rearrange("b t n -> (b t) n")


def block_attention_decode(nc, s):
    a, ring = s.args, s.ring
    NK = PAST + DEC
    NW = WIN + DEC
    with ExitStack() as ctx:
        sb = lambda name, shape, dt=F32: ctx.enter_context(nc.sbuf_tensor(name, shape, dt))
        sem = lambda name: s.semaphore("e_" + name)
        ptab = sb("page_table_sb", [1, NB * NPAGE], I32)
        win_add = sb("win_add", [QR, WIN])
        new_add = sb("new_add", [QR, NB, DEC])
        cover = sb("cover", [NCMP, NBLK + 1])
        same_gt = sb("same_gt", [QR, P])
        forced = sb("forced", [QR, NBLK + 1])
        slc = sb("slc_pages", [P, NPAGE, 512])
        win = sb("win_rows", [P, PT_, 512])
        seg = ring.whole[:].rearrange("p (s n) -> p s n", s=STRIDE)
        comp = Compress(nc, s, ctx, "dc", NSEG)
        kc = sb("kc_dec", [P, 2, NCMP])
        vc = sb("vc_dec", [NCMP, G * AD])
        kT = sb("k_turned", [P, 2, 2, 512])
        qb = sb("q_blocks", [P, 2, QR])
        sc = sb("cmp_prob", [QR, 2, NCMP])
        ss = sb("slc_prob", [QR, NK])
        sw = sb("win_prob", [QR, NW])
        pcT = sb("cmp_prob_turned", [NCMP, 2, QR])
        pT = sb("probs_turned", [P, 22, QR])
        imp = sb("importance", [QR, 2, NBLK + 1])
        top = sb("top8", [QR, 8])
        at_wait = sb("at_wait", [QR, 4])
        o_tm = sb("output_rows", [QR, G * AD])
        nmax = sb("minus_max_dec", [QR, 3])
        sums = sb("sums_dec", [QR, 3])
        alpha = sb("alpha_dec", [QR, 3])
        (const_in, keys_in, cmp_in, values_in, q_set, packed, c_max, c_prob, c_copied, imp_copied, s_max, s_scaled, w_max,
         w_scaled, out_done, k_moved, c_exp, w_exp, s_exp, p_moved, small_scored, k_turned, scored, c_turned, imp_done,
         p_turned, weighed, s_read, o_copied, o_turned, step) = [sem(n) for n in (
             "const_in", "keys_in", "cmp_in", "values_in", "q_set", "packed", "c_max", "c_prob", "c_copied", "imp_copied",
             "s_max", "s_scaled", "w_max", "w_scaled", "out_done", "k_moved", "c_exp", "w_exp", "s_exp", "p_moved",
             "small_scored", "k_turned", "scored", "c_turned", "imp_done", "p_turned", "weighed", "s_read", "o_copied", "o_turned", "step")]
        block = ctx.enter_context(nc.Block())
        KU = 10
        IN = 16 * (NPAGE + 1)
        K_MOVED, OUT = 2, 1

        @block.sync
        def _(sp):
            sp.dma_start(ptab[:], a["page_table"].rearrange("b p -> (b p)").unsqueeze(0)).then_inc(const_in, 16)
            for src, dst in (("win_add", win_add), ("new_add", new_add), ("cover", cover), ("same_gt", same_gt), ("forced", forced)):
                sp.dma_start(dst[:], a[src]).then_inc(const_in, 16)
            sp.wait_ge(const_in, 16)
            sp.wait_ge(const_in, 96)

            def load(b, value, loaded):
                c = slice(256 * value, 256 * (value + 1))
                w = a["cache_win_kv"][0, bass.ds(b, 1)].rearrange("o (n p) x g d -> p (o n) (x g d)", p=P)
                sp.dma_start(win[:, :, c], w[:, :, c]).then_inc(loaded, 16)
                for pg in range(NPAGE):
                    page = sp.value_load(ptab[0:1, bass.ds(b * NPAGE + pg, 1)], min_val=0, max_val=a["cache_slc_kv"].shape[1] - 1)
                    rows_ = a["cache_slc_kv"][0, bass.ds(page, 1)].rearrange("o n x g d -> (o n) (x g d)")
                    sp.dma_start(slc[:, pg, c], rows_[:, c]).then_inc(loaded, 16)

            load(0, 0, keys_in)
            load(0, 1, values_in)
            with sp.Fori(0, NB - 1) as i:
                sp.wait_ge(k_turned, i * KU + KU)
                load(i + 1, 0, keys_in)
                sp.wait_ge(weighed, i + 1)
                load(i + 1, 1, values_in)
            sp.wait_ge(comp.turned, 16 * NB)
            ring.begin(1)
            ring.load_part(sp, 0, matrix(a["w_in"][0], O_GA, 256))
            ring.load_part(sp, 1, matrix(a["w_branch_m"][0], 0, 256))

        @block.gpsimd
        def _(pool):
            pool.wait_ge(const_in, 96)

            def load(b):
                for pg in range(NPAGE):
                    page = pool.value_load(ptab[0:1, bass.ds(b * NPAGE + pg, 1)], min_val=0, max_val=a["cache_cmp_kv"].shape[1] - 1)
                    pool.dma_start(seg[8 * pg:8 * (pg + 1)],
                                   a["cache_cmp_kv"][0, bass.ds(page, 1)].rearrange("o (n s) x g d -> (o n) s (x g d)", s=STRIDE)).then_inc(cmp_in, 16)

            load(0)
            with pool.Fori(0, NB - 1) as i:
                pool.wait_ge(comp.turned, i * 16 + 16)
                load(i + 1)

        @block.tensor
        def _(pe):
            pe.sem_inc(comp.used, 2)

            def turn(out, rows_of_queries, waits):
                if waits:
                    return pe.matmul(out, rows_of_queries, s.ident[0:QR, 0:QR], start=True, stop=True)
                return pe.transpose(out, rows_of_queries, s.ident[0:QR, 0:QR])

            pe.wait_ge(const_in, 96)

            def sequence(b, more):
                pe.wait_ge(out_done, b + OUT)
                comp.tensor_second(pe, b)
                pe.wait_ge(packed, b + 1)
                pe.wait_ge(q_set, b + 1)
                for at, n, rhs in ((0, NCMP, kc), (128, DEC, s.kT_dec[:, 0]), (160, DEC, s.kT_dec[:, 1])):
                    for p in range(2):
                        last = pe.matmul(s.ps[0:QR, 5, at:at + n], qb[:, p, :], rhs[:, p, :], start=p == 0, stop=p == 1)
                last.then_inc(small_scored, 1)

                def turn_keys(v):
                    src = slc if v < 8 else win
                    if v == 0:
                        pe.wait_ge(keys_in, b * IN + IN)
                    pe.wait_ge(k_moved, b * KU + (v - 2 + 1 + K_MOVED))
                    for pg in range(4):
                        last = pe.transpose(s.ps[:, 6 + v % 2, P * pg:P * (pg + 1)],
                                            src[:, (4 * (v // 2) if v < 8 else 0) + pg, P * (v % 2):P * (v % 2 + 1)], s.ident[:])
                    last.then_inc(k_turned, 1)

                def score(c):
                    pe.wait_ge(k_moved, b * KU + (2 * c + 2 + K_MOVED))
                    for p in range(2):
                        last = pe.matmul(s.ps[0:QR, c, :], qb[:, p, :], kT[:, c % 2, p, :], start=p == 0, stop=p == 1)
                    last.then_inc(scored, 1)

                turn_keys(0)
                turn_keys(1)
                turn_keys(2)
                score(0)
                turn_keys(3)
                pe.wait_ge(c_prob, b + 1)
                for k in range(2):
                    last = turn(s.ps[0:NCMP, 5, 192 + QR * k:192 + QR * (k + 1)], sc[:, k, :], k == 0)
                last.then_inc(c_turned, 1)
                turn_keys(4)
                score(1)
                pe.wait_ge(c_copied, b + 1)
                pe.matmul(s.ps[0:QR, 5, 320:320 + NBLK + 1], pcT[:, 0, :], cover[:], start=True, stop=True).then_inc(imp_done, 1)
                turn_keys(5)
                turn_keys(6)
                score(2)
                pe.wait_ge(imp_copied, b + 1)
                pe.matmul(s.ps[:, 5, 360:360 + NBLK + 1], same_gt[:], imp[:, 0, :], start=True, stop=True).then_inc(imp_done, 1)
                turn_keys(7)
                turn_keys(8)
                score(3)
                turn_keys(9)
                score(4)
                if more:
                    pe.wait_ge(cmp_in, b * (16 * NPAGE) + 2 * 16 * NPAGE)
                    pe.wait_ge(s_read, b + 1)
                    comp.tensor_first(pe, seg, b + 1)
                for w, blocks in enumerate((range(16, 22), range(0, 8), range(8, 16))):
                    if w == 0:
                        pe.wait_ge(w_scaled, b + 1)
                    pe.wait_ge(s_scaled, b + 1)
                    if w == 2:
                        pe.wait_ge(p_moved, b * 3 + 1)
                    for n, blk in enumerate(blocks):
                        if blk < 16:
                            src = ss[:, P * blk:P * (blk + 1)]
                        elif blk < 20:
                            src = sw[:, P * (blk - 16):P * (blk - 15)]
                        else:
                            src = ss[:, PAST:NK] if blk == 20 else sw[:, WIN:NW]
                        k = P if blk < 20 else DEC
                        last = turn(s.ps[0:k, 6 + w % 2, QR * n:QR * (n + 1)], src, n == 0)
                    last.then_inc(p_turned, 1)
                pe.wait_ge(p_moved, b * 3 + 3)
                pe.wait_ge(values_in, b * IN + IN)
                terms = [(pcT[:, 1, :], vc[:])] + [(pT[:, n, :], slc[:, n, 256:512]) for n in range(16)] \
                    + [(pT[:, 16 + n, :], win[:, n, 256:512]) for n in range(4)] \
                    + [(pT[0:DEC, 20 + n, :], s.kv_dec[:, 512 * (1 + n) + 256:512 * (2 + n)]) for n in range(2)]
                for n, (lhs, rhs) in enumerate(terms):
                    last = pe.matmul(s.ps[0:QR, 4, 0:G * AD], lhs, rhs, start=n == 0, stop=n == len(terms) - 1)
                last.then_inc(weighed, 1)
                pe.wait_ge(o_copied, b + 1)
                for p in range(2):
                    last = turn(s.ps[:, 5, QR * p:QR * (p + 1)], o_tm[:, P * p:P * (p + 1)], p == 0)
                last.then_inc(o_turned, 1)

            pe.wait_ge(cmp_in, 16 * NPAGE)
            comp.tensor_first(pe, seg, 0)
            with pe.Fori(0, NB - 1) as b:
                sequence(b, True)
            sequence(NB - 1, False)

        @block.scalar
        def _(act):
            act.sem_inc(comp.moved, 2)
            act.sem_inc(k_moved, K_MOVED)

            def sequence(b, more):
                def move(v):
                    act.wait_ge(k_turned, b * KU + (v + 1))
                    if v >= 4:
                        act.wait_ge(scored, b * 5 + (v // 2 - 1))
                    act.copy(kT[:, (v // 2) % 2, v % 2, :], s.ps[:, 6 + v % 2, :]).then_inc(k_moved, 1)

                move(0)
                move(1)
                act.wait_ge(c_max, b + 1)
                act.activation(sc[:, 0, :], s.ps[0:QR, 5, 0:NCMP], ACT.Exp, bias=nmax[:, 0:1], accum_out=sums[:, 0:1]).then_inc(c_exp, 1)
                for v in range(2, KU):
                    move(v)

                def slc_exp():
                    act.wait_ge(s_max, b + 1)
                    act.activation(ss[:], ss[:], ACT.Exp, bias=nmax[:, 1:2], accum_out=sums[:, 1:2]).then_inc(s_exp, 1)

                def win_exp():
                    act.wait_ge(w_max, b + 1)
                    act.activation(sw[:], sw[:], ACT.Exp, bias=nmax[:, 2:3], accum_out=sums[:, 2:3]).then_inc(w_exp, 1)

                if more:
                    comp.scalar_first(act, b + 1, {1: slc_exp, 3: win_exp})
                else:
                    slc_exp()
                    win_exp()
                act.wait_ge(p_turned, b * 3 + 1)
                act.copy(pT[:, 16:20, :], s.ps[:, 6, 0:4 * QR].rearrange("p (a n) -> p a n", a=4))
                act.copy(pT[0:DEC, 20:22, :], s.ps[0:DEC, 6, 4 * QR:6 * QR].rearrange("p (a n) -> p a n", a=2)).then_inc(p_moved, 1)
                for w in range(1, 3):
                    act.wait_ge(p_turned, b * 3 + w + 1)
                    act.copy(pT[:, 8 * (w - 1):8 * w, :], s.ps[:, 6 + w % 2, :].rearrange("p (a n) -> p a n", a=8)).then_inc(p_moved, 1)

            comp.scalar_first(act, 0)
            with act.Fori(0, NB - 1) as b:
                sequence(b, True)
            sequence(NB - 1, False)

        @block.vector
        def _(dve):
            link = Chain(dve, step)
            dve.wait_ge(const_in, 96)
            dve.sem_inc(out_done, OUT)
            dve.sem_inc(comp.moved_odd, 2)
            link(dve.memset(qb[:], 0.0))
            STEPS = 17

            def sequence(b, more):
                for p in range(2):
                    for gp in range(2):
                        at = 32 * p + 16 * gp
                        last = dve.tensor_copy(qb[AD * gp:AD * (gp + 1), p, at:at + 16].rearrange("d (t r) -> d r t", t=NT),
                                               s.qT_dec[AD * gp:AD * (gp + 1), p, :, bass.ds(b * NT, NT)])
                last.then_inc(q_set, 1)
                comp.vector_second(dve, kc[:], vc[:], b).then_inc(packed, 1)
                dve.wait_ge(small_scored, b + 1)
                dve.tensor_reduce(nmax[:, 0:1], s.ps[0:QR, 5, 0:NCMP], X, ALU.max, negate=True).then_inc(c_max, 1)
                dve.wait_ge(c_exp, b + 1)
                link(dve.tensor_scalar(alpha[:, 0:1], sums[:, 0:1], TINY, None, ALU.max))
                link(dve.reciprocal(alpha[:, 0:1], alpha[:, 0:1]))
                link(dve.tensor_scalar(sc[:, 0, :], sc[:, 0, :], alpha[:, 0:1], None, ALU.mult))
                dve.tensor_scalar(sc[:, 1, :], sc[:, 0, :], s.gate_rows[:, bass.ds(b, 1), 0], None, ALU.mult).then_inc(c_prob, 1)
                dve.wait_ge(c_turned, b + 1)
                dve.tensor_copy(pcT[:], s.ps[0:NCMP, 5, 192:192 + 2 * QR].rearrange("p (a n) -> p a n", a=2)).then_inc(c_copied, 1)
                dve.wait_ge(imp_done, b * 2 + 1)
                dve.tensor_copy(imp[:, 0, :], s.ps[0:QR, 5, 320:320 + NBLK + 1]).then_inc(imp_copied, 1)
                dve.wait_ge(imp_done, b * 2 + 2)
                link(dve.tensor_tensor(imp[:, 1, :], s.ps[0:QR, 5, 360:360 + NBLK + 1], forced[:], ALU.add))
                for n in range(TOPK // 8):
                    dve.memset(at_wait[:, 2 * n:2 * n + 1], 0.0)
                    link(dve.max(top[:], imp[:, 1, :]))
                    dve.memset(at_wait[:, 2 * n + 1:2 * n + 2], 0.0)
                    link(dve.match_replace(imp[:, 1, :], top[:], imp[:, 1, :], -3e38))
                link(dve.tensor_scalar(imp[:, 1, :], imp[:, 1, :], -2e38, NEG, ALU.is_gt, ALU.mult))
                for c in range(4):
                    dve.wait_ge(scored, b * 5 + (c + 1))
                    last = dve.tensor_tensor(ss[:, 512 * c:512 * (c + 1)].rearrange("p (n k) -> p n k", k=BLK),
                                             s.ps[0:QR, c, :].rearrange("p (n k) -> p n k", k=BLK),
                                             imp[:, 1, 8 * c:8 * (c + 1)].unsqueeze(2).to_broadcast([QR, 8, BLK]), ALU.add)
                last.then_inc(s_read, 1)
                new = new_add[:, bass.ds(b, 1), :].rearrange("p o n -> p (o n)")
                link(dve.tensor_tensor(ss[:, PAST:NK], s.ps[0:QR, 5, 128:128 + DEC], new, ALU.add))
                dve.wait_ge(s_read, b + 1)

                def slc_max():
                    dve.tensor_reduce(nmax[:, 1:2], ss[:], X, ALU.max, negate=True).then_inc(s_max, 1)

                def win_max():
                    dve.wait_ge(scored, b * 5 + 5)
                    dve.tensor_tensor(sw[:, 0:WIN], s.ps[0:QR, 4, :], win_add[:], ALU.add)
                    link(dve.tensor_tensor(sw[:, WIN:NW], s.ps[0:QR, 5, 160:160 + DEC], new, ALU.add))
                    dve.tensor_reduce(nmax[:, 2:3], sw[:], X, ALU.max, negate=True).then_inc(w_max, 1)

                def scale(k, prob, expd, scaled):
                    dve.wait_ge(expd, b + 1)
                    link(dve.tensor_scalar(alpha[:, k:k + 1], sums[:, k:k + 1], TINY, None, ALU.max))
                    link(dve.reciprocal(alpha[:, k:k + 1], alpha[:, k:k + 1]))
                    link(dve.tensor_tensor(alpha[:, k:k + 1], alpha[:, k:k + 1], s.gate_rows[:, bass.ds(b, 1), k], ALU.mult))
                    dve.tensor_scalar(prob[:], prob[:], alpha[:, k:k + 1], None, ALU.mult).then_inc(scaled, 1)

                slc_scale = lambda: scale(1, ss, s_exp, s_scaled)
                win_scale = lambda: scale(2, sw, w_exp, w_scaled)
                if more:
                    comp.vector_first(dve, b + 1, {1: slc_max, 3: win_max, 5: slc_scale, 7: win_scale})
                else:
                    for part in (slc_max, win_max, slc_scale, win_scale):
                        part()
                dve.wait_ge(weighed, b + 1)
                dve.tensor_copy(o_tm[:], s.ps[0:QR, 4, 0:G * AD]).then_inc(o_copied, 1)
                dve.wait_ge(o_turned, b + 1)
                for gp in range(2):
                    for odd in range(2):
                        out = s.hat[AD * odd:AD * (odd + 1), :, bass.ds(b * NT + SEQ, NT)] \
                            .rearrange("d (p g h) t -> d g p h t", p=2, g=2)[:, gp]
                        o = s.ps[AD * gp:AD * (gp + 1), 5, 0:2 * 96].rearrange("d (p q) -> d p q", p=2)[:, :, 0:32] \
                            .rearrange("d p (g t h o) -> d g o p h t", g=2, t=NT, o=2)
                        last = dve.tensor_copy(out, o[:, gp, odd])
                last.then_inc(out_done, 1)

            comp.vector_first(dve, 0)
            with dve.Fori(0, NB - 1) as b:
                link.enter(b, STEPS)
                sequence(b, True)
                link.leave(NB - 1)
            sequence(NB - 1, False)


def block_modulation_rest(nc, s):
    a, ring = s.args, s.ring
    C = DEC + 1
    CHUNKS = (4, 5, 10, 11, 6, 7, 8, 9)
    with ExitStack() as ctx:
        sb = lambda name, shape: ctx.enter_context(nc.sbuf_tensor(name, shape, F32))
        sem = lambda name: s.semaphore("r_" + name)
        bias = sb("multiplier_bias", [C, 2, D])
        gain = sb("post_gain", [C, 2, D])
        gt = sb("residual_multipliers", [C, 2, D])
        ffn_rows = sb("ffn_modulation_rows", [C, 2, 512])
        rows_in, made, read, turned, summed, ready, stored, step = [sem(n) for n in (
            "rows_in", "made", "read", "turned", "summed", "ready", "stored", "step")]
        block = ctx.enter_context(nc.Block())

        @block.sync
        def _(sp):
            for n, g in enumerate(("g_post_mix", "g_post_ffn")):
                at = (2 + 3 * n) * D
                sp.dma_start(bias[:, n, :], a["b_ada"][0, at:at + D].partition_broadcast(C)).then_inc(rows_in, 16)
                sp.dma_start(gain[:, n, :], a[g][0].partition_broadcast(C)).then_inc(rows_in, 16)
            for n, c in enumerate(CHUNKS):
                ring.load(sp, n % 2, matrix(a["w_ada"][0], 512 * c), after=(made, n - 1) if n >= 2 else None)
            sp.wait_ge(ready, 4)
            sp.dma_start(s.multiplier_rows, gt[:]).then_inc(stored, 16)
            sp.wait_ge(stored, 16)

        @block.tensor
        def _(pe):
            for n in range(len(CHUNKS) + 1):
                if n < len(CHUNKS):
                    ring.await_load(pe, n % 2)
                    if n >= 2:
                        pe.wait_ge(read, n - 1)
                    for k in range(KT):
                        last = pe.matmul(s.ps[0:C, n % 2, :], s.cT[:, k, :], ring.view(n % 2)[:, k, :], start=k == 0, stop=k == KT - 1)
                    last.then_inc(made, 1)
                if n > 4:
                    pe.wait_ge(read, n)
                    if n > 6:
                        pe.wait_ge(summed, n - 6)
                    turn_modulation(pe, s, ffn_rows[:, n % 2, :], 2 + n % 2).then_inc(turned, 1)

        @block.vector
        def _(dve):
            link = Chain(dve, step)
            dve.wait_ge(rows_in, 64)
            for n in range(4):
                dve.wait_ge(made, n + 1)
                c = slice(512 * (n % 2), 512 * (n % 2 + 1))
                out = gt[:, n // 2, c]
                dve.tensor_tensor(out, s.ps[0:C, n % 2, :], bias[:, n // 2, c], ALU.add).then_inc(read, 1)
                dve.wait_ge(read, n + 1)
                dve.tensor_tensor(out, out, gain[:, n // 2, c], ALU.mult).then_inc(ready, 1)
            for n in range(4, len(CHUNKS)):
                dve.wait_ge(made, n + 1)
                if n >= 6:
                    dve.wait_ge(turned, n - 5)
                dve.tensor_copy(ffn_rows[:, (n + 1) % 2, :], s.ps[0:C, n % 2, :]).then_inc(read, 1)
                j = n - 4
                dve.wait_ge(turned, j + 1)
                dve.tensor_tensor(s.mod[:, 16 + 4 * j:20 + 4 * j, :], s.ps[:, 2 + (n + 1) % 2, 0:4 * C].rearrange("p (j n) -> p j n", j=4),
                                  s.vecT[:, 0, V_SHF + 4 * j:V_SHF + 4 * j + 4].unsqueeze(2).to_broadcast([P, 4, C]),
                                  ALU.add).then_inc(summed, 1)
            dve.wait_ge(summed, 4)
            link(dve.scalar_tensor_tensor(s.mod[:, 24:32, :], s.mod[:, 24:32, :], 1.0,
                                          s.vecT[:, 0, V_GF:V_GF + 8].unsqueeze(2).to_broadcast([P, 8, C]),
                                          ALU.add, ALU.mult))


NST = 2 * NB


def block_branches(nc, s, mix, project_loads):
    a, ring = s.args, s.ring
    w_in, w_m, w_a = a["w_in"][0], a["w_branch_m"][0], a["w_branch_a"][0]
    CHUNKS = [c for q in range(4) for c in ((w_in, O_GA + 256 * q, 0), (w_m, 256 * q, 1),
                                            (w_in, O_GA + D + 256 * q, 0), (w_a, 256 * q, 2))]
    NC = len(CHUNKS)
    with ExitStack() as ctx:
        sb = lambda name, shape: ctx.enter_context(nc.sbuf_tensor(name, shape, F32))
        sem = lambda name: s.semaphore("b_" + name)
        sg = sb("gate", [P, 2, 2, TOK])
        state_rows = sb("conv_state_rows", [NST, 2 * DFF])
        state_in, state_turned, state_moved = [sem(n) for n in ("state_in", "state_turned", "state_moved")]
        operands = (s.ht, s.hmt, s.hat)
        ring.room(nc, ctx, "branches")
        high, low = [ctx.enter_context(nc.sbuf_tensor(f"h_{n}", [P, KT, TOK], F32R)) for n in ("high", "low")]
        cut, split, w_cut, w_split = [sem(n) for n in ("h_cut", "h_split", "w_cut", "w_split")]
        w_parts = [ring.rounded[:, 0, n, :] for n in range(2)]
        tiles = lambda ap: ap.rearrange("p (k n) -> p k n", k=KT)
        gate_done, gate_free, branch_done, branch_free, gated = [sem(n) for n in (
            "gate_done", "gate_free", "branch_done", "branch_free", "gated")]
        block = ctx.enter_context(nc.Block())
        ring.begin(1)
        bank = lambda m, branch: s.ps[:, 4 * branch + 2 * (m % 2):4 * branch + 2 * (m % 2) + 2, 0:HALF]

        @block.sync
        def _(sp):
            sp.dma_start(state_rows[:], a["state_conv"][0].rearrange("b r n -> (b r) n")).then_inc(state_in, 16)
            for n in range(2, NC):
                w, c, _ = CHUNKS[n]
                ring.load_part(sp, n, matrix(w, c, 256), after=(branch_done if n % 2 else gate_done, 2 * (n // 2)))
            project_loads(sp, gate_done, branch_done)

        @block.tensor
        def _(pe):
            pe.wait_ge(state_in, 16)
            for f in range(2 * FT):
                last = pe.transpose(s.ps[:, 4 + f // FT, NST * (f % FT):NST * (f % FT + 1)], state_rows[:, P * f:P * (f + 1)],
                                    s.ident[0:NST, 0:NST])
            last.then_inc(state_turned, 1)
            for n in range(NC):
                if n == 1:
                    pe.wait_ge(state_moved, 1)
                x = CHUNKS[n][2]
                if x:
                    pe.wait_ge(ring.loaded[0], 16 * (ring.uses[0] + n // 2 + 1))
                else:
                    pe.wait_ge(w_split, n // 2 + 1)
                for j in range(2):
                    m = 2 * (n // 2) + j
                    if m >= 2:
                        pe.wait_ge(branch_free if x else gate_free, m - 1)
                    if x:
                        w = tiles(ring.part(n)[1])
                        for k in range(KT):
                            for half in range(2):
                                last = pe.matmul(bank(m, 1)[:, half, :], w[:, k, P * j:P * (j + 1)],
                                                 operands[x][:, k, half * HALF:(half + 1) * HALF], start=k == 0, stop=k == KT - 1)
                    else:
                        await_tile = (lambda k: pe.wait_ge(split, k + 1)) if n == 0 and j == 0 else None
                        last = fm_split_unit(pe, [tiles(ap) for ap in w_parts], P * j, (high, low), lambda half: bank(m, 0)[:, half, :], await_tile)
                    last.then_inc(branch_done if x else gate_done, 1)

        @block.scalar
        def _(act):
            def cut_weights(g):
                act.wait_ge(ring.loaded[1], 16 * (ring.uses[1] + g + 1))
                act.copy(w_parts[0], ring.part(0)[1]).then_inc(w_cut, 1)

            cut_weights(0)
            cut_tiles(act, s.ht, high, cut)
            for n in range(0, NC, 2):
                for j in range(2):
                    m = n + j
                    act.wait_ge(gate_done, m + 1)
                    if m >= 4:
                        act.wait_ge(gated, m - 3)
                    c, q = m // 2 % 2, m // 4
                    col = (V_GB if c else V_GA) + 2 * q + j
                    act.activation(halves(sg[:, c, j, :]), bank(m, 0), ACT.Sigmoid, bias=s.vecT[:, 0, col:col + 1]).then_inc(gate_free, 1)
                if n + 2 < NC:
                    cut_weights(n // 2 + 1)

        @block.vector
        def _(dve):
            def rest_weights(g):
                dve.wait_ge(w_cut, g + 1)
                dve.tensor_tensor(w_parts[1], ring.part(0)[1], w_parts[0], ALU.subtract).then_inc(w_split, 1)

            rest_weights(0)
            rest_tiles(dve, s.ht, high, low, cut, split)
            dve.wait_ge(state_turned, 1)
            dve.tensor_copy(s.before[:].rearrange("p (a f) n -> p a (f n)", a=2), s.ps[:, 4:6, 0:FT * NST]).then_inc(state_moved, 1)
            for n in range(0, NC, 2):
                for j in range(2):
                    m = n + j
                    dve.wait_ge(branch_done, m + 1)
                    dve.wait_ge(gate_free, m + 1)
                    c, q = m // 2 % 2, m // 4
                    out, gate = mix[:, 2 * q + j, :], sg[:, c, j, :]
                    if c == 0:
                        dve.tensor_tensor(halves(out), bank(m, 1), halves(gate), ALU.mult).then_inc(branch_free, 1)
                        dve.sem_inc(gated, 1)
                    else:
                        dve.tensor_tensor(halves(gate), bank(m, 1), halves(gate), ALU.mult).then_inc(branch_free, 1)
                        dve.wait_ge(branch_free, m + 1)
                        dve.tensor_tensor(out, out, gate, ALU.add).then_inc(gated, 1)
                    if j == 0 and n + 2 < NC:
                        rest_weights(n // 2 + 1)

        for n in range(2):
            ring.uses[n] += NC // 2


def block_project(nc, s, name, lhs, parts, slot, which, loads, x_src=None, y_dst=None):
    with ExitStack() as ctx:
        sb = lambda n, shape: ctx.enter_context(nc.sbuf_tensor(f"{name}_{n}", shape, F32))
        sem = lambda n: s.semaphore(f"{name}_{n}")
        y = sb("y", [P, TILES, D])
        junk = sb("squares", [P, 2, 512])
        s.ring.room(nc, ctx, name)
        x_split = ctx.enter_context(nc.sbuf_tensor(name + "_split_lhs", [P, 2, 2, 4, TOK], F32R))
        gt = sb("residual_multiplier", [DEC + 1, D])
        prompt_row = sb("prompt_row", [DEC + 1, P])
        ss = sb("square_sums", [P, TILES, 2])
        rs = sb("inverse_rms", [P, TILES])
        lhs_cut, lhs_split, gt_in, x_in, row_set, spread, done, used, copied, squared, summed, rooted, scaled, added, out, step = [sem(n) for n in (
            "lhs_cut", "lhs_split", "multiplier_in", "x_in", "row_set", "spread", "done", "used", "copied", "squared", "summed", "rooted", "scaled", "added", "out",
            "step")]
        block = ctx.enter_context(nc.Block())
        ktiles = max(k0 + n for _, k0, n in parts)
        s.ring.begin(slot)

        @block.sync
        def _(sp):
            sp.dma_start(gt[:], s.multiplier_rows[:, which, :]).then_inc(gt_in, 16)
            if x_src is not None:
                for t in range(TILES):
                    sp.dma_start(s.x[0:rows(t), t, :], x_src(t)).then_inc(x_in, 16)
            loads(sp, used)
            if y_dst is not None:
                for t in range(TILES):
                    sp.wait_ge(added, t + 1)
                    sp.dma_start(y_dst(t), s.x[0:rows(t), t, :]).then_inc(out, 16)
                sp.wait_ge(out, 16 * TILES)

        @block.tensor
        def _(pe):
            pe.wait_ge(row_set, 1)
            pe.wait_ge(gt_in, 16)
            for h in range(2):
                last = pe.matmul(s.ps[:, 6 + h, :], prompt_row[:], gt[:, 512 * h:512 * (h + 1)], start=True, stop=True)
            last.then_inc(spread, 1)
            for n, (h, k0, nk) in enumerate(parts):
                s.ring.await_ready(pe, n)
                wh, wl = s.ring.split(n, 512)
                for t in range(TILES):
                    if h == 1 and k0 == 0:
                        pe.wait_ge(copied, t + 1)
                    for k in range(nk):
                        if t == 0:
                            pe.wait_ge(lhs_split, ktiles * h + k0 + k + 1)
                        xh, xl = x_split[:, n % 2, 0], x_split[:, n % 2, 1]
                        for term, (x, w) in enumerate(((xh, wh), (xh, wl), (xl, wh))):
                            last = pe.matmul(s.ps[0:rows(t), t, :], x[:, k, cols(t)], w[:, k, :],
                                             start=k0 + k == 0 and term == 0, stop=k0 + k == ktiles - 1 and term == 2)
                    if k0 + nk == ktiles:
                        last.then_inc(done, 1)
                    elif t == PT_:
                        last.then_inc(used, 1)
                if k0 + nk == ktiles:
                    pe.wait_ge(done, TILES * (h + 1))
                    pe.sem_inc(used, 1)

        half = len(parts) // 2

        def cut(act, n):
            _, k0, nk = parts[n]
            s.ring.cut(act, n)
            cut_tiles(act, lhs[:, k0:k0 + nk, :], x_split[:, n % 2, 0], lhs_cut)

        def rest(dve, n):
            h, k0, nk = parts[n]
            s.ring.rest(dve, n)
            rest_tiles(dve, lhs[:, k0:k0 + nk, :], x_split[:, n % 2, 0], x_split[:, n % 2, 1], lhs_cut, lhs_split, ktiles * h + k0)

        @block.scalar
        def _(act):
            for n in range(half + 1):
                cut(act, n)
            for m in range(2 * TILES):
                if m == TILES:
                    for n in range(half + 1, len(parts)):
                        cut(act, n)
                h, t = m // TILES, m % TILES
                act.wait_ge(copied, m + 1)
                if m >= 2:
                    act.wait_ge(squared, m - 1)
                act.activation(junk[0:rows(t), m % 2, :], y[0:rows(t), t, 512 * h:512 * (h + 1)], ACT.Square,
                               accum_out=ss[0:rows(t), t, h:h + 1]).then_inc(squared, 1)
                if h == 1:
                    act.wait_ge(summed, t + 1)
                    act.activation(rs[0:rows(t), t:t + 1], ss[0:rows(t), t, 0:1], ACT.Sqrt).then_inc(rooted, 1)

        @block.vector
        def _(dve):
            link = Chain(dve, step)
            link(dve.memset(prompt_row[:], 0.0))
            dve.memset(prompt_row[DEC:DEC + 1, :], 1.0).then_inc(row_set, 1)
            for n in range(half + 1):
                rest(dve, n)
            for m in range(2 * TILES):
                if m == TILES:
                    for n in range(half + 1, len(parts)):
                        rest(dve, n)
                h, t = m // TILES, m % TILES
                r = rows(t)
                dve.wait_ge(done, m + 1)
                dve.tensor_copy(y[0:r, t, 512 * h:512 * (h + 1)], s.ps[0:r, t, :]).then_inc(copied, 1)
                if h == 1:
                    dve.wait_ge(squared, m + 1)
                    link(dve.tensor_tensor(ss[0:r, t, 0:1], ss[0:r, t, 0:1], ss[0:r, t, 1:2], ALU.add))
                    dve.tensor_scalar(ss[0:r, t, 0:1], ss[0:r, t, 0:1], 1.0 / D, EPS, ALU.mult, ALU.add).then_inc(summed, 1)
                    dve.wait_ge(rooted, t + 1)
                    link(dve.reciprocal(rs[0:r, t:t + 1], rs[0:r, t:t + 1]))
                    if t == 0:
                        dve.wait_ge(spread, 1)
                        dve.wait_ge(gt_in, 16)
                    row = s.ps[:, 6:8, :].rearrange("p a n -> p (a n)") if t < PT_ else gt[0:DEC, :]
                    dve.scalar_tensor_tensor(y[0:r, t, :], y[0:r, t, :], rs[0:r, t:t + 1], row, ALU.mult, ALU.mult).then_inc(scaled, 1)

        @block.gpsimd
        def _(pool):
            if x_src is not None:
                pool.wait_ge(x_in, 16 * TILES)
            for t in range(TILES):
                pool.wait_ge(scaled, t + 1)
                pool.tensor_tensor(s.x[0:rows(t), t, :], s.x[0:rows(t), t, :], y[0:rows(t), t, :], ALU.add).then_inc(added, 1)

        s.ring.end(len(parts))


def block_conv_state_out(nc, s):
    a = s.args
    NR = 2 * FT // 4
    with ExitStack() as ctx:
        state_rows = ctx.enter_context(nc.sbuf_tensor("new_conv_state_rows", [NST + 2, 2 * DFF], F32))
        turned, moved, stored = [s.semaphore(n) for n in ("last_turned", "last_moved", "last_stored")]
        block = ctx.enter_context(nc.Block())

        @block.sync
        def _(sp):
            sp.wait_ge(moved, NR)
            sp.dma_start(a["s_conv"][0].rearrange("b r n -> (b r) n"), state_rows[0:NST, :]).then_inc(stored, 16)
            sp.dma_start(a["p_conv"][0, 0], state_rows[NST:NST + 2, :]).then_inc(stored, 16)
            sp.wait_ge(stored, 32)

        @block.tensor
        def _(pe):
            for n in range(NR):
                if n >= 8:
                    pe.wait_ge(moved, n - 7)
                for f in range(4):
                    last = pe.transpose(s.ps[0:NST + 2, n % 8, P * f:P * (f + 1)], s.after[:, 4 * n + f, :], s.ident[:])
                last.then_inc(turned, 1)

        @block.vector
        def _(dve):
            for n in range(NR):
                dve.wait_ge(turned, n + 1)
                dve.tensor_copy(state_rows[:, 4 * P * n:4 * P * (n + 1)], s.ps[0:NST + 2, n % 8, :]).then_inc(moved, 1)


def block_ffn_up(nc, s, h2, act_fm, load_up, load_down):
    a, ring = s.args, s.ring
    STEPS = FT // 2
    UW = 2 + SEQ + NB * (2 + NT)
    with ExitStack() as ctx:
        sb = lambda name, shape: ctx.enter_context(nc.sbuf_tensor(name, shape, F32))
        sem = lambda name: s.semaphore("u_" + name)
        u = sb("u", [P, 2, 4, UW])
        cv = [sb("conv", [P, 4, UW])[:], s.ring.tail[:, 0:4 * UW].rearrange("p (m n) -> p m n", m=4)]
        ring.room(nc, ctx, "up")
        high, low = [ctx.enter_context(nc.sbuf_tensor(f"h2_{n}", [P, KT, TOK], F32R)) for n in ("high", "low")]
        before, after = s.before, s.after
        h_cut, h_split, zeroed, done, free, before_set, first, second, third, gelu, made, kept = [sem(n) for n in (
            "h_cut", "h_split", "zeroed", "done", "free", "before_set", "first_tap", "second_tap", "third_tap", "gelu", "made",
            "last_rows_kept")]
        block = ctx.enter_context(nc.Block())
        ring.begin(1, 2)
        decode = lambda ap: ap[:, 2 + SEQ:UW].rearrange("p (b t) -> p b t", b=NB)

        def tile(j, m):
            return j * 2 + (m // 2 + FT * (m % 2))

        def chunk(e, q, i):
            return (2 * e + q, i, 4) if i is not None else (2 * (STEPS - 1) + q,)

        def loop(eng, body):
            with eng.Fori(0, STEPS // 2) as i:
                for e in range(2):
                    body(i * 2 + e, e, i)
            body(STEPS - 1, 0, None)

        @block.sync
        def _(sp):
            with sp.Fori(0, STEPS - 1) as i:
                for q in range(2):
                    sp.wait_ge(done, i * 4 + 2 * (q + 1))
                    load_up(sp, i * 2 + (2 + q), q)
            for n in range(2):
                sp.wait_ge(done, 4 * (STEPS - 1) + 2 * (n + 1))
                load_down(sp, n)

        @block.tensor
        def _(pe):
            def product(j, e, i):
                for q in range(2):
                    ring.await_ready(pe, *chunk(e, q, i))
                    for m in (2 * q, 2 * q + 1):
                        pe.wait_ge(free, j * 4 + (m + 1))
                        if m > 0:
                            await_tile = None
                        else:
                            await_tile = lambda k: pe.wait_ge(h_split, k + 1)
                        fm_split_unit(pe, ring.split(q), P * (m % 2), (high, low), lambda half: s.ps[:, 2 * m + half, 0:HALF],
                                      await_tile).then_inc(done, 1)

            loop(pe, product)

        @block.scalar
        def _(act):
            act.sem_inc(free, 4)
            ring.cut(act, 0)
            cut_tiles(act, h2, high, h_cut)
            ring.cut(act, 1)

            def taps(j, e, units):
                for m in units:
                    n = j * 4 + m
                    act.wait_ge(done, n + 1)
                    act.wait_ge(third, n + 1)
                    act.wait_ge(kept, n + 1)
                    act.copy(u[:, e, m, 2:2 + HALF], s.ps[:, 2 * m, 0:HALF])
                    act.copy(u[:, e, m, 2 + HALF:2 + SEQ], s.ps[:, 2 * m + 1, 0:SEQ - HALF])
                    act.copy(decode(u[:, e, m, :])[:, :, 2:2 + NT],
                             s.ps[:, 2 * m + 1, SEQ - HALF:HALF].rearrange("p (b t) -> p b t", b=NB)).then_inc(free, 1)
                    act.wait_ge(free, n + 5)
                    act.wait_ge(before_set, n + 1)
                    act.wait_ge(made, j * 2 + (1 + m // 2))
                    act.wait_ge(zeroed, 1)
                    f = tile(j, m)
                    act.activation(cv[e][:, m, 2:UW], u[:, e, m, 2:UW], ACT.Identity, scale=s.vecT[:, 2, bass.ds(f, 1)],
                                   bias=s.vecT[:, 2, bass.ds(f + 2 * FT, 1)]).then_inc(first, 1)

            def gelus(j, e):
                for m in (1, 3):
                    act.wait_ge(third, j * 4 + (m + 1 + 8))
                    act.activation(cv[e][:, m, 2:UW], cv[e][:, m, 2:UW], ACT.Gelu_apprx_tanh).then_inc(gelu, 1)

            with act.Fori(0, STEPS // 2) as i:
                taps(i * 2, 0, (0, 1))
                ring.cut(act, 2, i, 4)
                taps(i * 2, 0, (2, 3))
                ring.cut(act, 3, i, 4)
                taps(i * 2 + 1, 1, (0, 1))
                ring.cut(act, 4, i, 4)
                gelus(i * 2, 0)
                taps(i * 2 + 1, 1, (2, 3))
                ring.cut(act, 5, i, 4)
                gelus(i * 2 + 1, 1)
            taps(STEPS - 1, 0, range(4))
            gelus(STEPS - 1, 0)

        @block.vector
        def _(dve):
            dve.sem_inc(third, 8)
            dve.sem_inc(made, 4)
            ring.rest(dve, 0)
            rest_tiles(dve, h2, high, low, h_cut, h_split)
            ring.rest(dve, 1)
            def taps(j, e, units):
                for m in units:
                    dve.wait_ge(first, j * 4 + (m + 1))
                    dve.scalar_tensor_tensor(cv[e][:, m, 2:UW], u[:, e, m, 1:UW - 1], s.vecT[:, 1, bass.ds(tile(j, m) + 2 * FT, 1)],
                                             cv[e][:, m, 2:UW], ALU.mult, ALU.add).then_inc(second, 1)
                for m in units:
                    dve.wait_ge(second, j * 4 + (m + 1))
                    dve.scalar_tensor_tensor(cv[e][:, m, 2:UW], u[:, e, m, 0:UW - 2], s.vecT[:, 1, bass.ds(tile(j, m), 1)],
                                             cv[e][:, m, 2:UW], ALU.mult, ALU.add).then_inc(third, 1)

            def product(j, e):
                for m in range(2):
                    dve.wait_ge(gelu, j * 2 + (m + 1))
                    out = act_fm[:, bass.ds(j * 2 + m, 1), :]
                    va, vg = cv[e][:, 2 * m, :], cv[e][:, 2 * m + 1, :]
                    dve.tensor_tensor(out[:, :, 0:SEQ], va[:, 2:2 + SEQ].unsqueeze(1), vg[:, 2:2 + SEQ].unsqueeze(1), ALU.mult)
                    dve.tensor_tensor(out[:, :, SEQ:TOK].rearrange("p o (b t) -> p (o b) t", b=NB), decode(va)[:, :, 2:2 + NT],
                                      decode(vg)[:, :, 2:2 + NT], ALU.mult).then_inc(made, 1)

            with dve.Fori(0, STEPS // 2) as i:
                taps(i * 2, 0, (0, 1))
                ring.rest(dve, 2, i, 4)
                taps(i * 2, 0, (2, 3))
                ring.rest(dve, 3, i, 4)
                taps(i * 2 + 1, 1, (0, 1))
                ring.rest(dve, 4, i, 4)
                product(i * 2, 0)
                taps(i * 2 + 1, 1, (2, 3))
                ring.rest(dve, 5, i, 4)
                product(i * 2 + 1, 1)
            taps(STEPS - 1, 0, (0, 1))
            taps(STEPS - 1, 0, (2, 3))
            product(STEPS - 1, 0)

        @block.gpsimd
        def _(pool):
            pool.memset(u[:, :, :, 0:2], 0.0).then_inc(zeroed, 1)
            pool.sem_inc(kept, 8)
            pool.wait_ge(zeroed, 1)

            def earlier(j, e, m):
                n = j * 4 + m
                pool.wait_ge(third, n + 1)
                pool.wait_ge(zeroed, 1)
                pool.tensor_copy(decode(u[:, e, m, :])[:, :, 0:2],
                                 before[:, bass.ds(tile(j, m), 1), :].rearrange("p o (b t) -> p (o b) t", b=NB)).then_inc(before_set, 1)

            def keep(j, e, m):
                out = after[:, bass.ds(tile(j, m), 1), :]
                pool.wait_ge(free, j * 4 + (m + 5))
                pool.wait_ge(zeroed, 1)
                pool.tensor_copy(out[:, :, 0:NST].rearrange("p o (b t) -> p (o b) t", b=NB), decode(u[:, e, m, :])[:, :, NT:NT + 2])
                pool.tensor_copy(out[:, :, NST:NST + 2], u[:, e, m, SEQ:SEQ + 2].unsqueeze(1)).then_inc(kept, 1)

            def body(j, e, i):
                for m in range(4):
                    earlier(j, e, m)
                    keep(j, e, m)

            loop(pool, body)

        ring.end(2 * STEPS)


def program(nc, args):
    with ExitStack() as ctx:
        sb = lambda name, shape: ctx.enter_context(nc.sbuf_tensor(name, shape, F32))
        s = Shared(args)
        semaphores = []

        def semaphore(name):
            semaphores.append(nc.alloc_semaphore(name))
            return semaphores[-1]

        s.semaphore = semaphore
        s.ps = ctx.enter_context(nc.psum_tensor("ps", [P, 8, 512], F32))
        s.ring = Ring(nc, ctx)
        s.ident = sb("ident_sb", [P, P])
        s.vecT = sb("vector_columns", [P, 3, NC2])
        s.mod = sb("modulation", [P, 32, DEC + 1])
        s.cT = sb("c_columns", [P, KT, DEC + 1])
        carry = s.carry = sb("mlstm_fm_then_residual", [P, TILES * D])
        s.hmt = carry[:, 0:KT * TOK].rearrange("p (k n) -> p k n", k=KT)
        up, down = args["w_up"][0], args["w_down"][0]

        def load_up(sp, j, k):
            for n in range(2):
                s.ring.load_part(sp, k, matrix(up, j * P + n * DFF, P), piece=slice(P * n, P * (n + 1)))

        def parts(ktiles):
            return [(h, k, min(4, ktiles - k)) for h in range(2) for k in range(0, ktiles, 4)]

        def load_rows(sp, w, part, k, after=None):
            h, k0, nk = part
            s.ring.load_part(sp, k, matrix(w[k0 * P:(k0 + nk) * P], 512 * h, k=nk), after=after)

        OUT, DOWN = parts(KT), parts(FT)

        with ExitStack() as front:
            s.ht = front.enter_context(nc.sbuf_tensor("h_fm", [P, KT, TOK], F32))
            with ExitStack() as inner:
                s.x = inner.enter_context(nc.sbuf_tensor("x1", [P, TILES, D], F32))
                norm = Norm(nc, s, inner, "n1", lambda t: token_rows(args["x_prompt"], args["x_sample"], t))
                block_modulation(nc, s, norm)
                block_norm(nc, s, "n1", s.ht, 0, 8, norm)
            with ExitStack() as inner:
                mb = lambda name, shape: inner.enter_context(nc.sbuf_tensor(name, shape, F32))
                s.qk = mb("qk_fm", [P, 2 * KT, TOK])
                s.va = mb("v_and_ones", [P, TILES, MH, MD + 1])
                s.og = mb("output_gates", [P, TILES, D])
                s.mneg = mb("minus_m", [P, MH, TOK])
                s.gates = mb("gate_rows", [MH, 2, TOK])
                s.gate_bias = mb("gate_bias", [MH, 2])
                s.head_row = mb("head_row_sb", [MH, MH, P])
                s.gcol = mb("gate_columns", [P, TILES, 3, MH])
                s.acol = mb("a_columns", [DEC, MH])
                s.alast = mb("a_last", [MH, NB])
                s.decay = mb("decay", [P, MH, NB])
                s.hdec = mb("h_dec", [DEC, MH, MD])
                block_mlstm_in(nc, s)
                with ExitStack() as g:
                    s.norm_w = g.enter_context(nc.sbuf_tensor("norm_w", [P, D], F32))
                    block_mlstm_gates(nc, s)
                block_mlstm_prompt(nc, s)
                block_mlstm_decode(nc, s)
                block_mlstm_out(nc, s)
            s.multiplier_rows = nc.dram_tensor("multiplier_rows", (DEC + 1, 2, D), F32, kind="Internal").ap()
            with ExitStack() as mixer:
                s.hat = mixer.enter_context(nc.sbuf_tensor("attention_fm", [P, KT, TOK], F32))
                with ExitStack() as attention:
                    ab = lambda name, shape: attention.enter_context(nc.sbuf_tensor(name, shape, F32))
                    s.kv_dec = ab("kv_dec", [DEC, 1536])
                    s.qT_dec = ab("qT_dec", [P, 2, R, DEC])
                    s.kT_dec = ab("kT_dec", [P, 2, 2, DEC])
                    s.branch_gates = ab("branch_gates", [P, TILES, 48])
                    s.gate_rows = ab("gate_rows_dec", [QR, NB, 3])
                    s.gate_scratch = nc.dram_tensor("gate_scratch", (DEC, 48), F32, kind="Internal").ap()
                    s.w1 = ab("cmp_w1_sb", [P, 2, STRIDE // 2, 2, AD])
                    s.w2 = ab("cmp_w2_sb", [AD, 2, AD])
                    s.pe_bias = ab("pe_bias", [AD, 2])
                    with ExitStack() as inner:
                        pb = lambda name, shape: inner.enter_context(nc.sbuf_tensor(name, shape, F32))
                        s.kv = pb("kv_prompt", [P, PT_, 1536])
                        s.kT = pb("kT_prompt", [P, 2, 2, SEQ])
                        s.qT = pb("qT_prompt", [P, 2, R, SEQ])
                        s.kc_p = pb("kc_prompt", [P, 2, PCMP])
                        s.vc_p = pb("vc_prompt", [PCMP, G * AD])
                        with ExitStack() as g:
                            s.q_tm = g.enter_context(nc.sbuf_tensor("q_tm", [P, TILES, D], F32))
                            block_attention_in(nc, s)
                            block_attention_turn(nc, s)
                        block_modulation_rest(nc, s)
                        block_compress_prompt(nc, s)
                        s.ha = pb("attention_tm", [P, PT_, D])
                        block_attention_prompt(nc, s)
                        block_attention_out(nc, s)
                    block_attention_decode(nc, s)
                nc.clear_and_free_semaphores(semaphores)
                nc.all_engine_barrier()
                mix = mixer.enter_context(nc.sbuf_tensor("mixed_fm", [P, KT, TOK], F32))

                def first_loads(sp, gate_done, branch_done):
                    load_rows(sp, args["w_out"][0], OUT[0], 0, after=(gate_done, 16))
                    load_rows(sp, args["w_out"][0], OUT[1], 1, after=(branch_done, 16))

                UW4 = 4 * (2 + SEQ + NB * (2 + NT))
                s.before = s.ring.tail[:, UW4:UW4 + 2 * FT * NST].rearrange("p (f n) -> p f n", n=NST)
                block_branches(nc, s, mix, first_loads)
                s.x = carry[:].rearrange("p (t n) -> p t n", t=TILES)

                def loads(sp, used):
                    for n in range(2, len(OUT)):
                        load_rows(sp, args["w_out"][0], OUT[n], n, after=(used, n - 1))
                    for n in range(2):
                        sp.wait_ge(used, len(OUT) - 1 + n)
                        load_up(sp, n, n)

                block_project(nc, s, "mixer_out", mix, OUT, 1, 0, loads,
                              x_src=lambda t: token_rows(args["x_prompt"], args["x_sample"], t))
        act_fm = sb("ffn_hidden_fm", [P, FT, TOK])
        h2 = act_fm[:, 0:KT, :]
        s.after = sb("u_after", [P, 2 * FT, NST + 2])
        block_norm(nc, s, "n2", h2, 16, 24)
        block_ffn_up(nc, s, h2, act_fm, load_up, lambda sp, n: load_rows(sp, down, DOWN[n], n))
        block_conv_state_out(nc, s)

        def loads(sp, used):
            for n in range(2, len(DOWN)):
                load_rows(sp, down, DOWN[n], n, after=(used, n - 1))

        block_project(nc, s, "ffn_out", act_fm, DOWN, 1, 1, loads,
                      y_dst=lambda t: token_rows(args["y_prompt"], args["y_sample"], t))
INPUTS = ["x_prompt", "x_sample", "cache_cmp_kv", "cache_slc_kv", "cache_win_kv", "state_C", "state_n", "state_m",
          "state_conv", "page_table", "c_prompt", "c_sample", "w_ada", "b_ada", "g_pre_mix", "g_post_mix", "g_pre_ffn",
          "g_post_ffn", "w_in", "b_in", "m_norm_w", "cmp_w1", "cmp_pe", "cmp_w2", "w_branch_m", "w_branch_a", "w_out",
          "w_up", "conv_w", "conv_b", "w_down"]
KV = (2, G, AD)
OUTPUTS = {"y_prompt": (1, SEQ, D), "y_sample": (NB, NT, D), "p_cmp": (1, 1, SEQ, *KV), "p_slc": (1, 1, SEQ, *KV),
           "p_win": (1, 1, SEQ, *KV), "p_C": (1, 1, MH, MD, MD), "p_n": (1, 1, MH, MD), "p_m": (1, 1, MH),
           "p_conv": (1, 1, 2, 2 * DFF), "s_cmp": (1, NB, NT, *KV), "s_slc": (1, NB, NT, *KV),
           "s_win": (1, NB, WIN, *KV), "s_C": (1, NB, MH, MD, MD), "s_n": (1, NB, MH, MD), "s_m": (1, NB, MH),
           "s_conv": (1, NB, 2, 2 * DFF)}


def kernel(**inputs):
    import numpy as _np
    import concourse.bacc as _bacc
    from concourse import mybir as _mybir
    from concourse.bass_utils import run_bass_kernel_spmd as _run

    nc = _bacc.Bacc("TRN2", target_bir_lowering=False, num_devices=1)
    arrays = {name: _np.ascontiguousarray(inputs[name]) for name in INPUTS}
    arrays.update(constants())
    args = {n: nc.dram_tensor("in_" + n, v.shape, _mybir.dt.from_np(v.dtype), kind="ExternalInput").ap()
            for n, v in arrays.items()}
    args.update({n: nc.dram_tensor("out_" + n, shape, F32, kind="ExternalOutput").ap() for n, shape in OUTPUTS.items()})
    program(nc, args)
    r = _run(nc, [{"in_" + n: v for n, v in arrays.items()}], core_ids=[0])
    return tuple(r.results[0]["out_" + n] for n in OUTPUTS)
```
